# Optimizing a Trainium2 kernel written in Bass

```python
import jax, jax.numpy as jnp
from jax import lax
import numpy as np
import math

D_MODEL = 1024
BATCH = 1
SEQ = 256
DEPTH = 2

N_META = 16
BLOCK = 128
WINDOW = 128
RET_HEADS = 8
RET_QK_DIM = D_MODEL // 16
RET_V_DIM = D_MODEL // 8
ATT_Q_HEADS = 8
ATT_KV_HEADS = 2
ATT_GROUP = ATT_Q_HEADS // ATT_KV_HEADS
ATT_HEAD_DIM = D_MODEL // 16
ROPE_DIM = ATT_HEAD_DIM // 4
ROPE_THETA = 500000.0
XPOS_THETA = 10000.0
D_FF = 4 * D_MODEL
EPS = 1e-6
NEG_INF = -1e30

RET_QK = RET_HEADS * RET_QK_DIM
RET_V = RET_HEADS * RET_V_DIM
ATT_Q = ATT_Q_HEADS * ATT_HEAD_DIM
ATT_KV = ATT_KV_HEADS * ATT_HEAD_DIM
SPLITS = (RET_QK, RET_QK, RET_V, RET_V, ATT_Q, ATT_KV, ATT_KV, D_MODEL, D_MODEL)
D_IN = sum(SPLITS)


def rms_norm(x, g):
    xf = x.astype(jnp.float32)
    y = xf * lax.rsqrt(jnp.mean(xf * xf, axis=-1, keepdims=True) + EPS)
    return (y * g.astype(jnp.float32)).astype(x.dtype)

def rotate(x, pos, theta, rot_dim):
    half = rot_dim // 2
    freqs = jnp.power(jnp.float32(theta), -jnp.arange(0, rot_dim, 2, dtype=jnp.float32) / rot_dim)
    ang = pos.astype(jnp.float32)[:, None] * freqs[None, :]
    cos = jnp.cos(ang)[:, None, :]
    sin = jnp.sin(ang)[:, None, :]
    xf = x.astype(jnp.float32)
    x1, x2 = xf[..., :half], xf[..., half:rot_dim]
    out = jnp.concatenate([x1 * cos - x2 * sin, x2 * cos + x1 * sin, xf[..., rot_dim:]], axis=-1)
    return out.astype(x.dtype)

def retention_dir(q, k, v, log_gamma, include_diag):
    C = q.shape[-2]
    idx = jnp.arange(C, dtype=jnp.float32)
    rel = idx[:, None] - idx[None, :]
    lg = log_gamma[:, None, None]
    mask = (rel >= 0) if include_diag else (rel > 0)
    decay_in = jnp.where(mask[None], jnp.exp(lg * jnp.maximum(rel, 0.0)[None]), 0.0)
    s = jnp.einsum('bhncd,bhnkd->bhnck', q, k) * decay_in[:, None]
    o_in = jnp.einsum('bhnck,bhnke->bhnce', s, v)
    k_dec = k * jnp.exp(lg * (C - 1 - idx)[None, :])[:, None, :, :].transpose(0, 1, 3, 2)
    kv = jnp.einsum('bhncd,bhnce->bhnde', k_dec, v)
    chunk_decay = jnp.exp(log_gamma * C)[:, None, None]

    def step(state, kv_n):
        return state * chunk_decay + kv_n, state

    init = jnp.zeros(kv.shape[:2] + kv.shape[3:], jnp.float32)
    _, s_prev = lax.scan(step, init, jnp.moveaxis(kv, 2, 0))
    s_prev = jnp.moveaxis(s_prev, 0, 2)
    q_dec = q * jnp.exp(lg * (idx + 1.0)[None, :])[:, None, :, :].transpose(0, 1, 3, 2)
    o_x = jnp.einsum('bhncd,bhnde->bhnce', q_dec, s_prev)
    return o_in + o_x

def retention_branch(q, k, v, gate, log_decay, pad):
    B, L = q.shape[:2]
    Lp = L + pad
    nc = Lp // BLOCK
    pos = jnp.arange(L)
    q = rotate(q, pos, XPOS_THETA, RET_QK_DIM) * (RET_QK_DIM ** -0.5)
    k = rotate(k, pos, XPOS_THETA, RET_QK_DIM)

    def chunk(t):
        t = jnp.pad(t.astype(jnp.float32), ((0, 0), (pad, 0), (0, 0), (0, 0)))
        return t.reshape(B, nc, BLOCK, t.shape[2], t.shape[3]).transpose(0, 3, 1, 2, 4)

    qc, kc, vc = chunk(q), chunk(k), chunk(v)
    flip = lambda t: t[:, :, ::-1, ::-1]
    o = retention_dir(qc, kc, vc, log_decay[0], True) + flip(
        retention_dir(flip(qc), flip(kc), flip(vc), log_decay[1], False))
    o = o.transpose(0, 2, 3, 1, 4).reshape(B, Lp, RET_HEADS, RET_V_DIM)[:, pad:]
    mu = jnp.mean(o, axis=-1, keepdims=True)
    var = jnp.mean(jnp.square(o - mu), axis=-1, keepdims=True)
    o = (o - mu) * lax.rsqrt(var + EPS)
    o = o.reshape(B, L, RET_V).astype(gate.dtype)
    return o * jax.nn.silu(gate)

def attention_branch(q, k, v, sink, pad):
    B, L = q.shape[:2]
    Lp = L + pad
    nb = Lp // BLOCK
    pos = jnp.arange(L)
    q = rotate(q, pos, ROPE_THETA, ROPE_DIM)
    k = rotate(k, pos, ROPE_THETA, ROPE_DIM)
    meta_k, meta_v = k[:, :N_META], v[:, :N_META]
    qb = jnp.pad(q, ((0, 0), (pad, 0), (0, 0), (0, 0))).reshape(
        B, nb, BLOCK, ATT_KV_HEADS, ATT_GROUP, ATT_HEAD_DIM)
    ext = ((0, 0), (pad + BLOCK, BLOCK), (0, 0), (0, 0))
    kb = jnp.pad(k, ext).reshape(B, nb + 2, BLOCK, ATT_KV_HEADS, ATT_HEAD_DIM)
    vb = jnp.pad(v, ext).reshape(B, nb + 2, BLOCK, ATT_KV_HEADS, ATT_HEAD_DIM)

    def band(t):
        return jnp.concatenate([t[:, :-2], t[:, 1:-1], t[:, 2:]], axis=2)

    kband, vband = band(kb), band(vb)
    qpos = jnp.arange(nb)[:, None] * BLOCK + jnp.arange(BLOCK)[None, :]
    kpos = (jnp.arange(nb)[:, None] - 1) * BLOCK + jnp.arange(3 * BLOCK)[None, :]
    valid = ((kpos[:, None, :] >= pad + N_META) & (kpos[:, None, :] < Lp)
             & (jnp.abs(qpos[:, :, None] - kpos[:, None, :]) <= WINDOW))
    scale = ATT_HEAD_DIM ** -0.5
    s_band = jnp.einsum('bnqgrd,bnkgd->bngrqk', qb, kband).astype(jnp.float32) * scale
    s_band = jnp.where(valid[None, :, None, None], s_band, NEG_INF)
    s_meta = jnp.einsum('bnqgrd,bmgd->bngrqm', qb, meta_k).astype(jnp.float32) * scale
    s_sink = jnp.broadcast_to(sink.astype(jnp.float32).reshape(1, 1, ATT_KV_HEADS, ATT_GROUP, 1, 1),
                              s_meta.shape[:-1] + (1,))
    p = jax.nn.softmax(jnp.concatenate([s_sink, s_meta, s_band], axis=-1), axis=-1).astype(v.dtype)
    o = (jnp.einsum('bngrqm,bmgd->bnqgrd', p[..., 1:1 + N_META], meta_v)
         + jnp.einsum('bngrqk,bnkgd->bnqgrd', p[..., 1 + N_META:], vband))
    return o.reshape(B, Lp, ATT_Q)[:, pad:]

def first_inputs(seed: int = 0) -> dict:
    key = jax.random.key(seed)
    ks = jax.random.split(key, 14)
    f = jnp.float32
    nrm = lambda k, shape, s: jax.random.normal(k, shape, f) * s
    heads = np.arange(RET_HEADS)
    base = np.log(-np.log(1.0 - 2.0 ** (-5.0 - heads))).astype(np.float32)
    return {
        "x": nrm(ks[0], (BATCH, SEQ, D_MODEL), 1.0),
        "meta_tokens": nrm(ks[1], (N_META, D_MODEL), 1.0),
        "w_in": nrm(ks[2], (DEPTH, D_MODEL, D_IN), D_MODEL ** -0.5),
        "w_ret_o": nrm(ks[3], (DEPTH, RET_V, D_MODEL), RET_V ** -0.5),
        "w_att_o": nrm(ks[4], (DEPTH, ATT_Q, D_MODEL), ATT_Q ** -0.5),
        "w_mix_o": nrm(ks[5], (DEPTH, D_MODEL, D_MODEL), D_MODEL ** -0.5),
        "w_ff1": nrm(ks[6], (DEPTH, D_MODEL, D_FF), D_MODEL ** -0.5),
        "w_ff2": nrm(ks[7], (DEPTH, D_FF, D_MODEL), D_FF ** -0.5),
        "norm_mix_pre": 1.0 + nrm(ks[8], (DEPTH, D_MODEL), 0.02),
        "norm_mix_post": 1.0 + nrm(ks[9], (DEPTH, D_MODEL), 0.02),
        "norm_ff_pre": 1.0 + nrm(ks[10], (DEPTH, D_MODEL), 0.02),
        "norm_ff_post": 1.0 + nrm(ks[11], (DEPTH, D_MODEL), 0.02),
        "ret_decay": jnp.asarray(base)[None, None, :] + nrm(ks[12], (DEPTH, 2, RET_HEADS), 0.05),
        "attn_sink": nrm(ks[13], (DEPTH, ATT_Q_HEADS), 0.5),
    }

def first_block(x, meta_tokens, w_in, w_ret_o, w_att_o, w_mix_o, w_ff1, w_ff2,
              norm_mix_pre, norm_mix_post, norm_ff_pre, norm_ff_post, ret_decay, attn_sink):
    B = x.shape[0]
    h = jnp.concatenate([jnp.broadcast_to(meta_tokens[None].astype(x.dtype), (B, N_META, D_MODEL)), x], axis=1)
    L = h.shape[1]
    pad = (-L) % BLOCK
    for l in range(DEPTH):
        u = rms_norm(h, norm_mix_pre[l])
        proj = u @ w_in[l]
        parts, off = [], 0
        for size in SPLITS:
            parts.append(proj[..., off:off + size])
            off += size
        q_r, k_r, v_r, g_r, q_a, k_a, v_a, gate_r, gate_a = parts
        log_decay = -jnp.exp(ret_decay[l].astype(jnp.float32))
        y_r = retention_branch(q_r.reshape(B, L, RET_HEADS, RET_QK_DIM),
                               k_r.reshape(B, L, RET_HEADS, RET_QK_DIM),
                               v_r.reshape(B, L, RET_HEADS, RET_V_DIM),
                               g_r, log_decay, pad) @ w_ret_o[l]
        y_a = attention_branch(q_a.reshape(B, L, ATT_Q_HEADS, ATT_HEAD_DIM),
                               k_a.reshape(B, L, ATT_KV_HEADS, ATT_HEAD_DIM),
                               v_a.reshape(B, L, ATT_KV_HEADS, ATT_HEAD_DIM),
                               attn_sink[l], pad) @ w_att_o[l]
        mix = (jax.nn.sigmoid(gate_r) * y_r + jax.nn.sigmoid(gate_a) * y_a) @ w_mix_o[l]
        h = h + rms_norm(mix, norm_mix_post[l])
        u = rms_norm(h, norm_ff_pre[l])
        ff = jnp.square(jax.nn.relu(u @ w_ff1[l])) @ w_ff2[l]
        h = h + rms_norm(ff, norm_ff_post[l])
    return h[:, N_META:]


DEPTH_2 = 1

HEAD_DIM = 64
N_HEADS = D_MODEL // HEAD_DIM
N_HEADS_SB = N_HEADS // 2
N_HEADS_DIL = N_HEADS - N_HEADS_SB
D_SB = N_HEADS_SB * HEAD_DIM
D_DIL = N_HEADS_DIL * HEAD_DIM
DIL_PATTERNS = ((128, 1), (512, 4), (2048, 16))
N_BUCKETS = 32
MAX_DISTANCE = 2048
N_EXPERTS = 16
N_GROUPS = 4
EXPERTS_PER_GROUP = N_EXPERTS // N_GROUPS
TOP_K = 2
D_FF_EXPERT = 1024
ALPHA = (2.0 * DEPTH_2) ** 0.25
BETA = (8.0 * DEPTH_2) ** -0.25
LN_EPS = 1e-5
NEG_INF_2 = -1e30


def layer_norm(x, g, b):
    xf = x.astype(jnp.float32)
    mu = xf.mean(-1, keepdims=True)
    var = jnp.square(xf - mu).mean(-1, keepdims=True)
    return ((xf - mu) * lax.rsqrt(var + LN_EPS) * g.astype(jnp.float32) + b.astype(jnp.float32)).astype(x.dtype)

def head_rms_merge(o, g):
    b, h, s, dh = o.shape
    of = o.astype(jnp.float32)
    of = of * lax.rsqrt(jnp.mean(jnp.square(of), -1, keepdims=True) + 1e-6)
    of = of.transpose(0, 2, 1, 3).reshape(b, s, h * dh)
    return (of * g.astype(jnp.float32)).astype(o.dtype)

def t5_bucket(dist):
    max_exact = N_BUCKETS // 2
    d = jnp.maximum(dist, 0)
    large = max_exact + (jnp.log(jnp.maximum(d, 1).astype(jnp.float32) / max_exact)
                         / math.log(MAX_DISTANCE / max_exact) * (N_BUCKETS - max_exact)).astype(jnp.int32)
    large = jnp.minimum(large, N_BUCKETS - 1)
    return jnp.where(d < max_exact, d, large)

def stick_breaking_attention(q, k, v):
    b, h, s, dh = q.shape
    nb = s // BLOCK
    scale = dh ** -0.5
    qb = q.reshape(b, h, nb, BLOCK, dh).transpose(2, 0, 1, 3, 4)
    kpos = jnp.arange(s)

    def one_block(args):
        qblk, n = args
        z = jnp.einsum('bhqd,bhkd->bhqk', qblk, k).astype(jnp.float32) * scale
        qpos = n * BLOCK + jnp.arange(BLOCK)
        causal = kpos[None, :] < qpos[:, None]
        log_beta = jax.nn.log_sigmoid(z)
        log_1m = jnp.where(causal, jax.nn.log_sigmoid(-z), 0.0)
        between = lax.cumsum(log_1m, axis=3, reverse=True) - log_1m
        a = jnp.where(causal, jnp.exp(log_beta + between), 0.0)
        return jnp.einsum('bhqk,bhkd->bhqd', a.astype(v.dtype), v)

    out = lax.map(one_block, (qb, jnp.arange(nb)))
    return out.transpose(1, 2, 0, 3, 4).reshape(b, h, s, dh)

def dilated_branch(q, k, v, rel_bias, window, dilation):
    b, h, s, dh = q.shape
    span = window // dilation
    n_cls = s // dilation
    nb = -(-n_cls // BLOCK)
    pad = nb * BLOCK - n_cls

    def to_classes(t):
        t = t.reshape(b, h, n_cls, dilation, dh).transpose(0, 1, 3, 2, 4)
        t = jnp.pad(t, ((0, 0), (0, 0), (0, 0), (0, pad), (0, 0)))
        return t.reshape(b, h, dilation, nb, BLOCK, dh)

    def with_prev(t):
        prev = jnp.pad(t, ((0, 0), (0, 0), (0, 0), (1, 0), (0, 0), (0, 0)))[:, :, :, :nb]
        return jnp.concatenate([prev, t], axis=4)

    qc = to_classes(q)
    kk = with_prev(to_classes(k))
    vv = with_prev(to_classes(v))
    logits = jnp.einsum('bhrnqd,bhrnkd->bhrnqk', qc, kk).astype(jnp.float32) * dh ** -0.5

    qi = jnp.arange(BLOCK)[:, None]
    kj = jnp.arange(2 * BLOCK)[None, :]
    steps = qi + BLOCK - kj
    bias = rel_bias[t5_bucket(jnp.maximum(steps, 0) * dilation)].astype(jnp.float32)
    bias = bias.transpose(2, 0, 1)
    key_cls = (jnp.arange(nb)[:, None, None] - 1) * BLOCK + kj[None]
    valid = (steps >= 0) & (steps <= span) & (key_cls >= 0)
    logits = jnp.where(valid, logits + bias[None, :, None, None], NEG_INF_2)

    m = logits.max(-1, keepdims=True)
    p = jnp.exp(logits - m)
    denom = p.sum(-1, keepdims=True)
    o = jnp.einsum('bhrnqk,bhrnkd->bhrnqd', p.astype(vv.dtype), vv).astype(jnp.float32) / denom
    lse = (m + jnp.log(denom))[..., 0]

    def from_classes(t):
        t = t.reshape((b, h, dilation, nb * BLOCK) + t.shape[5:])[:, :, :, :n_cls]
        t = jnp.moveaxis(t, 2, 3)
        return t.reshape((b, h, s) + t.shape[4:])

    return from_classes(o), from_classes(lse)

def dilated_attention(q, k, v, rel_bias):
    outs, lses = [], []
    for window, dilation in DIL_PATTERNS:
        o, l = dilated_branch(q, k, v, rel_bias, window, dilation)
        outs.append(o)
        lses.append(l)
    w = jax.nn.softmax(jnp.stack(lses, 0), axis=0)
    return jnp.einsum('gbhs,gbhsd->bhsd', w, jnp.stack(outs, 0)).astype(q.dtype)

def token_mixer(x, w_in, g_sb, g_dil, w_out, rel_bias):
    b, s, _ = x.shape
    proj = jnp.einsum('bsd,de->bse', x, w_in)
    q_sb, k_sb, v_sb, q_dl, k_dl, v_dl = jnp.split(
        proj, [D_SB, 2 * D_SB, 3 * D_SB, 3 * D_SB + D_DIL, 3 * D_SB + 2 * D_DIL], axis=-1)
    to_heads = lambda t: t.reshape(b, s, -1, HEAD_DIM).transpose(0, 2, 1, 3)
    o_sb = stick_breaking_attention(to_heads(q_sb), to_heads(k_sb), to_heads(v_sb))
    o_dl = dilated_attention(to_heads(q_dl), to_heads(k_dl), to_heads(v_dl), rel_bias)
    y = jnp.concatenate([head_rms_merge(o_sb, g_sb), head_rms_merge(o_dl, g_dil)], axis=-1)
    return jnp.einsum('bse,ed->bsd', y, w_out)

def grouped_moe(x, w_router, b_router, w_gate, w_up, w_down):
    b, s, d = x.shape
    t = x.reshape(b * s, d)
    logits = (t @ w_router).astype(jnp.float32) + b_router.astype(jnp.float32)
    probs = jax.nn.softmax(logits, axis=-1)
    pg = probs.reshape(-1, N_GROUPS, EXPERTS_PER_GROUP)
    vals, idx = lax.top_k(pg, TOP_K)
    g_sel = jnp.argmax(vals.sum(-1), axis=-1)
    vals_sel = jnp.take_along_axis(vals, g_sel[:, None, None], axis=1)[:, 0]
    idx_sel = jnp.take_along_axis(idx, g_sel[:, None, None], axis=1)[:, 0]
    expert_ids = g_sel[:, None] * EXPERTS_PER_GROUP + idx_sel
    gates = vals_sel / vals_sel.sum(-1, keepdims=True)
    gate_dense = (jax.nn.one_hot(expert_ids, N_EXPERTS, dtype=jnp.float32) * gates[..., None]).sum(1)
    y = jnp.zeros_like(t)
    for e in range(N_EXPERTS):
        h = jax.nn.silu(t @ w_gate[e]) * (t @ w_up[e])
        y = y + gate_dense[:, e:e + 1].astype(t.dtype) * (h @ w_down[e])
    return y.reshape(b, s, d)

def second_inputs(seed: int = 0) -> dict:
    key = jax.random.key(seed)
    ks = jax.random.split(key, 20)
    f32 = jnp.float32
    d = D_MODEL
    s_in = d ** -0.5
    nrm = lambda k, shape: jax.random.normal(k, shape, f32)
    x = nrm(ks[0], (BATCH, SEQ, d))

    def qkv_cols(k, width):
        kq, kk, kv = jax.random.split(k, 3)
        return [nrm(kq, (DEPTH_2, d, width)) * s_in,
                nrm(kk, (DEPTH_2, d, width)) * s_in,
                nrm(kv, (DEPTH_2, d, width)) * (s_in * BETA)]

    w_in = jnp.concatenate(qkv_cols(ks[1], D_SB) + qkv_cols(ks[2], D_DIL), axis=-1)
    g_sb = 1.0 + 0.05 * nrm(ks[3], (DEPTH_2, D_SB))
    g_dil = 1.0 + 0.05 * nrm(ks[4], (DEPTH_2, D_DIL))
    w_out = nrm(ks[5], (DEPTH_2, d, d)) * (s_in * BETA)
    ln1_g = 1.0 + 0.05 * nrm(ks[6], (DEPTH_2, d))
    ln1_b = 0.02 * nrm(ks[7], (DEPTH_2, d))
    ln2_g = 1.0 + 0.05 * nrm(ks[8], (DEPTH_2, d))
    ln2_b = 0.02 * nrm(ks[9], (DEPTH_2, d))
    rel_bias = 0.5 * nrm(ks[10], (N_BUCKETS, N_HEADS_DIL))
    w_router = nrm(ks[11], (d, N_EXPERTS)) * s_in
    b_router = 0.01 * nrm(ks[12], (N_EXPERTS,))
    w_gate = nrm(ks[13], (DEPTH_2, N_EXPERTS, d, D_FF_EXPERT)) * s_in
    w_up = nrm(ks[14], (DEPTH_2, N_EXPERTS, d, D_FF_EXPERT)) * (s_in * BETA)
    w_down = nrm(ks[15], (DEPTH_2, N_EXPERTS, D_FF_EXPERT, d)) * (D_FF_EXPERT ** -0.5 * BETA)
    return {"x": x, "w_in": w_in, "g_sb": g_sb, "g_dil": g_dil, "w_out": w_out,
            "ln1_g": ln1_g, "ln1_b": ln1_b, "ln2_g": ln2_g, "ln2_b": ln2_b,
            "rel_bias": rel_bias, "w_router": w_router, "b_router": b_router,
            "w_gate": w_gate, "w_up": w_up, "w_down": w_down}

def second_block(x, w_in, g_sb, g_dil, w_out, ln1_g, ln1_b, ln2_g, ln2_b,
              rel_bias, w_router, b_router, w_gate, w_up, w_down):
    for l in range(DEPTH_2):
        h = token_mixer(x, w_in[l], g_sb[l], g_dil[l], w_out[l], rel_bias)
        x = layer_norm(ALPHA * x + h, ln1_g[l], ln1_b[l])
        h = grouped_moe(x, w_router, b_router, w_gate[l], w_up[l], w_down[l])
        x = layer_norm(ALPHA * x + h, ln2_g[l], ln2_b[l])
    return x


def setup_inputs(seed=0):
    out = dict(first_inputs(seed))
    for name, value in second_inputs(seed + 1).items():
        if name != "x":
            out[name + "_2"] = value
    return out


def reference(
    x, meta_tokens, w_in, w_ret_o, w_att_o, w_mix_o, w_ff1, w_ff2, norm_mix_pre, norm_mix_post,
    norm_ff_pre, norm_ff_post, ret_decay, attn_sink, w_in_2, g_sb_2, g_dil_2, w_out_2, ln1_g_2,
    ln1_b_2, ln2_g_2, ln2_b_2, rel_bias_2, w_router_2, b_router_2, w_gate_2, w_up_2, w_down_2,
):
    x = first_block(
        x, meta_tokens, w_in, w_ret_o, w_att_o, w_mix_o, w_ff1, w_ff2, norm_mix_pre,
        norm_mix_post, norm_ff_pre, norm_ff_post, ret_decay, attn_sink,
    )
    return second_block(
        x, w_in_2, g_sb_2, g_dil_2, w_out_2, ln1_g_2, ln1_b_2, ln2_g_2, ln2_b_2, rel_bias_2,
        w_router_2, b_router_2, w_gate_2, w_up_2, w_down_2,
    )


_drawn_inputs = setup_inputs


def setup_inputs(seed=0):
    import zlib

    import numpy as np

    out = dict(_drawn_inputs(seed))
    spreads = {}
    factors = {'attn_sink': 8.0, 'g_sb_2': 4.657, 'g_dil_2': 4.711, 'ln2_b_2': 2.721, 'b_router_2': 6.099}
    for name, (base, spread) in spreads.items():
        noise = np.random.default_rng([zlib.crc32(name.encode()), seed]).standard_normal(out[name].shape)
        drawn = base * np.exp(spread * noise) if base else spread * noise
        out[name] = __import__('jax').numpy.asarray(drawn.astype(out[name].dtype))
    for name, factor in factors.items():
        out[name] = (out[name] * factor).astype(out[name].dtype)
    return out
```

```python
from contextlib import ExitStack

import concourse.bass as bass
from concourse import mybir

F32 = mybir.dt.float32
F32R = mybir.dt.float32r
ALU = mybir.AluOpType
ACT = mybir.ActivationFunctionType
AX = mybir.AxisListType

D = 1024
SEQ = 256
META = 16
TOK = SEQ + META
LAYERS = 2
KT = D // 128
PAIRS = 4
D_FF = 4 * D
FF_HALVES = 2
FF_BLOCKS = D_FF // 128 // FF_HALVES
EXPERTS = 16
TILES = [(0, 128), (128, 128), (256, TOK - 256)]
SPAN = 2 * TOK
ALPHA = 2.0 ** 0.25
RMS_EPS, HEAD_EPS, LN_EPS = 1e-6, 1e-6, 1e-5
NEG = -1e30

SLOTS = 4
G_GATE, G_SIG, G_RET, G_ATT = 0, 2, 6, 10
G_RETO, G_ATTO, G_MIX, G_FF = 12, 14, 15, 17
G_HALF = 8
G_LAYER = 33
G_QKV = LAYERS * G_LAYER
G_OUT = G_QKV + 6
G_EXP = G_OUT + 2
G_END = G_EXP + 6 * EXPERTS
GROUPS = G_END + 1

A_GATE, A_SIG, A_RET, A_ATT, A_RETO, A_ATTO, A_MIX, A_FF = 0, 4, 12, 20, 23, 27, 31, 35
A_HALF = 12
A_LAYER = 59
A_QKV = LAYERS * A_LAYER
A_OUT = A_QKV + 12
A_EXP = A_OUT + 4

C_GAIN, C_DECAY, C_SINK, C_LAYER = 0, 32, 48, 56
C_LN, C_GHEAD, C_BROUTER, C_SECOND = 0, 32, 40, 56
LN_SETS = 6


def load_exp_ln(nc, act):
    act.add_instruction(mybir.InstLoadActFuncSet(
        name=nc.get_next_instruction_name(), engine=mybir.EngineType.Activation,
        act_func_set_id=LN_SETS, ins=[], outs=[]))


def build_program(nc, weights, h_in, layer_par, second_par, rope, toeplitz, att_mask, squares,
                  stick, bias_map, bias_add, rel_bias, w_router, tie_order, out):
    with ExitStack() as ctx:
        def sb(name, shape, dt=F32):
            return ctx.enter_context(nc.sbuf_tensor(name, shape, dt))

        def sem(name):
            return ctx.enter_context(nc.semaphore(name))

        raw = sb("raw", [128, SLOTS, KT, 128])
        w_hi = sb("w_hi", [128, SLOTS, KT, 128], F32R)
        w_lo = sb("w_lo", [128, SLOTS, KT, 128], F32R)
        h = sb("h", [128, KT, TOK])
        wide = sb("wide", [128, KT, TOK])
        x_hi = sb("x_hi", [128, KT, TOK], F32R)
        x_lo = sb("x_lo", [128, KT, TOK], F32R)
        f_hi = sb("f_hi", [128, FF_BLOCKS, TOK], F32R)
        f_lo = sb("f_lo", [128, FF_BLOCKS, TOK], F32R)
        gates = sb("gates", [128, 3 * KT, TOK])
        q_att = sb("q_att", [128, PAIRS, TOK])
        raw_qk = sb("raw_qk", [128, 2, TOK])
        raw_v = sb("raw_v", [128, 2, TOK])
        q_rot = sb("q_rot", [128, TOK])
        k_rot = sb("k_rot", [128, TOK])
        v_tok = sb("v_tok", [128, 2, 3, 128])
        probs = sb("probs", [128, 4 * 3 * TOK])
        prob = probs[:, 0:6 * TOK].rearrange("p (j t n) -> p j t n", j=2, t=3)
        prob_t = probs[:, 6 * TOK:12 * TOK].rearrange("p (j t n) -> p j t n", j=2, t=3)
        decay = probs[:, 0:2 * SPAN].rearrange("p (j n) -> p j n", j=2)
        head_bias = probs[:, 0:8 * 384].rearrange("p (h n) -> p h n", h=8)
        head_sq = sb("head_sq", [128, 2, TOK])
        head_rstd = sb("head_rstd", [128, 2, TOK])
        head_y = sb("head_y", [128, 2, TOK])
        row_sum = sb("row_sum", [128, TOK])
        rstd = sb("rstd", [128, TOK])
        small = sb("small", [128, 2, 4, 4])
        sink_col = sb("sink_col", [128, 2])
        decay_rate = sb("decay_rate", [128, 16])
        par = sb("par", [128, LAYERS, C_LAYER])
        lay = sb("lay", [128, C_LAYER])
        par2 = sb("par2", [128, C_SECOND])
        rope_t = sb("rope_t", [128, 8, TOK])
        dist = sb("dist", [128, 2, SPAN])
        mask = sb("mask", [128, 3, TOK])
        sq = sb("sq", [128, 10, 128])
        tri = sb("tri", [128, 2, 384])
        eps = sb("eps", [128, 2])
        def two_tiles(t):
            axes = "p a n -> p (a n)"
            return t[:, :, :].rearrange(axes)[:, 0:2 * 384].rearrange("p (j n) -> p j n", j=2)
        prob_flat = two_tiles(q_att)
        prob_tf = two_tiles(dist)
        log_rest = two_tiles(mask)
        start = gates[:, :, :].rearrange("p a n -> p (a n)")
        bmap, badd, brow = start[0:32, 0:512], start[0:8, 512:1024], start[0:8, 1024:1536]
        relb = sb("relb", [32, 8])
        wr = sb("wr", [128, KT, EXPERTS])
        rt = sb("rt", [128, 2, 12, 16])
        cmp = sb("cmp", [128, 2, 2, 64])
        gate_row = sb("gate_row", [EXPERTS, SEQ])
        early = sb("early", [128, 64])
        bias_dram = nc.dram_tensor("bias_dram", (8, 512), F32).ap()

        PERM_R, PERM_A, CENTER, IDENT, ONES_D, ONES_HEAD, ONES_HALF, AFTER, ALL_ONES, FLIP = range(10)
        lin = [ctx.enter_context(nc.psum_tensor(f"lin{i}", [128, 512], F32)) for i in range(2)]
        ps = [ctx.enter_context(nc.psum_tensor(f"ps{i}", [128, 512], F32)) for i in range(6)]

        landed = [sem(f"landed{i}") for i in range(SLOTS)]
        hi_ready = sem("hi_ready")
        split_ready = sem("split_ready")
        chunk_done = sem("chunk_done")
        acc_free = [sem("acc_free0"), sem("acc_free1")]
        consts = sem("consts")
        h_in_s = sem("h_in_s")
        bias_s = sem("bias_s")
        brow_s = sem("brow_s")
        bias_stored = sem("bias_stored")
        bmm_s = sem("bmm_s")
        lay_ready = sem("lay_ready")
        set_up = sem("set_up")
        rate_ready = sem("rate_ready")
        norm_sq, norm_sum, norm_bc, norm_rstd = sem("norm_sq"), sem("norm_sum"), sem("norm_bc"), sem("norm_rstd")
        h_ready = sem("h_ready")
        u_ready, u_hi, u_lo = sem("u_ready"), sem("u_hi"), sem("u_lo")
        gates_ready = sem("gates_ready")
        ret_raw, perm_done, ret_rot = sem("ret_raw"), sem("perm_done"), sem("ret_rot")
        v_turned, v_ready = sem("v_turned"), sem("v_ready")
        decay_arg, decay_ready = sem("decay_arg"), sem("decay_ready")
        scores, decayed = sem("scores"), sem("decayed")
        head_out, squared, var_done, head_rs = sem("head_out"), sem("squared"), sem("var_done"), sem("head_rs")
        y_ready, y_hi, y_lo = sem("y_ready"), sem("y_hi"), sem("y_lo")
        a_raw, a_perm, a_rot, a_vt, a_v = sem("a_raw"), sem("a_perm"), sem("a_rot"), sem("a_vt"), sem("a_v")
        a_stage, a_qperm, a_qrot = sem("a_stage"), sem("a_qperm"), sem("a_qrot")
        a_scores, a_max, a_exp, a_prob, a_pt, a_ptc, a_o, a_hi, a_lo = [
            sem("a_" + n) for n in ("scores", "max", "exp", "prob", "pt", "ptc", "o", "hi", "lo")]
        m_ready, m_hi, m_lo = sem("m_ready"), sem("m_hi"), sem("m_lo")
        mix_ready = sem("mix_ready")
        f_act, f_hi_s, f_lo_s = sem("f_act"), sem("f_hi_s"), sem("f_lo_s")
        y_sum = sem("y_sum")
        s_stage, s_vt, s_v, s_z = sem("s_stage"), sem("s_vt"), sem("s_v"), sem("s_z")
        s_abs, s_log, s_L, s_btw, s_arg, s_a, s_am = [sem("s_" + n) for n in ("abs", "log", "L", "btw", "arg", "a", "am")]
        s_o, s_sq, s_var, s_rs, s_y, s_hi, s_lo = [sem("s_" + n) for n in ("o", "sq", "var", "rs", "y", "hi", "lo")]
        d_S, d_max, d_exp, d_prob, d_pt, d_ptc = [sem("d_" + n) for n in ("S", "max", "exp", "prob", "pt", "ptc")]
        qkv_ready = sem("qkv_ready")
        r_ready = sem("r_ready")
        ln_s1, ln_mean, ln_c, ln_sq, ln_s2, ln_var, ln_rs, ln_out = [
            sem("ln_" + n) for n in ("s1", "mean", "c", "sq", "s2", "var", "rs", "out")]
        x1_hi, x1_lo = sem("x1_hi"), sem("x1_lo")
        logit_s, rt_max, rt_exp, rt_gate, rt_t, rt_row, rt_bc, rt_all = [
            sem("rt_" + n) for n in ("logit", "max", "exp", "gate", "t", "row", "bc", "all")]
        silu_s, hid_s, hid_hi, hid_lo = sem("silu_s"), sem("hid_s"), sem("hid_hi"), sem("hid_lo")
        out_s = sem("out_s")

        N_CONST = 12
        block = ctx.enter_context(nc.Block())

        def at(t, i, n=TOK, p=slice(0, 128)):
            if type(i) is int:
                return t[p, i, 0:n]
            return t[p, bass.ds(i, 1), 0:n].rearrange("p a n -> p (a n)")

        def col(t, i):
            return t[:, bass.ds(i, 1)] if type(i) is not int else t[:, i:i + 1]

        @block.sync
        def _(sp):
            sp.dma_start(h[:, :, :], h_in).then_inc(h_in_s, 16)
            for dst, src in ((par, layer_par), (par2, second_par), (rope_t, rope), (dist, toeplitz),
                             (mask, att_mask), (sq, squares), (tri, stick), (bmap, bias_map),
                             (badd, bias_add), (relb, rel_bias), (wr, w_router), (early, tie_order)):
                sp.dma_start(dst[tuple(slice(None) for _ in dst.shape)], src).then_inc(consts, 16)
            with sp.Fori(0, GROUPS) as g:
                for s in range(SLOTS):
                    sp.wait_ge(split_ready, g * SLOTS + (s + 1))
                    sp.dma_start(raw[:, s, :, :], weights[bass.ds(g * SLOTS + s, 1)].rearrange(
                        "a p (k m) -> p (a k) m", m=128)).then_inc(landed[s], 16)
            sp.wait_ge(ln_out, 2)
            sp.dma_start(out, wide[:, :, 0:SEQ]).then_inc(out_s, 16)
            sp.wait_ge(out_s, 16)

        @block.gpsimd
        def _(pool):
            pool.wait_ge(brow_s, 1)
            pool.dma_start(bias_dram, brow[:, :]).then_inc(bias_stored, 16)
            pool.wait_ge(bias_stored, 16)
            pool.wait_ge(mix_ready, LAYERS)
            for first, start, n in ((0, 128, 128), (128, 0, 256)):
                src = bass.AP(bias_dram.tensor, start, [[1, 128], [512, 8], [1, n]])
                pool.dma_start(head_bias[:, :, first:first + n], src).then_inc(bias_s, 16)

        @block.tensor
        def _(pe):
            def chunk_mm(g, s, bank, rhs, kts, n, first=True, last=True, lhs_k=0, done=True):
                hi, lo = rhs
                steps = len(kts)
                for i, k in enumerate(kts):
                    pe.matmul(lin[bank][:, 0:n], w_lo[:, s, lhs_k + i, :], hi[:, k, 0:n],
                              start=first and i == 0, stop=False)
                    pe.matmul(lin[bank][:, 0:n], w_hi[:, s, lhs_k + i, :], lo[:, k, 0:n],
                              start=False, stop=False)
                    mm = pe.matmul(lin[bank][:, 0:n], w_hi[:, s, lhs_k + i, :], hi[:, k, 0:n],
                                   start=False, stop=last and i == steps - 1)
                if done:
                    mm.then_inc(chunk_done, 1)
                return mm

            def chunk(g, s, bank, a, rhs, kts, n, first=True, last=True):
                pe.wait_ge(split_ready, g * SLOTS + (s + 1 + SLOTS))
                if first:
                    pe.wait_ge(acc_free[bank], a + 1)
                chunk_mm(g, s, bank, rhs, kts, n, first, last)

            def group(g, a, rhs, n):
                for s in range(SLOTS):
                    chunk(g, s, s % 2, a + s // 2, rhs, range(KT), n)

            def norm(w):
                pe.wait_ge(norm_sum, w + 1)
                pe.matmul(ps[0][:, 0:TOK], sq[:, ONES_D, :], row_sum[:, 0:TOK], start=True, stop=True)\
                    .then_inc(norm_bc, 1)

            X = (x_hi, x_lo)
            FF = (f_hi, f_lo)

            pe.sem_inc(chunk_done, SLOTS)
            pe.wait_ge(consts, 16 * N_CONST)
            pe.matmul(ps[5][0:8, :], relb[:, :], bmap[:, :], start=True, stop=True).then_inc(bmm_s, 1)

            with pe.Fori(0, LAYERS) as l:
                G = l * G_LAYER
                A = l * A_LAYER
                norm(l * 4)
                with pe.Fori(0, 2) as i:
                    pe.wait_ge(u_lo, l * 2 + 1)
                    group(G + G_GATE + i, A + A_GATE + i * 2, X, TOK)
                with pe.Fori(0, 4) as i:
                    group(G + G_SIG + i, A + A_SIG + i * 2, X, TOK)
                with pe.Fori(0, PAIRS) as i:
                    u = l * PAIRS + i
                    group(G + G_RET + i, A + A_RET + i * 2, X, TOK)
                    for j in range(2):
                        pe.wait_ge(ret_raw, u * 4 + j + 1)
                        pe.matmul(ps[j][:, 0:TOK], sq[:, PERM_R, :], raw_qk[:, j, :],
                                  start=True, stop=True).then_inc(perm_done, 1)
                    for j in range(2):
                        pe.wait_ge(ret_raw, u * 4 + j + 3)
                        for t, (t0, tn) in enumerate(TILES):
                            mm = pe.matmul(ps[2 + j][0:tn, t * 128:(t + 1) * 128], raw_v[:, j, t0:t0 + tn],
                                           sq[:, CENTER, :], start=True, stop=True)
                        mm.then_inc(v_turned, 1)
                    pe.wait_ge(ret_rot, u * 2 + 2)
                    bank = [[0, 1, 4], [5, 2, 3]]
                    for j in range(2):
                        p = slice(64 * j, 64 * j + 64)
                        if j == 1:
                            pe.wait_ge(v_ready, u * 2 + 2)
                        for t, (t0, tn) in enumerate(TILES):
                            mm = pe.matmul(ps[bank[j][t]][0:tn, 0:TOK], k_rot[p, t0:t0 + tn], q_rot[p, :],
                                           start=True, stop=True)
                        mm.then_inc(scores, 1)
                    for j in range(2):
                        pe.wait_ge(decayed, u * 2 + j + 1)
                        for t, (t0, tn) in enumerate(TILES):
                            mm = pe.matmul(ps[bank[j][0]][:, 0:TOK], v_tok[0:tn, j, t, :], prob_t[0:tn, j, t, :],
                                           start=t == 0, stop=t == 2)
                        mm.then_inc(head_out, 1)
                    for j in range(2):
                        pe.wait_ge(squared, u * 2 + j + 1)
                        pe.matmul(ps[bank[j][1]][:, 0:TOK], sq[:, ONES_HEAD, :], head_sq[:, j, :],
                                  start=True, stop=True).then_inc(var_done, 1)
                for s in range(SLOTS):
                    chunk(G + G_ATT, s, s % 2, A + A_ATT + s // 2, X, range(KT), TOK)
                for s in range(2):
                    chunk(G + G_ATT + 1, s, s % 2, A + A_ATT + 2, X, range(KT), TOK)
                for s in range(2, SLOTS):
                    pe.drain()
                    pe.wait_ge(split_ready, (G + G_ATT + 1) * SLOTS + (s + 1 + SLOTS))
                    pe.sem_inc(chunk_done, 1)
                pe.wait_ge(a_raw, l * 2 + 1)
                pe.matmul(ps[0][:, 0:TOK], sq[:, PERM_A, :], raw_qk[:, 1, :], start=True, stop=True)\
                    .then_inc(a_perm, 1)
                pe.wait_ge(a_raw, l * 2 + 2)
                for t, (t0, tn) in enumerate(TILES):
                    mm = pe.matmul(ps[2][0:tn, t * 128:(t + 1) * 128], raw_v[:, 0, t0:t0 + tn],
                                   sq[:, IDENT, :], start=True, stop=True)
                mm.then_inc(a_vt, 1)
                with pe.Fori(0, PAIRS) as i:
                    u = l * PAIRS + i
                    pe.wait_ge(a_rot, l + 1)
                    pe.wait_ge(a_v, l + 1)
                    pe.wait_ge(a_stage, u + 1)
                    pe.matmul(ps[0][:, 0:TOK], sq[:, PERM_A, :], raw_qk[:, 0, :], start=True, stop=True)\
                        .then_inc(a_qperm, 1)
                    pe.wait_ge(a_qrot, u + 1)
                    for j in range(2):
                        p = slice(64 * j, 64 * j + 64)
                        for t, (t0, tn) in enumerate(TILES):
                            mm = pe.matmul(ps[3 * j + t][0:tn, 0:TOK], q_rot[p, t0:t0 + tn], k_rot[p, :],
                                           start=True, stop=True)
                        mm.then_inc(a_scores, 1)
                    for j in range(2):
                        pe.wait_ge(a_prob, u * 2 + j + 1)
                        for k, (k0, kn) in enumerate(TILES):
                            for t, (t0, tn) in enumerate(TILES):
                                mm = pe.transpose(ps[3 * j + k][0:kn, t0:t0 + tn], prob[0:tn, j, t, k0:k0 + kn],
                                                  sq[0:tn, IDENT, 0:tn])
                        mm.then_inc(a_pt, 1)
                    for j in range(2):
                        p = slice(64 * j, 64 * j + 64)
                        pe.wait_ge(a_ptc, u * 2 + j + 1)
                        for k, (k0, kn) in enumerate(TILES):
                            mm = pe.matmul(ps[3 * j][p, 0:TOK], v_tok[0:kn, 0, k, p], prob_t[0:kn, j, k, :],
                                           start=k == 0, stop=k == 2)
                        mm.then_inc(a_o, 1)
                with pe.Fori(0, 2) as i:
                    pe.wait_ge(y_lo, (l + 1) * 2 * PAIRS)
                    group(G + G_RETO + i, A + A_RETO + i * 2, FF, TOK)
                pe.wait_ge(a_lo, (l + 1) * 2 * PAIRS)
                for s in range(SLOTS):
                    pe.wait_ge(split_ready, (G + G_ATTO) * SLOTS + (s + 1 + SLOTS))
                    for b in range(2):
                        pe.wait_ge(acc_free[b], A + A_ATTO + s + 1)
                        chunk_mm(0, s, b, FF, range(8, 12), TOK, lhs_k=4 * b, done=b == 1)
                with pe.Fori(0, 2) as i:
                    pe.wait_ge(m_lo, l + 1)
                    group(G + G_MIX + i, A + A_MIX + i * 2, X, TOK)
                norm(l * 4 + 1)
                norm(l * 4 + 2)
                with pe.Fori(0, FF_HALVES) as f:
                    with pe.Fori(0, 4) as i:
                        pe.wait_ge(u_lo, l * 2 + 2)
                        group(G + G_FF + f * G_HALF + i, A + A_FF + f * A_HALF + i * 2, X, TOK)
                    with pe.Fori(0, 4) as i:
                        pe.wait_ge(f_lo_s, (l * FF_HALVES + f + 1) * FF_BLOCKS)
                        for s in range(SLOTS):
                            chunk(G + G_FF + 4 + f * G_HALF + i, s, s // 2, A + A_FF + 8 + f * A_HALF + i, FF,
                                  range(KT * (s % 2), KT * (s % 2) + KT), TOK, first=s % 2 == 0, last=s % 2 == 1)
                norm(l * 4 + 3)

            pe.wait_ge(x1_lo, 1)
            with pe.Fori(0, 6) as i:
                group(i + G_QKV, i * 2 + A_QKV, X, SEQ)

            def stage_values(u):
                pe.wait_ge(s_stage, u + 1)
                for t in range(2):
                    mm = pe.matmul(ps[2][:, t * 128:(t + 1) * 128], raw_v[:, 0, t * 128:(t + 1) * 128],
                                   sq[:, IDENT, :], start=True, stop=True)
                mm.then_inc(s_vt, 1)

            def head_output(u, ready):
                pe.wait_ge(s_v, u + 1)
                for j in range(2):
                    p = slice(64 * j, 64 * j + 64)
                    pe.wait_ge(ready, ready_at(u, j))
                    pe.matmul(ps[4][p, 0:SEQ], v_tok[:, 0, 0, p], prob_tf[:, j, 0:SEQ], start=True, stop=False)
                    mm = pe.matmul(ps[4][p, 128:SEQ], v_tok[:, 0, 1, p], prob_tf[:, j, SEQ:384],
                                   start=False, stop=True)
                mm.then_inc(s_o, 1)
                pe.wait_ge(s_sq, u + 1)
                pe.matmul(ps[5][:, 0:SEQ], sq[:, ONES_HALF, :], head_sq[:, 0, 0:SEQ], start=True, stop=True)\
                    .then_inc(s_var, 1)

            with pe.Fori(0, PAIRS) as u:
                def ready_at(u, j):
                    return u * 2 + j + 1
                stage_values(u)
                for j in range(2):
                    p = slice(64 * j, 64 * j + 64)
                    pe.matmul(ps[j][:, 0:SEQ], raw_qk[p, 1, 0:128], raw_qk[p, 0, 0:SEQ], start=True, stop=True)
                    pe.matmul(ps[j][:, SEQ:384], raw_qk[p, 1, 128:SEQ], raw_qk[p, 0, 128:SEQ],
                              start=True, stop=True).then_inc(s_z, 1)
                for j in range(2):
                    pe.wait_ge(s_L, u * 2 + j + 1)
                    L = log_rest[:, j, :]
                    pe.matmul(ps[j][:, 0:SEQ], sq[:, AFTER, :], L[:, 0:SEQ], start=True, stop=False)
                    pe.matmul(ps[j][:, 128:SEQ], sq[:, ALL_ONES, :], L[:, SEQ:384], start=False, stop=True)
                    pe.matmul(ps[j][:, SEQ:384], sq[:, AFTER, :], L[:, SEQ:384], start=True, stop=True)\
                        .then_inc(s_btw, 1)
                head_output(u, s_am)

            pe.wait_ge(bias_s, 32)
            with pe.Fori(0, PAIRS) as n:
                def ready_at(u, j):
                    return (u - PAIRS) * 2 + j + 1
                u = n + PAIRS
                stage_values(u)
                for j in range(2):
                    p = slice(64 * j, 64 * j + 64)
                    pe.matmul(ps[j][:, 0:384], sq[:, FLIP, :], at(head_bias, n * 2 + j, 384),
                              start=True, stop=False)
                    pe.matmul(ps[j][:, 0:128], raw_qk[p, 0, 0:128], raw_qk[p, 1, 0:128],
                              start=False, stop=False)
                    pe.matmul(ps[j][:, 128:384], raw_qk[p, 0, 128:SEQ], raw_qk[p, 1, 0:SEQ],
                              start=False, stop=True).then_inc(d_S, 1)
                for j in range(2):
                    pe.wait_ge(d_prob, n * 2 + j + 1)
                    P = prob_flat[:, j, :]
                    pe.transpose(ps[j][:, 0:128], P[:, 0:128], sq[:, IDENT, :])
                    pe.transpose(ps[j][:, 128:256], P[:, 128:256], sq[:, IDENT, :])
                    pe.transpose(ps[j][:, 256:384], P[:, 256:384], sq[:, IDENT, :]).then_inc(d_pt, 1)
                head_output(u, d_ptc)

            pe.wait_ge(s_lo, 2 * PAIRS)
            with pe.Fori(0, 2) as i:
                group(i + G_OUT, i * 2 + A_OUT, X, SEQ)

            def layer_norm(k):
                pe.wait_ge(ln_s1, k + 1)
                pe.matmul(ps[0][:, 0:SEQ], sq[:, ONES_D, :], row_sum[:, 0:SEQ], start=True, stop=True)\
                    .then_inc(ln_mean, 1)
                pe.wait_ge(ln_s2, k + 1)
                pe.matmul(ps[1][:, 0:SEQ], sq[:, ONES_D, :], row_sum[:, 0:SEQ], start=True, stop=True)\
                    .then_inc(ln_var, 1)

            layer_norm(0)
            pe.wait_ge(ln_out, 1)
            for t in range(2):
                for k in range(KT):
                    mm = pe.matmul(ps[2][:, t * 16:(t + 1) * 16], h[:, k, t * 128:(t + 1) * 128], wr[:, k, :],
                                   start=k == 0, stop=k == KT - 1)
            mm.then_inc(logit_s, 1)
            pe.wait_ge(rt_gate, 1)
            for t in range(2):
                mm = pe.transpose(ps[3][0:EXPERTS, t * 128:(t + 1) * 128], rt[:, t, 11, :], sq[:, IDENT, :])
            mm.then_inc(rt_t, 1)
            pe.wait_ge(rt_row, 1)
            for e in range(EXPERTS):
                if e >= 2:
                    pe.wait_ge(rt_all, e - 1)
                pe.matmul(ps[4 + e % 2][:, 0:SEQ], sq[0:EXPERTS, IDENT, e:e + 1].broadcast_to((EXPERTS, 128)), gate_row[:, :], start=True, stop=True)\
                    .then_inc(rt_bc, 1)

            pe.wait_ge(x1_lo, 2)
            with pe.Fori(0, EXPERTS) as e:
                with pe.Fori(0, 4) as i:
                    group(e * 6 + i + G_EXP, e * 12 + i * 2 + A_EXP, X, SEQ)
                with pe.Fori(0, 2) as i:
                    pe.wait_ge(hid_lo, e * KT + KT)
                    group(e * 6 + i + (G_EXP + 4), e * 12 + i * 2 + (A_EXP + 8), FF, SEQ)
            layer_norm(1)

        @block.scalar
        def _(act):
            A_ = nc.scalar.activation

            def split(g, s):
                act.wait_ge(landed[s], (g + 1) * 16)
                act.wait_ge(chunk_done, g * SLOTS + (s + 1))
                A_(w_hi[:, s, :, :], raw[:, s, :, :], ACT.Copy).then_inc(hi_ready, 1)

            def ahead(g, s):
                split(g + (s + 2) // SLOTS, (s + 2) % SLOTS)

            def product(g, s):
                act.wait_ge(chunk_done, g * SLOTS + (s + 1 + SLOTS))

            def power_half(dst, src, scale, bias):
                A_(dst, src, ACT.Ln, scale=scale, bias=bias)
                act.drain()
                return A_(dst, dst, ACT.Exp, scale=-0.5)

            def evac(g, s, dst, func=ACT.Copy, scale=1.0):
                product(g, s)
                return A_(dst, lin[s % 2][:, 0:TOK], func, scale=scale)

            act.wait_ge(set_up, 1)
            split(0, 0)
            split(0, 1)

            with act.Fori(0, LAYERS) as l:
                G = l * G_LAYER
                load_exp_ln(nc, act)
                act.wait_ge(lay_ready, l + 1)
                A_(decay_rate[:, :], lay[:, C_DECAY:C_DECAY + 16], ACT.Exp).then_inc(rate_ready, 1)
                act.wait_ge(h_ready, l * 2 + 1)
                A_(wide[:, :, :], h[:, :, :], ACT.Square).then_inc(norm_sq, 1)
                act.wait_ge(norm_bc, l * 4 + 1)
                power_half(rstd[:, :], ps[0][:, 0:TOK], 1.0, eps[:, 0:1]).then_inc(norm_rstd, 1)
                for k in range(KT):
                    act.wait_ge(u_ready, (l * 2) * KT + k + 1)
                    A_(x_hi[:, k, :], wide[:, k, :], ACT.Copy).then_inc(u_hi, 1)
                act.wait_ge(bias_stored, 16)
                with act.Fori(0, 2) as i:
                    for s in range(SLOTS):
                        ahead(G + G_GATE + i, s)
                        evac(G + G_GATE + i, s, at(gates, i * 4 + s), ACT.Silu).then_inc(acc_free[s % 2], 1)
                with act.Fori(0, 4) as i:
                    for s in range(SLOTS):
                        ahead(G + G_SIG + i, s)
                        evac(G + G_SIG + i, s, at(gates, i * 4 + (s + KT)), ACT.Sigmoid).then_inc(acc_free[s % 2], 1)
                act.drain().then_inc(gates_ready, 1)
                load_exp_ln(nc, act)
                with act.Fori(0, PAIRS) as i:
                    u = l * PAIRS + i
                    g = G + G_RET + i
                    for j in range(2):
                        act.wait_ge(decay_arg, u * 2 + j + 1)
                        A_(decay[:, j, :], decay[:, j, :], ACT.Exp, scale=-1.0).then_inc(decay_ready, 1)
                    for s in range(SLOTS):
                        ahead(g, s)
                        product(g, s)
                        dst = raw_qk[:, s, :] if s < 2 else raw_v[:, s - 2, :]
                        A_(dst, lin[s % 2][:, 0:TOK], ACT.Copy).then_inc(ret_raw, 1)
                        act.drain().then_inc(acc_free[s % 2], 1)
                    for j in range(2):
                        act.wait_ge(v_turned, u * 2 + j + 1)
                        A_(v_tok[:, j, 0:2, :], ps[2 + j][:, 0:256].rearrange("p (t n) -> p t n", t=2), ACT.Copy)
                        A_(v_tok[0:16, j, 2, :], ps[2 + j][0:16, 256:384], ACT.Copy).then_inc(v_ready, 1)
                    for j in range(2):
                        act.wait_ge(head_out, u * 2 + j + 1)
                        A_(head_sq[:, j, :], ps[(0, 5)[j]][:, 0:TOK], ACT.Square).then_inc(squared, 1)
                    for j in range(2):
                        act.wait_ge(var_done, u * 2 + j + 1)
                        power_half(head_rstd[:, j, :], ps[(1, 2)[j]][:, 0:TOK], 1.0, eps[:, 0:1]).then_inc(head_rs, 1)
                    for j in range(2):
                        act.wait_ge(y_ready, u * 2 + j + 1)
                        A_(at(f_hi, i * 2 + j), head_y[:, j, :], ACT.Copy).then_inc(y_hi, 1)
                for s in range(SLOTS):
                    g = G + G_ATT
                    ahead(g, s)
                    product(g, s)
                    if s < 2:
                        dst = raw_qk[:, 1, :] if s == 0 else raw_v[:, 0, :]
                        A_(dst, lin[s % 2][:, 0:TOK], ACT.Copy).then_inc(a_raw, 1)
                        act.drain().then_inc(acc_free[s % 2], 1)
                    else:
                        A_(q_att[:, s - 2, :], lin[s % 2][:, 0:TOK], ACT.Copy).then_inc(acc_free[s % 2], 1)
                for s in range(SLOTS):
                    g = G + G_ATT + 1
                    ahead(g, s)
                    if s < 2:
                        product(g, s)
                        A_(q_att[:, s + 2, :], lin[s % 2][:, 0:TOK], ACT.Copy).then_inc(acc_free[s % 2], 1)
                act.wait_ge(a_vt, l + 1)
                A_(v_tok[:, 0, 0:2, :], ps[2][:, 0:256].rearrange("p (t n) -> p t n", t=2), ACT.Copy)
                A_(v_tok[0:16, 0, 2, :], ps[2][0:16, 256:384], ACT.Copy).then_inc(a_v, 1)
                act.drain()
                with act.Fori(0, PAIRS) as i:
                    u = l * PAIRS + i
                    A_(raw_qk[:, 0, :], at(q_att, i), ACT.Copy).then_inc(a_stage, 1)
                    for j in range(2):
                        act.wait_ge(a_max, u * 2 + j + 1)
                        for t, (t0, tn) in enumerate(TILES):
                            A_(prob[0:tn, j, t, :], prob[0:tn, j, t, :], ACT.Exp, bias=small[0:tn, j, 1, t:t + 1],
                               accum_out=small[0:tn, j, 2, t:t + 1])
                        for t, (t0, tn) in enumerate(TILES):
                            mm = A_(small[0:tn, j, 3, t:t + 1], sink_col[0:tn, j:j + 1], ACT.Exp,
                                    bias=small[0:tn, j, 1, t:t + 1])
                        mm.then_inc(a_exp, 1)
                    for j in range(2):
                        act.wait_ge(a_pt, u * 2 + j + 1)
                        for k, (k0, kn) in enumerate(TILES):
                            mm = A_(prob_t[0:kn, j, k, :], ps[3 * j + k][0:kn, 0:TOK], ACT.Copy)
                        mm.then_inc(a_ptc, 1)
                    for j in range(2):
                        p = slice(64 * j, 64 * j + 64)
                        act.wait_ge(a_o, u * 2 + j + 1)
                        A_(at(f_hi, i + 8, p=p), ps[3 * j][p, 0:TOK], ACT.Copy).then_inc(a_hi, 1)
                    act.wait_ge(a_lo, u * 2 + 2)
                with act.Fori(0, 2) as i:
                    for s in range(SLOTS):
                        ahead(G + G_RETO + i, s)
                for s in range(SLOTS):
                    ahead(G + G_ATTO, s)
                for k in range(KT):
                    act.wait_ge(m_ready, l * KT + k + 1)
                    A_(x_hi[:, k, :], wide[:, k, :], ACT.Copy).then_inc(m_hi, 1)
                with act.Fori(0, 2) as i:
                    for s in range(SLOTS):
                        ahead(G + G_MIX + i, s)
                        if s == 0:
                            act.wait_ge(m_lo, l + 1)
                        evac(G + G_MIX + i, s, at(wide, i * 4 + s)).then_inc(acc_free[s % 2], 1)
                act.drain().then_inc(mix_ready, 1)
                A_(gates[:, 0:KT, :], wide[:, :, :], ACT.Square).then_inc(norm_sq, 1)
                act.wait_ge(norm_bc, l * 4 + 2)
                power_half(rstd[:, :], ps[0][:, 0:TOK], 1.0, eps[:, 0:1]).then_inc(norm_rstd, 1)
                act.wait_ge(h_ready, l * 2 + 2)
                A_(wide[:, :, :], h[:, :, :], ACT.Square).then_inc(norm_sq, 1)
                act.wait_ge(norm_bc, l * 4 + 3)
                power_half(rstd[:, :], ps[0][:, 0:TOK], 1.0, eps[:, 0:1]).then_inc(norm_rstd, 1)
                for k in range(KT):
                    act.wait_ge(u_ready, (l * 2 + 1) * KT + k + 1)
                    A_(x_hi[:, k, :], wide[:, k, :], ACT.Copy).then_inc(u_hi, 1)
                with act.Fori(0, FF_HALVES) as f:
                    with act.Fori(0, 4) as i:
                        for s in range(SLOTS):
                            ahead(G + G_FF + f * G_HALF + i, s)
                            act.wait_ge(f_act, (l * FF_HALVES + f) * FF_BLOCKS + i * 4 + (s + 1))
                            A_(at(f_hi, i * 4 + s), head_y[:, s % 2, :], ACT.Copy).then_inc(f_hi_s, 1)
                    with act.Fori(0, 4) as i:
                        for s in range(SLOTS):
                            ahead(G + G_FF + 4 + f * G_HALF + i, s)
                act.wait_ge(y_sum, l + 1)
                A_(gates[:, 0:KT, :], wide[:, :, :], ACT.Square).then_inc(norm_sq, 1)
                act.wait_ge(norm_bc, l * 4 + 4)
                power_half(rstd[:, :], ps[0][:, 0:TOK], 1.0, eps[:, 0:1]).then_inc(norm_rstd, 1)

            act.wait_ge(h_ready, 2 * LAYERS + 1)
            A_(x_hi[:, :, 0:SEQ], h[:, :, META:TOK], ACT.Copy).then_inc(x1_hi, 1)
            with act.Fori(0, 6) as i:
                for s in range(SLOTS):
                    ahead(i + G_QKV, s)
                    product(i + G_QKV, s)
                    A_(at(gates, i * 4 + s, SEQ), lin[s % 2][:, 0:SEQ], ACT.Copy).then_inc(acc_free[s % 2], 1)
            act.drain()

            def stage(block0, u):
                A_(raw_qk[:, 0, 0:SEQ], at(gates, block0, SEQ), ACT.Copy, scale=0.125)
                A_(raw_qk[:, 1, 0:SEQ], at(gates, block0 + 1, SEQ), ACT.Copy)
                A_(raw_v[:, 0, 0:SEQ], at(gates, block0 + 2, SEQ), ACT.Copy)
                act.drain().then_inc(s_stage, 1)
                act.wait_ge(s_vt, u + 1)
                A_(v_tok[:, 0, 0:2, :], ps[2][:, 0:256].rearrange("p (t n) -> p t n", t=2), ACT.Copy)\
                    .then_inc(s_v, 1)

            def finish(u):
                act.wait_ge(s_o, u + 1)
                A_(head_sq[:, 0, 0:SEQ], ps[4][:, 0:SEQ], ACT.Square).then_inc(s_sq, 1)
                act.wait_ge(s_var, u + 1)
                power_half(head_rstd[:, 0, 0:SEQ], ps[5][:, 0:SEQ], 1.0, eps[:, 0:1]).then_inc(s_rs, 1)
                act.wait_ge(s_y, u + 1)
                A_(at(x_hi, u, SEQ), head_y[:, 0, 0:SEQ], ACT.Copy).then_inc(s_hi, 1)
                act.wait_ge(s_lo, u + 1)

            with act.Fori(0, PAIRS) as u:
                stage(u * 3, u)
                for j in range(2):
                    act.wait_ge(s_z, u * 2 + j + 1)
                    t = prob_flat[:, j, :]
                    A_(t, ps[j][:, 0:384], ACT.Abs)
                    act.drain()
                    A_(t, t, ACT.Exp, scale=-1.0)
                    act.drain()
                    A_(t, t, ACT.Ln, bias=1.0).then_inc(s_log, 1)
                for j in range(2):
                    act.wait_ge(s_arg, u * 2 + j + 1)
                    A_(prob_tf[:, j, :], prob_flat[:, j, :], ACT.Exp).then_inc(s_a, 1)
                finish(u)
            with act.Fori(0, PAIRS) as n:
                u = n + PAIRS
                stage(n * 3 + 12, u)
                for j in range(2):
                    act.wait_ge(d_max, n * 2 + j + 1)
                    P = prob_flat[:, j, :]
                    A_(P[:, 0:128], ps[j][:, 0:128], ACT.Exp, bias=small[:, j, 1, 0:1], accum_out=small[:, j, 2, 0:1])
                    A_(P[:, 128:384], ps[j][:, 128:384], ACT.Exp, bias=small[:, j, 1, 1:2],
                       accum_out=small[:, j, 2, 1:2]).then_inc(d_exp, 1)
                for j in range(2):
                    act.wait_ge(d_pt, n * 2 + j + 1)
                    T = prob_tf[:, j, :]
                    A_(T, ps[j][:, 0:384], ACT.Copy).then_inc(d_ptc, 1)
                finish(u)
            with act.Fori(0, 2) as i:
                for s in range(SLOTS):
                    ahead(i + G_OUT, s)

            def layer_norm(k):
                act.wait_ge(ln_c, k + 1)
                A_(gates[:, 0:KT, 0:SEQ], wide[:, :, 0:SEQ], ACT.Square).then_inc(ln_sq, 1)
                act.wait_ge(ln_var, k + 1)
                power_half(rstd[:, 0:SEQ], ps[1][:, 0:SEQ], 1.0, eps[:, 1:2]).then_inc(ln_rs, 1)

            layer_norm(0)
            act.wait_ge(ln_out, 1)
            A_(x_hi[:, :, 0:SEQ], h[:, :, 0:SEQ], ACT.Copy).then_inc(x1_hi, 1)
            act.wait_ge(rt_max, 1)
            for t in range(2):
                mm = A_(rt[:, t, 2, :], rt[:, t, 0, :], ACT.Exp, bias=rt[:, t, 1, 0:1], accum_out=rt[:, t, 1, 1:2])
            mm.then_inc(rt_exp, 1)
            for e in range(EXPERTS):
                act.wait_ge(rt_bc, e + 1)
                A_(gates[:, e, 0:SEQ], ps[4 + e % 2][:, 0:SEQ], ACT.Copy).then_inc(rt_all, 1)
            with act.Fori(0, EXPERTS) as e:
                with act.Fori(0, 4) as i:
                    g = e * 6 + i + G_EXP
                    for j in range(2):
                        ahead(g, 2 * j)
                        product(g, 2 * j)
                        A_(raw_v[:, j, 0:SEQ], lin[0][:, 0:SEQ], ACT.Silu).then_inc(acc_free[0], 1)
                        act.drain().then_inc(silu_s, 1)
                        ahead(g, 2 * j + 1)
                        act.wait_ge(hid_s, e * 8 + i * 2 + (j + 1))
                        A_(at(f_hi, i * 2 + j, SEQ), head_y[:, j, 0:SEQ], ACT.Copy).then_inc(hid_hi, 1)
                with act.Fori(0, 2) as i:
                    for s in range(SLOTS):
                        ahead(e * 6 + i + (G_EXP + 4), s)
            load_exp_ln(nc, act)
            layer_norm(1)

        @block.vector
        def _(dve):
            TT, TS, STT = nc.vector.tensor_tensor, nc.vector.tensor_scalar, nc.vector.scalar_tensor_tensor

            def split(g, s):
                dve.wait_ge(hi_ready, g * SLOTS + (s + 1))
                TT(w_lo[:, s, :, :], raw[:, s, :, :], w_hi[:, s, :, :], ALU.subtract).then_inc(split_ready, 1)

            def ahead(g, s):
                split(g + (s + 2) // SLOTS, (s + 2) % SLOTS)

            def product(g, s):
                dve.wait_ge(chunk_done, g * SLOTS + (s + 1 + SLOTS))

            def norm_sums(w, src):
                dve.wait_ge(norm_sq, w + 1)
                nc.vector.tensor_reduce(row_sum[:, :], src[:, 0:KT, :].rearrange("p k n -> p n k"), AX.X, ALU.add)\
                    .then_inc(norm_sum, 1)
                dve.wait_ge(norm_rstd, w + 1)

            def scaled_input(w, which, gain):
                norm_sums(w, wide)
                for k in range(KT):
                    STT(wide[:, k, :], h[:, k, :], lay[:, gain + k:gain + k + 1], rstd[:, :],
                        ALU.mult, ALU.mult).then_inc(u_ready, 1)
                for k in range(KT):
                    dve.wait_ge(u_hi, which * KT + k + 1)
                    TT(x_lo[:, k, :], wide[:, k, :], x_hi[:, k, :], ALU.subtract)
                dve.drain().then_inc(u_lo, 1)

            def add_normed(w, gain):
                norm_sums(w, gates)
                for k in range(KT):
                    STT(wide[:, k, :], wide[:, k, :], lay[:, gain + k:gain + k + 1], rstd[:, :], ALU.mult, ALU.mult)
                dve.drain()
                for k in range(KT):
                    TT(h[:, k, :], h[:, k, :], wide[:, k, :], ALU.add)
                dve.drain().then_inc(h_ready, 1)

            def rope(dst, raw_in, turned, tab):
                TT(head_sq[:, 0, :], raw_in, rope_t[:, tab, :], ALU.mult)
                TT(head_sq[:, 1, :], turned, rope_t[:, tab + 1, :], ALU.mult)
                dve.drain()
                return TT(dst, head_sq[:, 0, :], head_sq[:, 1, :], ALU.add)

            dve.memset(eps[:, 0:1], RMS_EPS)
            dve.memset(eps[:, 1:2], LN_EPS)
            dve.memset(small[:, :, :, :], 1.0)
            dve.drain().then_inc(set_up, 1)
            dve.sem_inc(split_ready, SLOTS)
            dve.sem_inc(acc_free[0], 1)
            dve.sem_inc(acc_free[1], 1)
            dve.wait_ge(h_in_s, 16)
            dve.wait_ge(consts, 16 * N_CONST)
            dve.sem_inc(h_ready, 1)
            dve.wait_ge(bmm_s, 1)
            TT(brow[:, :], ps[5][0:8, :], badd[:, :], ALU.add).then_inc(brow_s, 1)
            split(0, 0)
            split(0, 1)

            with dve.Fori(0, LAYERS) as l:
                G = l * G_LAYER
                nc.vector.tensor_copy(lay[:, :], at(par, l, C_LAYER)).then_inc(lay_ready, 1)
                dve.drain()
                scaled_input(l * 4, l * 2, C_GAIN)
                with dve.Fori(0, 6) as i:
                    for s in range(SLOTS):
                        ahead(G + G_GATE + i, s)
                with dve.Fori(0, PAIRS) as i:
                    dve.wait_ge(gates_ready, l + 1)
                    dve.wait_ge(rate_ready, l + 1)
                    u = l * PAIRS + i
                    g = G + G_RET + i
                    for j in range(2):
                        TS(decay[:, j, :], dist[:, 0, :], col(decay_rate, i * 2 + j), None, ALU.mult)
                    dve.drain()
                    for j in range(2):
                        STT(decay[:, j, :], dist[:, 1, :], col(decay_rate, i * 2 + (8 + j)), decay[:, j, :],
                            ALU.mult, ALU.add).then_inc(decay_arg, 1)
                    ahead(g, 0)
                    ahead(g, 1)
                    ahead(g, 2)
                    for j in range(2):
                        dve.wait_ge(perm_done, u * 2 + j + 1)
                        rope((q_rot, k_rot)[j][:, :], raw_qk[:, j, :], ps[j][:, 0:TOK], 2 * j).then_inc(ret_rot, 1)
                        dve.drain()
                        if j == 0:
                            ahead(g, 3)
                    for j in range(2):
                        dve.wait_ge(scores, u * 2 + j + 1)
                        dve.wait_ge(decay_ready, u * 2 + j + 1)
                        for t, (t0, tn) in enumerate(TILES):
                            TT(prob_t[0:tn, j, t, :], ps[((0, 1, 4), (5, 2, 3))[j][t]][0:tn, 0:TOK],
                               decay[0:tn, j, 256 - t0:256 - t0 + TOK], ALU.mult)
                        dve.drain().then_inc(decayed, 1)
                    for j in range(2):
                        dve.wait_ge(head_rs, u * 2 + j + 1)
                        TT(head_y[:, j, :], ps[(0, 5)[j]][:, 0:TOK], head_rstd[:, j, :], ALU.mult)
                    dve.drain()
                    for j in range(2):
                        TT(head_y[:, j, :], head_y[:, j, :], at(gates, i * 2 + j), ALU.mult)
                    dve.drain().then_inc(y_ready, 2)
                    for j in range(2):
                        dve.wait_ge(y_hi, u * 2 + j + 1)
                        TT(at(f_lo, i * 2 + j), head_y[:, j, :], at(f_hi, i * 2 + j), ALU.subtract)
                    dve.drain().then_inc(y_lo, 2)
                for s in range(SLOTS):
                    ahead(G + G_ATT, s)
                for s in range(SLOTS):
                    ahead(G + G_ATT + 1, s)
                dve.wait_ge(a_perm, l + 1)
                rope(k_rot[:, :], raw_qk[:, 1, :], ps[0][:, 0:TOK], 6).then_inc(a_rot, 1)
                dve.drain()
                with dve.Fori(0, PAIRS) as i:
                    u = l * PAIRS + i
                    dve.wait_ge(a_qperm, u + 1)
                    rope(q_rot[:, :], raw_qk[:, 0, :], ps[0][:, 0:TOK], 4).then_inc(a_qrot, 1)
                    dve.drain()
                    for j in range(2):
                        dve.wait_ge(a_scores, u * 2 + j + 1)
                        nc.vector.tensor_copy(sink_col[:, j:j + 1], col(lay, i * 2 + (C_SINK + j)))
                        dve.drain()
                        for t, (t0, tn) in enumerate(TILES):
                            nc.vector.tensor_tensor_reduce(
                                prob[0:tn, j, t, :], ps[3 * j + t][0:tn, 0:TOK], mask[0:tn, t, :], 1.0,
                                sink_col[0:tn, j:j + 1], ALU.add, ALU.max, small[0:tn, j, 0, t:t + 1])
                        dve.drain()
                        TS(small[:, j, 1, 0:3], small[:, j, 0, 0:3], -1.0, None, ALU.mult).then_inc(a_max, 1)
                    for j in range(2):
                        dve.wait_ge(a_exp, u * 2 + j + 1)
                        TT(small[:, j, 2, 0:3], small[:, j, 2, 0:3], small[:, j, 3, 0:3], ALU.add)
                        dve.drain()
                        nc.vector.reciprocal(small[:, j, 2, 0:3], small[:, j, 2, 0:3])
                        dve.drain()
                        for t, (t0, tn) in enumerate(TILES):
                            TS(prob[0:tn, j, t, :], prob[0:tn, j, t, :], small[0:tn, j, 2, t:t + 1], None, ALU.mult)
                        dve.drain().then_inc(a_prob, 1)
                    for j in range(2):
                        p = slice(64 * j, 64 * j + 64)
                        dve.wait_ge(a_hi, u * 2 + j + 1)
                        TT(at(f_lo, i + 8, p=p), ps[3 * j][p, 0:TOK], at(f_hi, i + 8, p=p), ALU.subtract)\
                            .then_inc(a_lo, 1)
                with dve.Fori(0, 2) as i:
                    for s in range(SLOTS):
                        ahead(G + G_RETO + i, s)
                        product(G + G_RETO + i, s)
                        TT(at(wide, i * 4 + s), lin[s % 2][:, 0:TOK], at(gates, i * 4 + (s + KT)), ALU.mult)\
                            .then_inc(acc_free[s % 2], 1)
                dve.drain()
                for s in range(SLOTS):
                    ahead(G + G_ATTO, s)
                    product(G + G_ATTO, s)
                    for b in range(2):
                        TT(head_y[:, b, :], lin[b][:, 0:TOK], gates[:, 2 * KT + 2 * s + b, :], ALU.mult)\
                            .then_inc(acc_free[b], 1)
                    dve.drain()
                    for b in range(2):
                        TT(wide[:, 2 * s + b, :], wide[:, 2 * s + b, :], head_y[:, b, :], ALU.add)\
                            .then_inc(m_ready, 1)
                    dve.drain()
                for k in range(KT):
                    dve.wait_ge(m_hi, l * KT + k + 1)
                    TT(x_lo[:, k, :], wide[:, k, :], x_hi[:, k, :], ALU.subtract)
                dve.drain().then_inc(m_lo, 1)
                with dve.Fori(0, 2) as i:
                    for s in range(SLOTS):
                        ahead(G + G_MIX + i, s)
                dve.wait_ge(mix_ready, l + 1)
                add_normed(l * 4 + 1, C_GAIN + 8)
                scaled_input(l * 4 + 2, l * 2 + 1, C_GAIN + 16)
                dve.memset(wide[:, :, :], 0.0)
                dve.drain()
                with dve.Fori(0, FF_HALVES) as f:
                    with dve.Fori(0, 4) as i:
                        g = G + G_FF + f * G_HALF + i
                        n = (l * FF_HALVES + f) * FF_BLOCKS + i * 4
                        for s in range(SLOTS):
                            ahead(g, s)
                            product(g, s)
                            dst = head_y[:, s % 2, :]
                            TS(dst, lin[s % 2][:, 0:TOK], 0.0, None, ALU.max).then_inc(acc_free[s % 2], 1)
                            dve.drain()
                            TT(dst, dst, dst, ALU.mult).then_inc(f_act, 1)
                            dve.wait_ge(f_hi_s, n + (s + 1))
                            TT(at(f_lo, i * 4 + s), dst, at(f_hi, i * 4 + s), ALU.subtract).then_inc(f_lo_s, 1)
                            dve.drain()
                    with dve.Fori(0, 4) as i:
                        g = G + G_FF + 4 + f * G_HALF + i
                        for s in range(SLOTS):
                            ahead(g, s)
                            if s % 2 == 1:
                                product(g, s)
                                b = s // 2
                                dst = at(wide, i * 2 + b)
                                TT(dst, lin[b][:, 0:TOK], dst, ALU.add).then_inc(acc_free[b], 1)
                    dve.drain()
                dve.drain().then_inc(y_sum, 1)
                add_normed(l * 4 + 3, C_GAIN + 24)

            dve.wait_ge(x1_hi, 1)
            TT(x_lo[:, :, 0:SEQ], h[:, :, META:TOK], x_hi[:, :, 0:SEQ], ALU.subtract).then_inc(x1_lo, 1)
            dve.drain()
            with dve.Fori(0, 6) as i:
                for s in range(SLOTS):
                    ahead(i + G_QKV, s)

            def finish(u):
                dve.wait_ge(s_rs, u + 1)
                STT(head_y[:, 0, 0:SEQ], ps[4][:, 0:SEQ], col(par2, u + C_GHEAD), head_rstd[:, 0, 0:SEQ],
                    ALU.mult, ALU.mult).then_inc(s_y, 1)
                dve.wait_ge(s_hi, u + 1)
                TT(at(x_lo, u, SEQ), head_y[:, 0, 0:SEQ], at(x_hi, u, SEQ), ALU.subtract).then_inc(s_lo, 1)
                dve.drain()

            with dve.Fori(0, PAIRS) as u:
                for j in range(2):
                    dve.wait_ge(s_log, u * 2 + j + 1)
                    sp_ = prob_flat[:, j, :]
                    L = log_rest[:, j, :]
                    STT(L, ps[j][:, 0:384], 0.0, sp_, ALU.max, ALU.add)
                    dve.drain()
                    TT(L, L, tri[:, 1, :], ALU.mult)
                    STT(sp_, ps[j][:, 0:384], 0.0, sp_, ALU.min, ALU.subtract)
                    dve.drain().then_inc(s_L, 1)
                for j in range(2):
                    dve.wait_ge(s_btw, u * 2 + j + 1)
                    TT(prob_flat[:, j, :], prob_flat[:, j, :], ps[j][:, 0:384], ALU.add).then_inc(s_arg, 1)
                for j in range(2):
                    dve.wait_ge(s_a, u * 2 + j + 1)
                    TT(prob_tf[:, j, :], prob_tf[:, j, :], tri[:, 0, :], ALU.mult).then_inc(s_am, 1)
                finish(u)
            with dve.Fori(0, PAIRS) as n:
                u = n + PAIRS
                for j in range(2):
                    dve.wait_ge(d_S, n * 2 + j + 1)
                    nc.vector.tensor_reduce(small[:, j, 0, 0:1], ps[j][:, 0:128], AX.X, ALU.max)
                    nc.vector.tensor_reduce(small[:, j, 0, 1:2], ps[j][:, 128:384], AX.X, ALU.max)
                    dve.drain()
                    TS(small[:, j, 1, 0:2], small[:, j, 0, 0:2], -1.0, None, ALU.mult).then_inc(d_max, 1)
                for j in range(2):
                    dve.wait_ge(d_exp, n * 2 + j + 1)
                    P = prob_flat[:, j, :]
                    nc.vector.reciprocal(small[:, j, 2, 0:2], small[:, j, 2, 0:2])
                    dve.drain()
                    TS(P[:, 0:128], P[:, 0:128], small[:, j, 2, 0:1], None, ALU.mult)
                    TS(P[:, 128:384], P[:, 128:384], small[:, j, 2, 1:2], None, ALU.mult)
                    dve.drain().then_inc(d_prob, 1)
                finish(u)
            with dve.Fori(0, 2) as i:
                for s in range(SLOTS):
                    ahead(i + G_OUT, s)
                    product(i + G_OUT, s)
                    src = h[:, bass.ds(i * 4 + s, 1), META:TOK].rearrange("p a n -> p (a n)")
                    STT(at(wide, i * 4 + s, SEQ), src, ALPHA, lin[s % 2][:, 0:SEQ], ALU.mult, ALU.add)\
                        .then_inc(acc_free[s % 2], 1)
            dve.drain()

            def layer_norm(k, dst):
                nc.vector.tensor_reduce(row_sum[:, 0:SEQ], wide[:, :, 0:SEQ].rearrange("p k n -> p n k"),
                                        AX.X, ALU.add).then_inc(ln_s1, 1)
                dve.wait_ge(ln_mean, k + 1)
                for t in range(KT):
                    TT(wide[:, t, 0:SEQ], wide[:, t, 0:SEQ], ps[0][:, 0:SEQ], ALU.subtract)
                dve.drain().then_inc(ln_c, 1)
                dve.wait_ge(ln_sq, k + 1)
                nc.vector.tensor_reduce(row_sum[:, 0:SEQ], gates[:, 0:KT, 0:SEQ].rearrange("p k n -> p n k"),
                                        AX.X, ALU.add).then_inc(ln_s2, 1)
                dve.wait_ge(ln_rs, k + 1)
                for t in range(KT):
                    TT(wide[:, t, 0:SEQ], wide[:, t, 0:SEQ], rstd[:, 0:SEQ], ALU.mult)
                dve.drain()
                c = C_LN + 16 * k
                for t in range(KT):
                    TS(dst[:, t, 0:SEQ], wide[:, t, 0:SEQ], par2[:, c + t:c + t + 1],
                       par2[:, c + 8 + t:c + 9 + t], ALU.mult, ALU.add)
                dve.drain().then_inc(ln_out, 1)

            layer_norm(0, h)
            dve.wait_ge(x1_hi, 2)
            TT(x_lo[:, :, 0:SEQ], h[:, :, 0:SEQ], x_hi[:, :, 0:SEQ], ALU.subtract).then_inc(x1_lo, 1)
            dve.wait_ge(logit_s, 1)
            for t in range(2):
                TT(rt[:, t, 0, :], ps[2][:, t * 16:(t + 1) * 16], par2[:, C_BROUTER:C_BROUTER + 16], ALU.add)
            dve.drain()
            for t in range(2):
                nc.vector.tensor_reduce(rt[:, t, 1, 2:3], rt[:, t, 0, :], AX.X, ALU.max)
            dve.drain()
            for t in range(2):
                TS(rt[:, t, 1, 0:1], rt[:, t, 1, 2:3], -1.0, None, ALU.mult)
            dve.drain().then_inc(rt_max, 1)
            dve.wait_ge(rt_exp, 1)
            for t in range(2):
                nc.vector.reciprocal(rt[:, t, 1, 3:4], rt[:, t, 1, 1:2])
            dve.drain()
            for t in range(2):
                TS(rt[:, t, 3, :], rt[:, t, 2, :], rt[:, t, 1, 3:4], None, ALU.mult)
            dve.drain()

            def others_ahead(t, values, n_in, width, dst):
                a = values.rearrange("p (g e) -> p g e", e=n_in)
                g = width // n_in
                m = n_in * n_in * g
                shape4 = lambda x: x.rearrange("p (g a b) -> p g a b", a=n_in, b=n_in)
                other = a.unsqueeze(2).broadcast_to((128, g, n_in, n_in))
                own = a.unsqueeze(3).broadcast_to((128, g, n_in, n_in))
                TT(shape4(cmp[:, t, 0, 0:m]), other, own, ALU.is_gt)
                TT(shape4(cmp[:, t, 1, 0:m]), other, own, ALU.is_equal)
                dve.drain()
                TT(cmp[:, t, 1, 0:m], cmp[:, t, 1, 0:m], early[:, 0:m], ALU.mult)
                dve.drain()
                TT(cmp[:, t, 0, 0:m], cmp[:, t, 0, 0:m], cmp[:, t, 1, 0:m], ALU.add)
                dve.drain()
                nc.vector.tensor_reduce(dst, cmp[:, t, 0, 0:m].rearrange("p (a b) -> p a b", b=n_in), AX.X, ALU.add)
                dve.drain()

            for t in range(2):
                R = lambda i, n=16: rt[:, t, i, 0:n]
                others_ahead(t, R(3), 4, 16, R(4))
                TS(R(5), R(4), 1.5, None, ALU.is_lt)
                dve.drain()
                TT(R(6), R(5), R(3), ALU.mult)
                dve.drain()
                nc.vector.tensor_reduce(R(7, 4), R(6).rearrange("p (g e) -> p g e", e=4), AX.X, ALU.add)
                dve.drain()
                others_ahead(t, R(7, 4), 4, 4, R(8, 4))
                TS(R(9, 4), R(8, 4), 0.5, None, ALU.is_lt)
                nc.vector.reciprocal(rt[:, t, 9, 4:8], R(7, 4))
                dve.drain()
                TT(rt[:, t, 10, 0:4], R(9, 4), rt[:, t, 9, 4:8], ALU.mult)
                dve.drain()
                TT(R(11).rearrange("p (g e) -> p g e", e=4), R(6).rearrange("p (g e) -> p g e", e=4),
                   rt[:, t, 10, 0:4].unsqueeze(2).broadcast_to((128, 4, 4)), ALU.mult)
                dve.drain()
            dve.drain().then_inc(rt_gate, 1)
            dve.wait_ge(rt_t, 1)
            nc.vector.tensor_copy(gate_row[:, :], ps[3][0:EXPERTS, 0:SEQ]).then_inc(rt_row, 1)
            TS(wide[:, :, 0:SEQ], h[:, :, 0:SEQ], ALPHA, None, ALU.mult)
            dve.wait_ge(rt_all, EXPERTS)
            dve.drain()
            with dve.Fori(0, EXPERTS) as e:
                with dve.Fori(0, 4) as i:
                    g = e * 6 + i + G_EXP
                    for j in range(2):
                        n = e * 8 + i * 2 + (j + 1)
                        ahead(g, 2 * j)
                        ahead(g, 2 * j + 1)
                        dve.wait_ge(silu_s, n)
                        TT(head_sq[:, j, 0:SEQ], raw_v[:, j, 0:SEQ], at(gates, e, SEQ), ALU.mult)
                        dve.drain()
                        product(g, 2 * j + 1)
                        TT(head_y[:, j, 0:SEQ], head_sq[:, j, 0:SEQ], lin[1][:, 0:SEQ], ALU.mult)\
                            .then_inc(acc_free[1], 1)
                        dve.drain().then_inc(hid_s, 1)
                        dve.wait_ge(hid_hi, n)
                        TT(at(f_lo, i * 2 + j, SEQ), head_y[:, j, 0:SEQ], at(f_hi, i * 2 + j, SEQ), ALU.subtract)\
                            .then_inc(hid_lo, 1)
                with dve.Fori(0, 2) as i:
                    g = e * 6 + i + (G_EXP + 4)
                    for s in range(SLOTS):
                        ahead(g, s)
                        product(g, s)
                        dst = at(wide, i * 4 + s, SEQ)
                        TT(dst, lin[s % 2][:, 0:SEQ], dst, ALU.add).then_inc(acc_free[s % 2], 1)
                dve.drain()
            layer_norm(1, wide)


_INS = ["weights", "h_in", "layer_par", "second_par", "rope", "toeplitz", "att_mask", "squares", "stick",
        "bias_map", "bias_add", "rel_bias", "w_router", "tie_order"]


def feature_blocks(v):
    import numpy as np
    v = np.asarray(v)
    return np.moveaxis(v.reshape(*v.shape[:-1], -1, 128), -1, 0)


def lay_out_weights(x):
    import numpy as np
    weights = np.zeros((GROUPS * SLOTS, 128, KT * 128), np.float32)

    def tile_rows(w):
        return w.reshape(-1, 128, w.shape[-1]).transpose(1, 0, 2)

    def put(at, w, block, k0=0):
        weights[at] = w[:, k0:k0 + KT, block * 128:(block + 1) * 128].reshape(128, -1)

    for l in range(LAYERS):
        at = l * G_LAYER * SLOTS
        w_in = x["w_in"][l]
        cuts = np.cumsum([0, 512, 512, 1024, 1024, 512, 128, 128, 1024, 1024])
        q_r, k_r, v_r, g_r, q_a, k_a, v_a, gate_r, gate_a = [
            tile_rows(w_in[:, a:b]) for a, b in zip(cuts[:-1], cuts[1:])]
        q_a = q_a.reshape(128, KT, 2, PAIRS, 64).transpose(0, 1, 3, 2, 4).reshape(128, KT, 512)
        order = [(g_r, b) for b in range(KT)] + [(gate_r, b) for b in range(KT)] + [(gate_a, b) for b in range(KT)]
        for i in range(PAIRS):
            order += [(q_r, i), (k_r, i), (v_r, 2 * i), (v_r, 2 * i + 1)]
        order += [(k_a, 0), (v_a, 0)] + [(q_a, i) for i in range(PAIRS)]
        for n, (w, b) in enumerate(order):
            put(at + n, w, b)
        ret_o, mix_o = tile_rows(x["w_ret_o"][l]), tile_rows(x["w_mix_o"][l])
        att_o = x["w_att_o"][l].reshape(2, PAIRS, 64, D).transpose(1, 0, 2, 3).reshape(512, D)
        att_o = tile_rows(att_o)
        for b in range(KT):
            put(at + G_RETO * SLOTS + b, ret_o, b)
            put(at + G_MIX * SLOTS + b, mix_o, b)
        for n in range(KT // 2):
            two = att_o[:, :, n * 256:(n + 1) * 256].reshape(128, 4, 2, 128).transpose(0, 2, 1, 3)
            weights[at + G_ATTO * SLOTS + n] = two.reshape(128, -1)
        ff1, ff2 = tile_rows(x["w_ff1"][l]), tile_rows(x["w_ff2"][l])
        for f in range(FF_HALVES):
            base = at + (G_FF + f * G_HALF) * SLOTS
            for n in range(FF_BLOCKS):
                put(base + n, ff1, f * FF_BLOCKS + n)
                put(base + FF_BLOCKS + n, ff2, n // 2, f * FF_BLOCKS + KT * (n % 2))
    w_in = x["w_in_2"][0]
    sb_q, sb_k, sb_v, dl_q, dl_k, dl_v = [tile_rows(w_in[:, i * 512:(i + 1) * 512]) for i in range(6)]
    n = G_QKV * SLOTS
    for three in ((sb_q, sb_k, sb_v), (dl_q, dl_k, dl_v)):
        for i in range(PAIRS):
            for w in three:
                put(n, w, i)
                n += 1
    w_out = tile_rows(x["w_out_2"][0])
    for b in range(KT):
        put(G_OUT * SLOTS + b, w_out, b)
    n = G_EXP * SLOTS
    for e in range(EXPERTS):
        gate, up, down = [tile_rows(x[name][0, e]) for name in ("w_gate_2", "w_up_2", "w_down_2")]
        for b in range(KT):
            put(n + 2 * b, gate, b)
            put(n + 2 * b + 1, up, b)
            put(n + 2 * KT + b, down, b)
        n += 3 * KT
    return weights


def bucket(dist):
    import math

    import numpy as np
    d = np.maximum(dist, 0)
    ratio = np.log(np.maximum(d, 1).astype(np.float32) / np.float32(16)) / np.float32(math.log(2048 / 16))
    large = np.minimum(16 + (ratio * np.float32(16)).astype(np.int32), 31)
    return np.where(d < 16, d, large)


def tables():
    import numpy as np
    f = np.float32
    pos = np.arange(TOK, dtype=f)
    rope = np.zeros((128, 8, TOK), f)
    turn = {}
    for at, (theta, dim) in ((0, (10000.0, 64)), (4, (500000.0, 16))):
        half = dim // 2
        freqs = np.power(f(theta), -np.arange(0, dim, 2, dtype=f) / f(dim)).astype(f)
        ang = (pos[:, None] * freqs[None, :]).astype(f)
        cos, sin = np.ones((64, TOK), f), np.zeros((64, TOK), f)
        cos[:half] = cos[half:dim] = np.cos(ang).T
        sin[:half] = sin[half:dim] = np.sin(ang).T
        for n, t in enumerate((cos / 8, sin / 8, cos, sin)):
            rope[:, at + n] = np.tile(t, (2, 1))
        m = np.zeros((64, 64), f)
        for i in range(half):
            m[i + half, i], m[i, i + half] = -1, 1
        turn[at] = np.kron(np.eye(2, dtype=f), m)
    eye = np.eye(128, dtype=f)
    row, column = np.arange(128)[:, None], np.arange(128)[None, :]
    squares = np.stack([
        turn[0], turn[4], eye - f(1 / 128), eye, np.full((128, 128), 1 / D, f), np.full((128, 128), 1 / 128, f),
        np.kron(np.eye(2, dtype=f), np.full((64, 64), 1 / 64, f)), (row > column).astype(f),
        np.ones((128, 128), f), eye[::-1]], 1)
    rel = np.arange(SPAN)[None, :] - 256 - np.arange(128)[:, None]
    toeplitz = np.stack([np.maximum(rel, 0), np.maximum(-rel, 0)], 1).astype(f)
    i = np.arange(3)[None, :, None] * 128 + np.arange(128)[:, None, None]
    j = np.arange(TOK)[None, None, :]
    att_mask = np.where((j < META) | (np.abs(i - j) <= 128), 0, NEG).astype(f)
    causal = np.concatenate([np.arange(128)[:, None] < np.arange(SEQ)[None, :], row < column], 1).astype(f)
    stick = np.stack([causal, -causal], 1)
    dist = 255 - np.arange(512)
    bias_map = (bucket(dist)[None, :] == np.arange(32)[:, None]).astype(f)
    times = (dist <= 128) * 1 + (dist % 4 == 0) * 1 + (dist % 16 == 0) * 1
    times = np.where(dist >= 0, times, 0)
    add = np.where(times > 0, np.log(np.maximum(times, 1)), NEG).astype(f)
    bias_add = np.tile(add, (8, 1))
    own, other = np.arange(4)[:, None], np.arange(4)[None, :]
    tie_order = np.tile((other < own).astype(f).ravel(), (128, 4))
    return dict(rope=rope, toeplitz=toeplitz, att_mask=att_mask, squares=np.ascontiguousarray(squares),
                stick=stick, bias_map=bias_map, bias_add=bias_add, tie_order=tie_order)


def kernel(**inputs):
    import numpy as np
    import concourse.bacc as bacc
    from concourse.bass_utils import run_bass_kernel_spmd as run

    x = {k: np.asarray(v) for k, v in inputs.items()}
    arrays = tables()
    arrays["weights"] = lay_out_weights(x)
    tokens = np.concatenate([x["meta_tokens"], x["x"][0]], 0)
    arrays["h_in"] = tokens.T.reshape(KT, 128, TOK).transpose(1, 0, 2)
    gains = np.stack([feature_blocks(x[n]) for n in (
        "norm_mix_pre", "norm_mix_post", "norm_ff_pre", "norm_ff_post")], 2)
    every = lambda v: np.broadcast_to(v[None], (128, *v.shape))
    sink = x["attn_sink"].reshape(LAYERS, 2, PAIRS).transpose(0, 2, 1).reshape(LAYERS, 8)
    arrays["layer_par"] = np.concatenate([
        gains.reshape(128, LAYERS, 32), every(x["ret_decay"].reshape(LAYERS, 16)), every(sink)], 2)
    arrays["second_par"] = np.concatenate(
        [feature_blocks(x[n][0]) for n in ("ln1_g_2", "ln1_b_2", "ln2_g_2", "ln2_b_2", "g_sb_2", "g_dil_2")]
        + [every(x["b_router_2"])], 1)
    arrays["rel_bias"] = x["rel_bias_2"]
    arrays["w_router"] = x["w_router_2"].reshape(KT, 128, EXPERTS).transpose(1, 0, 2)

    nc = bacc.Bacc("TRN2", target_bir_lowering=False, num_devices=1)
    arrays = {f"in_{n}": np.ascontiguousarray(arrays[n]) for n in _INS}
    args = [nc.dram_tensor(n, a.shape, mybir.dt.from_np(a.dtype), kind="ExternalInput").ap()
            for n, a in arrays.items()]
    args.append(nc.dram_tensor("y_out", (128, KT, SEQ), F32, kind="ExternalOutput").ap())
    build_program(nc, *args)
    r = run(nc, [arrays], core_ids=[0])
    y = r.results[0]["y_out"]
    return y.transpose(2, 1, 0).reshape(1, SEQ, D)
```

```python
from contextlib import ExitStack

import concourse.bass as bass
from concourse import mybir

F32 = mybir.dt.float32
F32R = mybir.dt.float32r
ALU = mybir.AluOpType
ACT = mybir.ActivationFunctionType
AX = mybir.AxisListType

D = 1024
SEQ = 256
META = 16
TOK = SEQ + META
LAYERS = 2
KT = D // 128
PAIRS = 4
D_FF = 4 * D
FF_HALVES = 2
FF_BLOCKS = D_FF // 128 // FF_HALVES
EXPERTS = 16
TILES = [(0, 128), (128, 128), (256, TOK - 256)]
SPAN = 2 * TOK
ALPHA = 2.0 ** 0.25
RMS_EPS, HEAD_EPS, LN_EPS = 1e-6, 1e-6, 1e-5
NEG = -1e30

SLOTS = 4
G_GATE, G_SIG, G_RET, G_ATT = 0, 2, 6, 10
G_RETO, G_ATTO, G_MIX, G_FF = 12, 14, 15, 17
G_HALF = 8
G_LAYER = 33
G_QKV = LAYERS * G_LAYER
G_OUT = G_QKV + 6
G_EXP = G_OUT + 2
G_END = G_EXP + 6 * EXPERTS
GROUPS = G_END + 1

A_GATE, A_SIG, A_RET, A_ATT, A_RETO, A_ATTO, A_MIX, A_FF = 0, 4, 12, 20, 23, 27, 31, 35
A_HALF = 12
A_LAYER = 59
A_QKV = LAYERS * A_LAYER
A_OUT = A_QKV + 12
A_EXP = A_OUT + 4

C_GAIN, C_DECAY, C_SINK, C_LAYER = 0, 32, 48, 56
C_LN, C_GHEAD, C_BROUTER, C_SECOND = 0, 32, 40, 56
LN_SETS = 6


def load_exp_ln(nc, act):
    act.add_instruction(mybir.InstLoadActFuncSet(
        name=nc.get_next_instruction_name(), engine=mybir.EngineType.Activation,
        act_func_set_id=LN_SETS, ins=[], outs=[]))


def build_program(nc, weights, h_in, layer_par, second_par, rope, toeplitz, att_mask, squares,
                  stick, bias_map, bias_add, rel_bias, w_router, tie_order, lanes, ln_rows, out):
    with ExitStack() as ctx:
        def sb(name, shape, dt=F32):
            return ctx.enter_context(nc.sbuf_tensor(name, shape, dt))

        def sem(name):
            return ctx.enter_context(nc.semaphore(name))

        raw = sb("raw", [128, SLOTS, KT, 128])
        w_hi = sb("w_hi", [128, SLOTS, KT, 128], F32R)
        w_lo = sb("w_lo", [128, SLOTS, KT, 128], F32R)
        h = sb("h", [128, KT, TOK])
        wide = sb("wide", [128, KT, TOK])
        x_hi = sb("x_hi", [128, KT, TOK], F32R)
        x_lo = sb("x_lo", [128, KT, TOK], F32R)
        f_hi = sb("f_hi", [128, FF_BLOCKS, TOK], F32R)
        f_lo = sb("f_lo", [128, FF_BLOCKS, TOK], F32R)
        gates = sb("gates", [128, 3 * KT, TOK])
        q_att = sb("q_att", [128, PAIRS, TOK])
        raw_qk = sb("raw_qk", [128, 2, TOK])
        raw_v = sb("raw_v", [128, 2, TOK])
        q_rot = sb("q_rot", [128, TOK])
        k_rot = sb("k_rot", [128, TOK])
        v_tok = sb("v_tok", [128, 2, 3, 128])
        probs = sb("probs", [128, 4 * 3 * TOK])
        prob = probs[:, 0:6 * TOK].rearrange("p (j t n) -> p j t n", j=2, t=3)
        prob_t = probs[:, 6 * TOK:12 * TOK].rearrange("p (j t n) -> p j t n", j=2, t=3)
        decay = probs[:, 0:2 * SPAN].rearrange("p (j n) -> p j n", j=2)
        head_bias = probs[:, 0:8 * 384].rearrange("p (h n) -> p h n", h=8)
        head_sq = sb("head_sq", [128, 2, TOK])
        head_rstd = sb("head_rstd", [128, 2, TOK])
        head_y = sb("head_y", [128, 2, TOK])
        row_sum = sb("row_sum", [128, TOK])
        rstd = sb("rstd", [128, TOK])
        small = sb("small", [128, 2, 4, 4])
        sink_col = sb("sink_col", [128, 2])
        decay_rate = sb("decay_rate", [128, 16])
        par = sb("par", [128, LAYERS, C_LAYER])
        lay = sb("lay", [128, C_LAYER])
        par2 = sb("par2", [128, C_SECOND])
        rope_t = sb("rope_t", [128, 8, TOK])
        dist = sb("dist", [128, 2, SPAN])
        mask = sb("mask", [128, 3, TOK])
        sq = sb("sq", [128, 10, 128])
        tri = sb("tri", [128, 2, 384])
        eps = sb("eps", [128, 2])
        def two_tiles(t):
            axes = "p a n -> p (a n)"
            return t[:, :, :].rearrange(axes)[:, 0:2 * 384].rearrange("p (j n) -> p j n", j=2)
        prob_flat = two_tiles(q_att)
        prob_tf = two_tiles(dist)
        log_rest = two_tiles(mask)
        start = gates[:, :, :].rearrange("p a n -> p (a n)")
        bmap, badd, brow = start[0:32, 0:512], start[0:8, 512:1024], start[0:8, 1024:1536]
        relb = sb("relb", [32, 8])
        wr = sb("wr", [128, KT, EXPERTS])
        rt = sb("rt", [128, 2, 14, 16])
        slot_of = sb("slot_of", [128, 2, EXPERTS + 1])
        slot_gate = sb("slot_gate", [128, 1])
        flag_f = sb("flag_f", [128, 1])
        flag = sb("flag", [128, 1], mybir.dt.int32)
        stats = sb("stats", [128, 2, 2, 6])
        moments = sb("moments", [128, 2, 4])
        early = sb("early", [128, 64])
        bias_dram = nc.dram_tensor("bias_dram", (8, 512), F32).ap()

        PERM_R, PERM_A, CENTER, IDENT, ONES_D, ONES_HEAD, ONES_HALF, AFTER, ALL_ONES, FLIP = range(10)
        banks = ctx.enter_context(nc.psum_tensor("banks", [128, 8, 512], F32))
        lin = [banks[:, i, :] for i in range(2)]
        ps = [banks[:, 2 + i, :] for i in range(6)]

        def flat(t):
            return t[:, :, :].rearrange("p a n -> p (a n)")
        ROW = D
        tok_hi, tok_lo = flat(f_hi)[:, 0:2 * ROW], flat(f_lo)[:, 0:2 * ROW]
        out_hi, out_lo = flat(f_hi)[:, 2 * ROW:3 * ROW], flat(f_lo)[:, 2 * ROW:3 * ROW]
        sel = flat(f_hi)[:, 3 * ROW:3 * ROW + SEQ].rearrange("p (t n) -> p t n", t=2)
        sel_t = flat(f_lo)[:, 3 * ROW:3 * ROW + SEQ]
        cmp = flat(head_sq)[:, 0:256].rearrange("p (t c m) -> p t c m", t=2, c=2)
        slot_none = flat(head_rstd)[0:1, 0:512]
        lane = flat(head_y)[:, 0:2 + SEQ]
        gate_row = q_rot[0:EXPERTS, 0:SEQ]
        slot_x_hi = flat(x_hi)[:, 0:ROW].rearrange("p (k n) -> p k n", k=KT)
        slot_x_lo = flat(x_lo)[:, 0:ROW].rearrange("p (k n) -> p k n", k=KT)
        slot_h_hi = flat(x_hi)[:, ROW:2 * ROW].rearrange("p (k n) -> p k n", k=KT)
        slot_h_lo = flat(x_lo)[:, ROW:2 * ROW].rearrange("p (k n) -> p k n", k=KT)
        silu_row, hid_row = probs[:, 0:ROW], probs[:, ROW:2 * ROW]
        res_row = flat(wide)[:, 0:2 * ROW]
        gain_rows = flat(gates)[:, 2 * KT * TOK:2 * KT * TOK + 2 * ROW]
        gate_bank = banks[:, 0:2, :].rearrange("p a n -> p (a n)")
        up_bank = banks[:, 2:4, :].rearrange("p a n -> p (a n)")
        sum_bank = banks[:, 4:8, :].rearrange("p a n -> p (a n)")

        landed = [sem(f"landed{i}") for i in range(SLOTS)]
        hi_ready = sem("hi_ready")
        split_ready = sem("split_ready")
        chunk_done = sem("chunk_done")
        acc_free = [sem("acc_free0"), sem("acc_free1")]
        consts = sem("consts")
        h_in_s = sem("h_in_s")
        bias_s = sem("bias_s")
        brow_s = sem("brow_s")
        bias_stored = sem("bias_stored")
        bmm_s = sem("bmm_s")
        lay_ready = sem("lay_ready")
        set_up = sem("set_up")
        rate_ready = sem("rate_ready")
        norm_sq, norm_sum, norm_bc, norm_rstd = sem("norm_sq"), sem("norm_sum"), sem("norm_bc"), sem("norm_rstd")
        h_ready = sem("h_ready")
        u_ready, u_hi, u_lo = sem("u_ready"), sem("u_hi"), sem("u_lo")
        gates_ready = sem("gates_ready")
        ret_raw, perm_done, ret_rot = sem("ret_raw"), sem("perm_done"), sem("ret_rot")
        v_turned, v_ready = sem("v_turned"), sem("v_ready")
        decay_arg, decay_ready = sem("decay_arg"), sem("decay_ready")
        scores, decayed = sem("scores"), sem("decayed")
        head_out, squared, var_done, head_rs = sem("head_out"), sem("squared"), sem("var_done"), sem("head_rs")
        y_ready, y_hi, y_lo = sem("y_ready"), sem("y_hi"), sem("y_lo")
        a_raw, a_perm, a_rot, a_vt, a_v = sem("a_raw"), sem("a_perm"), sem("a_rot"), sem("a_vt"), sem("a_v")
        a_stage, a_qperm, a_qrot = sem("a_stage"), sem("a_qperm"), sem("a_qrot")
        a_scores, a_max, a_exp, a_prob, a_pt, a_ptc, a_o, a_hi, a_lo = [
            sem("a_" + n) for n in ("scores", "max", "exp", "prob", "pt", "ptc", "o", "hi", "lo")]
        m_ready, m_hi, m_lo = sem("m_ready"), sem("m_hi"), sem("m_lo")
        mix_ready = sem("mix_ready")
        f_act, f_hi_s, f_lo_s = sem("f_act"), sem("f_hi_s"), sem("f_lo_s")
        y_sum = sem("y_sum")
        s_stage, s_vt, s_v, s_z = sem("s_stage"), sem("s_vt"), sem("s_v"), sem("s_z")
        s_abs, s_log, s_L, s_btw, s_arg, s_a, s_am = [sem("s_" + n) for n in ("abs", "log", "L", "btw", "arg", "a", "am")]
        s_o, s_sq, s_var, s_rs, s_y, s_hi, s_lo = [sem("s_" + n) for n in ("o", "sq", "var", "rs", "y", "hi", "lo")]
        d_S, d_max, d_exp, d_prob, d_pt, d_ptc = [sem("d_" + n) for n in ("S", "max", "exp", "prob", "pt", "ptc")]
        qkv_ready = sem("qkv_ready")
        r_ready = sem("r_ready")
        ln_s1, ln_mean, ln_c, ln_sq, ln_s2, ln_var, ln_rs, ln_out = [
            sem("ln_" + n) for n in ("s1", "mean", "c", "sq", "s2", "var", "rs", "out")]
        x1_hi, x1_lo = sem("x1_hi"), sem("x1_lo")
        logit_s, rt_max, rt_exp, rt_gate, rt_t, rt_row, rt_bc, rt_all = [
            sem("rt_" + n) for n in ("logit", "max", "exp", "gate", "t", "row", "bc", "all")]
        slots_mm, slots_ready, flag_ready = sem("slots_mm"), sem("slots_ready"), sem("flag_ready")
        tok_turned, tok_split, sum_open = sem("tok_turned"), sem("tok_split"), sem("sum_open")
        tok_hi_s = sem("tok_hi_s")
        sel_ready = sem("sel_ready")
        gathered = sem("gathered")
        x_hi_got, x_lo_got = sem("x_hi_got"), sem("x_lo_got")
        silu_done, hid_done, hid_turned = sem("silu_done"), sem("hid_done"), sem("hid_turned")
        hid_hi, hid_lo = sem("hid_hi"), sem("hid_lo")
        gated_hi = sem("gated_hi")
        gated_lo = sem("gated_lo")
        scattered = sem("scattered")
        cleared = sem("cleared")
        sum_done = sem("sum_done")
        rows_s = sem("rows_s")
        lane_s = sem("lane_s")
        var_ready, fin_rstd = sem("var_ready"), sem("fin_rstd")
        y_half = sem("y_half")
        out_s = sem("out_s")

        N_CONST = 12
        block = ctx.enter_context(nc.Block())

        def at(t, i, n=TOK, p=slice(0, 128)):
            if type(i) is int:
                return t[p, i, 0:n]
            return t[p, bass.ds(i, 1), 0:n].rearrange("p a n -> p (a n)")

        def col(t, i):
            return t[:, bass.ds(i, 1)] if type(i) is not int else t[:, i:i + 1]

        @block.sync
        def _(sp):
            sp.dma_start(h[:, :, :], h_in).then_inc(h_in_s, 16)
            for dst, src in ((par, layer_par), (par2, second_par), (rope_t, rope), (dist, toeplitz),
                             (mask, att_mask), (sq, squares), (tri, stick), (bmap, bias_map),
                             (badd, bias_add), (relb, rel_bias), (wr, w_router), (early, tie_order)):
                sp.dma_start(dst[tuple(slice(None) for _ in dst.shape)], src).then_inc(consts, 16)
            with sp.Fori(0, GROUPS) as g:
                for s in range(SLOTS):
                    sp.wait_ge(split_ready, g * SLOTS + (s + 1))
                    sp.dma_start(raw[:, s, :, :], weights[bass.ds(g * SLOTS + s, 1)].rearrange(
                        "a p (k m) -> p (a k) m", m=128)).then_inc(landed[s], 16)
            sp.wait_ge(flag_ready, 1)
            crowded = sp.value_load(flag[0:1, 0:1], min_val=0, max_val=1)
            with sp.If(crowded > 0):
                with sp.Fori(0, G_END - G_EXP) as g:
                    for s in range(SLOTS):
                        sp.wait_ge(split_ready, g * SLOTS + (GROUPS * SLOTS + s + 1))
                        sp.dma_start(raw[:, s, :, :], weights[bass.ds(g * SLOTS + ((G_EXP + 1) * SLOTS + s), 1)]
                                     .rearrange("a p (k m) -> p (a k) m", m=128)).then_inc(landed[s], 16)
            for t in range(2):
                sp.wait_ge(y_half, t + 1)
                sp.dma_start(out[t], res_row[:, t * ROW:(t + 1) * ROW]).then_inc(out_s, 16)
            sp.wait_ge(out_s, 32)

        @block.gpsimd
        def _(pool):
            pool.wait_ge(brow_s, 1)
            pool.dma_start(bias_dram, brow[:, :]).then_inc(bias_stored, 16)
            pool.wait_ge(bias_stored, 16)
            pool.wait_ge(mix_ready, LAYERS)
            for first, start, n in ((0, 128, 128), (128, 0, 256)):
                src = bass.AP(bias_dram.tensor, start, [[1, 128], [512, 8], [1, n]])
                pool.dma_start(head_bias[:, :, first:first + n], src).then_inc(bias_s, 16)
            pool.wait_ge(ln_s1, 1)
            for r in range(2):
                pool.dma_start(gain_rows[:, r * ROW:(r + 1) * ROW],
                               bass.AP(ln_rows.tensor, r * ROW, [[0, 128], [1, ROW]])).then_inc(rows_s, 16)
            pool.dma_start(lane, lanes).then_inc(lane_s, 16)

        @block.tensor
        def _(pe):
            def chunk_mm(g, s, bank, rhs, kts, n, first=True, last=True, lhs_k=0, done=True):
                hi, lo = rhs
                steps = len(kts)
                for i, k in enumerate(kts):
                    pe.matmul(lin[bank][:, 0:n], w_lo[:, s, lhs_k + i, :], hi[:, k, 0:n],
                              start=first and i == 0, stop=False)
                    pe.matmul(lin[bank][:, 0:n], w_hi[:, s, lhs_k + i, :], lo[:, k, 0:n],
                              start=False, stop=False)
                    mm = pe.matmul(lin[bank][:, 0:n], w_hi[:, s, lhs_k + i, :], hi[:, k, 0:n],
                                   start=False, stop=last and i == steps - 1)
                if done:
                    mm.then_inc(chunk_done, 1)
                return mm

            def chunk(g, s, bank, a, rhs, kts, n, first=True, last=True):
                pe.wait_ge(split_ready, g * SLOTS + (s + 1 + SLOTS))
                if first:
                    pe.wait_ge(acc_free[bank], a + 1)
                chunk_mm(g, s, bank, rhs, kts, n, first, last)

            def group(g, a, rhs, n):
                for s in range(SLOTS):
                    chunk(g, s, s % 2, a + s // 2, rhs, range(KT), n)

            def norm(w):
                pe.wait_ge(norm_sum, w + 1)
                pe.matmul(ps[0][:, 0:TOK], sq[:, ONES_D, :], row_sum[:, 0:TOK], start=True, stop=True)\
                    .then_inc(norm_bc, 1)

            X = (x_hi, x_lo)
            FF = (f_hi, f_lo)

            pe.sem_inc(chunk_done, SLOTS)
            pe.wait_ge(consts, 16 * N_CONST)
            pe.matmul(ps[5][0:8, :], relb[:, :], bmap[:, :], start=True, stop=True).then_inc(bmm_s, 1)

            with pe.Fori(0, LAYERS) as l:
                G = l * G_LAYER
                A = l * A_LAYER
                norm(l * 4)
                with pe.Fori(0, 2) as i:
                    pe.wait_ge(u_lo, l * 2 + 1)
                    group(G + G_GATE + i, A + A_GATE + i * 2, X, TOK)
                with pe.Fori(0, 4) as i:
                    group(G + G_SIG + i, A + A_SIG + i * 2, X, TOK)
                with pe.Fori(0, PAIRS) as i:
                    u = l * PAIRS + i
                    group(G + G_RET + i, A + A_RET + i * 2, X, TOK)
                    for j in range(2):
                        pe.wait_ge(ret_raw, u * 4 + j + 1)
                        pe.matmul(ps[j][:, 0:TOK], sq[:, PERM_R, :], raw_qk[:, j, :],
                                  start=True, stop=True).then_inc(perm_done, 1)
                    for j in range(2):
                        pe.wait_ge(ret_raw, u * 4 + j + 3)
                        for t, (t0, tn) in enumerate(TILES):
                            mm = pe.matmul(ps[2 + j][0:tn, t * 128:(t + 1) * 128], raw_v[:, j, t0:t0 + tn],
                                           sq[:, CENTER, :], start=True, stop=True)
                        mm.then_inc(v_turned, 1)
                    pe.wait_ge(ret_rot, u * 2 + 2)
                    bank = [[0, 1, 4], [5, 2, 3]]
                    for j in range(2):
                        p = slice(64 * j, 64 * j + 64)
                        if j == 1:
                            pe.wait_ge(v_ready, u * 2 + 2)
                        for t, (t0, tn) in enumerate(TILES):
                            mm = pe.matmul(ps[bank[j][t]][0:tn, 0:TOK], k_rot[p, t0:t0 + tn], q_rot[p, :],
                                           start=True, stop=True)
                        mm.then_inc(scores, 1)
                    for j in range(2):
                        pe.wait_ge(decayed, u * 2 + j + 1)
                        for t, (t0, tn) in enumerate(TILES):
                            mm = pe.matmul(ps[bank[j][0]][:, 0:TOK], v_tok[0:tn, j, t, :], prob_t[0:tn, j, t, :],
                                           start=t == 0, stop=t == 2)
                        mm.then_inc(head_out, 1)
                    for j in range(2):
                        pe.wait_ge(squared, u * 2 + j + 1)
                        pe.matmul(ps[bank[j][1]][:, 0:TOK], sq[:, ONES_HEAD, :], head_sq[:, j, :],
                                  start=True, stop=True).then_inc(var_done, 1)
                for s in range(SLOTS):
                    chunk(G + G_ATT, s, s % 2, A + A_ATT + s // 2, X, range(KT), TOK)
                for s in range(2):
                    chunk(G + G_ATT + 1, s, s % 2, A + A_ATT + 2, X, range(KT), TOK)
                for s in range(2, SLOTS):
                    pe.drain()
                    pe.wait_ge(split_ready, (G + G_ATT + 1) * SLOTS + (s + 1 + SLOTS))
                    pe.sem_inc(chunk_done, 1)
                pe.wait_ge(a_raw, l * 2 + 1)
                pe.matmul(ps[0][:, 0:TOK], sq[:, PERM_A, :], raw_qk[:, 1, :], start=True, stop=True)\
                    .then_inc(a_perm, 1)
                pe.wait_ge(a_raw, l * 2 + 2)
                for t, (t0, tn) in enumerate(TILES):
                    mm = pe.matmul(ps[2][0:tn, t * 128:(t + 1) * 128], raw_v[:, 0, t0:t0 + tn],
                                   sq[:, IDENT, :], start=True, stop=True)
                mm.then_inc(a_vt, 1)
                with pe.Fori(0, PAIRS) as i:
                    u = l * PAIRS + i
                    pe.wait_ge(a_rot, l + 1)
                    pe.wait_ge(a_v, l + 1)
                    pe.wait_ge(a_stage, u + 1)
                    pe.matmul(ps[0][:, 0:TOK], sq[:, PERM_A, :], raw_qk[:, 0, :], start=True, stop=True)\
                        .then_inc(a_qperm, 1)
                    pe.wait_ge(a_qrot, u + 1)
                    for j in range(2):
                        p = slice(64 * j, 64 * j + 64)
                        for t, (t0, tn) in enumerate(TILES):
                            mm = pe.matmul(ps[3 * j + t][0:tn, 0:TOK], q_rot[p, t0:t0 + tn], k_rot[p, :],
                                           start=True, stop=True)
                        mm.then_inc(a_scores, 1)
                    for j in range(2):
                        pe.wait_ge(a_prob, u * 2 + j + 1)
                        for k, (k0, kn) in enumerate(TILES):
                            for t, (t0, tn) in enumerate(TILES):
                                mm = pe.transpose(ps[3 * j + k][0:kn, t0:t0 + tn], prob[0:tn, j, t, k0:k0 + kn],
                                                  sq[0:tn, IDENT, 0:tn])
                        mm.then_inc(a_pt, 1)
                    for j in range(2):
                        p = slice(64 * j, 64 * j + 64)
                        pe.wait_ge(a_ptc, u * 2 + j + 1)
                        for k, (k0, kn) in enumerate(TILES):
                            mm = pe.matmul(ps[3 * j][p, 0:TOK], v_tok[0:kn, 0, k, p], prob_t[0:kn, j, k, :],
                                           start=k == 0, stop=k == 2)
                        mm.then_inc(a_o, 1)
                with pe.Fori(0, 2) as i:
                    pe.wait_ge(y_lo, (l + 1) * 2 * PAIRS)
                    group(G + G_RETO + i, A + A_RETO + i * 2, FF, TOK)
                pe.wait_ge(a_lo, (l + 1) * 2 * PAIRS)
                for s in range(SLOTS):
                    pe.wait_ge(split_ready, (G + G_ATTO) * SLOTS + (s + 1 + SLOTS))
                    for b in range(2):
                        pe.wait_ge(acc_free[b], A + A_ATTO + s + 1)
                        chunk_mm(0, s, b, FF, range(8, 12), TOK, lhs_k=4 * b, done=b == 1)
                with pe.Fori(0, 2) as i:
                    pe.wait_ge(m_lo, l + 1)
                    group(G + G_MIX + i, A + A_MIX + i * 2, X, TOK)
                norm(l * 4 + 1)
                norm(l * 4 + 2)
                with pe.Fori(0, FF_HALVES) as f:
                    with pe.Fori(0, 4) as i:
                        pe.wait_ge(u_lo, l * 2 + 2)
                        group(G + G_FF + f * G_HALF + i, A + A_FF + f * A_HALF + i * 2, X, TOK)
                    with pe.Fori(0, 4) as i:
                        pe.wait_ge(f_lo_s, (l * FF_HALVES + f + 1) * FF_BLOCKS)
                        for s in range(SLOTS):
                            chunk(G + G_FF + 4 + f * G_HALF + i, s, s // 2, A + A_FF + 8 + f * A_HALF + i, FF,
                                  range(KT * (s % 2), KT * (s % 2) + KT), TOK, first=s % 2 == 0, last=s % 2 == 1)
                norm(l * 4 + 3)

            pe.wait_ge(x1_lo, 1)
            with pe.Fori(0, 6) as i:
                group(i + G_QKV, i * 2 + A_QKV, X, SEQ)

            def stage_values(u):
                pe.wait_ge(s_stage, u + 1)
                for t in range(2):
                    mm = pe.matmul(ps[2][:, t * 128:(t + 1) * 128], raw_v[:, 0, t * 128:(t + 1) * 128],
                                   sq[:, IDENT, :], start=True, stop=True)
                mm.then_inc(s_vt, 1)

            def head_output(u, ready):
                pe.wait_ge(s_v, u + 1)
                for j in range(2):
                    p = slice(64 * j, 64 * j + 64)
                    pe.wait_ge(ready, ready_at(u, j))
                    pe.matmul(ps[4][p, 0:SEQ], v_tok[:, 0, 0, p], prob_tf[:, j, 0:SEQ], start=True, stop=False)
                    mm = pe.matmul(ps[4][p, 128:SEQ], v_tok[:, 0, 1, p], prob_tf[:, j, SEQ:384],
                                   start=False, stop=True)
                mm.then_inc(s_o, 1)
                pe.wait_ge(s_sq, u + 1)
                pe.matmul(ps[5][:, 0:SEQ], sq[:, ONES_HALF, :], head_sq[:, 0, 0:SEQ], start=True, stop=True)\
                    .then_inc(s_var, 1)

            with pe.Fori(0, PAIRS) as u:
                def ready_at(u, j):
                    return u * 2 + j + 1
                stage_values(u)
                for j in range(2):
                    p = slice(64 * j, 64 * j + 64)
                    pe.matmul(ps[j][:, 0:SEQ], raw_qk[p, 1, 0:128], raw_qk[p, 0, 0:SEQ], start=True, stop=True)
                    pe.matmul(ps[j][:, SEQ:384], raw_qk[p, 1, 128:SEQ], raw_qk[p, 0, 128:SEQ],
                              start=True, stop=True).then_inc(s_z, 1)
                for j in range(2):
                    pe.wait_ge(s_L, u * 2 + j + 1)
                    L = log_rest[:, j, :]
                    pe.matmul(ps[j][:, 0:SEQ], sq[:, AFTER, :], L[:, 0:SEQ], start=True, stop=False)
                    pe.matmul(ps[j][:, 128:SEQ], sq[:, ALL_ONES, :], L[:, SEQ:384], start=False, stop=True)
                    pe.matmul(ps[j][:, SEQ:384], sq[:, AFTER, :], L[:, SEQ:384], start=True, stop=True)\
                        .then_inc(s_btw, 1)
                head_output(u, s_am)

            pe.wait_ge(bias_s, 32)
            with pe.Fori(0, PAIRS) as n:
                def ready_at(u, j):
                    return (u - PAIRS) * 2 + j + 1
                u = n + PAIRS
                stage_values(u)
                for j in range(2):
                    p = slice(64 * j, 64 * j + 64)
                    pe.matmul(ps[j][:, 0:384], sq[:, FLIP, :], at(head_bias, n * 2 + j, 384),
                              start=True, stop=False)
                    pe.matmul(ps[j][:, 0:128], raw_qk[p, 0, 0:128], raw_qk[p, 1, 0:128],
                              start=False, stop=False)
                    pe.matmul(ps[j][:, 128:384], raw_qk[p, 0, 128:SEQ], raw_qk[p, 1, 0:SEQ],
                              start=False, stop=True).then_inc(d_S, 1)
                for j in range(2):
                    pe.wait_ge(d_prob, n * 2 + j + 1)
                    P = prob_flat[:, j, :]
                    pe.transpose(ps[j][:, 0:128], P[:, 0:128], sq[:, IDENT, :])
                    pe.transpose(ps[j][:, 128:256], P[:, 128:256], sq[:, IDENT, :])
                    pe.transpose(ps[j][:, 256:384], P[:, 256:384], sq[:, IDENT, :]).then_inc(d_pt, 1)
                head_output(u, d_ptc)

            pe.wait_ge(s_lo, 2 * PAIRS)
            with pe.Fori(0, 2) as i:
                group(i + G_OUT, i * 2 + A_OUT, X, SEQ)

            def layer_norm(k):
                pe.wait_ge(ln_s1, k + 1)
                pe.matmul(ps[0][:, 0:SEQ], sq[:, ONES_D, :], row_sum[:, 0:SEQ], start=True, stop=True)\
                    .then_inc(ln_mean, 1)
                pe.wait_ge(ln_s2, k + 1)
                pe.matmul(ps[1][:, 0:SEQ], sq[:, ONES_D, :], row_sum[:, 0:SEQ], start=True, stop=True)\
                    .then_inc(ln_var, 1)

            layer_norm(0)
            pe.wait_ge(ln_out, 1)
            for t in range(2):
                for k in range(KT):
                    mm = pe.matmul(ps[0][:, t * 16:(t + 1) * 16], h[:, k, t * 128:(t + 1) * 128], wr[:, k, :],
                                   start=k == 0, stop=k == KT - 1)
            mm.then_inc(logit_s, 1)
            for t in range(2):
                for k in range(KT):
                    mm = pe.transpose(sum_bank[:, t * ROW + k * 128:t * ROW + (k + 1) * 128],
                                      h[:, k, t * 128:(t + 1) * 128], sq[:, IDENT, :])
            mm.then_inc(tok_turned, 1)
            pe.wait_ge(rt_gate, 1)
            before = tri[:, 0, 0:128]
            pe.matmul(ps[1][:, 0:16], before, rt[:, 0, 12, :], start=True, stop=True)
            pe.matmul(ps[1][:, 16:32], before, rt[:, 1, 12, :], start=True, stop=False)
            pe.matmul(ps[1][:, 16:32], sq[:, ALL_ONES, :], rt[:, 0, 12, :], start=False, stop=True)
            pe.matmul(ps[1][:, 32:48], sq[:, ALL_ONES, :], rt[:, 0, 12, :], start=True, stop=False)
            pe.matmul(ps[1][:, 32:48], sq[:, ALL_ONES, :], rt[:, 1, 12, :], start=False, stop=True)\
                .then_inc(slots_mm, 1)
            pe.wait_ge(slots_ready, 1)
            for t in range(2):
                mm = pe.transpose(ps[1][0:EXPERTS, t * 128:(t + 1) * 128], slot_of[:, t, 0:EXPERTS], sq[:, IDENT, :])
            mm.then_inc(rt_t, 1)
            pe.wait_ge(rt_row, 1)
            for e in range(EXPERTS):
                if e >= 2:
                    pe.wait_ge(rt_all, e - 1)
                pe.matmul(lin[e % 2][:, 0:SEQ], sq[0:EXPERTS, IDENT, e:e + 1].broadcast_to((EXPERTS, 128)),
                          gate_row[:, :], start=True, stop=True).then_inc(rt_bc, 1)
            pe.wait_ge(rt_all, EXPERTS)
            pe.wait_ge(tok_split, 1)
            for b in range(4):
                mm = pe.matmul(banks[:, 4 + b, :], sq[:, IDENT, :], res_row[:, b * 512:(b + 1) * 512],
                               start=True, stop=False, skip_group_check=True)
            mm.then_inc(sum_open, 1)

            def gather(half):
                src = (tok_hi, tok_lo)[half]
                for k in range(KT):
                    for t in range(2):
                        mm = pe.matmul(gate_bank[:, k * 128:(k + 1) * 128],
                                       src[:, t * ROW + k * 128:t * ROW + (k + 1) * 128], sel[:, t, :],
                                       start=t == 0, stop=t == 1)
                mm.then_inc(gathered, 1)

            def scatter():
                for t in range(2):
                    for src in (out_lo, out_hi):
                        for b in range(2):
                            mm = pe.matmul(banks[:, 4 + 2 * t + b, :], sel_t[:, t * 128:(t + 1) * 128],
                                           src[:, b * 512:(b + 1) * 512], start=False, stop=False,
                                           skip_group_check=True)
                mm.then_inc(scattered, 1)

            def experts(p):
                base = G_EXP + p * (G_END - G_EXP)
                pe.wait_ge(sel_ready, 17 * p + 1)
                gather(0)
                pe.wait_ge(x_hi_got, 17 * p + 1)
                gather(1)
                with pe.Fori(0, EXPERTS) as e:
                    E = e + EXPERTS * p
                    X = e + 17 * p

                    def rows(n, hi, lo, dst):
                        s, k = n % SLOTS, n % KT
                        pe.wait_ge(split_ready, (e * 6 + (base + n // SLOTS)) * SLOTS + (s + 1 + SLOTS))
                        wh, wl = [w[:, s, :, :].rearrange("p k m -> p (k m)") for w in (w_hi, w_lo)]
                        steps = [(lo, wh), (hi, wl), (hi, wh)]
                        for i, (x, w) in enumerate(steps):
                            for b in range(2):
                                mm = pe.matmul(banks[:, dst + b, :], x[:, k, :], w[:, b * 512:(b + 1) * 512],
                                               start=k == 0 and i == 0, stop=k == KT - 1 and i == 2)
                        mm.then_inc(chunk_done, 1)

                    pe.wait_ge(x_lo_got, X + 1)
                    for n in range(0, 8):
                        rows(n, slot_x_hi, slot_x_lo, 0)
                    pe.wait_ge(gated_lo, E + 1)
                    for n in range(8, 16):
                        rows(n, slot_x_hi, slot_x_lo, 2)
                        if n == 8:
                            scatter()
                    pe.wait_ge(hid_done, E + 1)
                    for t in range(2):
                        pe.matmul(banks[:, 2, 0:1], sel[:, t, :].bitcast(F32), col(rt[:, t, 11, :], e),
                                  start=t == 0, stop=t == 1)
                    for k in range(KT):
                        mm = pe.transpose(gate_bank[:, k * 128:(k + 1) * 128], hid_row[:, k * 128:(k + 1) * 128],
                                          sq[:, IDENT, :])
                    mm.then_inc(hid_turned, 1)
                    pe.wait_ge(hid_lo, E + 1)
                    for n in range(16, 24):
                        rows(n, slot_h_hi, slot_h_lo, 2)
                        if n == 18:
                            pe.wait_ge(sel_ready, X + 2)
                            gather(0)
                        if n == 21:
                            pe.wait_ge(x_hi_got, X + 2)
                            gather(1)
                pe.wait_ge(gated_lo, EXPERTS * (p + 1) + 1)
                scatter()

            experts(0)
            pe.wait_ge(flag_ready, 1)
            crowded = pe.value_load(flag[0:1, 0:1], min_val=0, max_val=1)
            with pe.If(crowded > 0):
                pe.wait_ge(cleared, 1)
                experts(1)
            for b in range(4):
                mm = pe.matmul(banks[:, 4 + b, :], slot_none[0:1, 0:128], slot_none[0:1, 0:512],
                               start=False, stop=True, skip_group_check=True)
            mm.then_inc(sum_done, 1)

        @block.scalar
        def _(act):
            A_ = nc.scalar.activation

            def split(g, s):
                act.wait_ge(landed[s], (g + 1) * 16)
                act.wait_ge(chunk_done, g * SLOTS + (s + 1))
                A_(w_hi[:, s, :, :], raw[:, s, :, :], ACT.Copy).then_inc(hi_ready, 1)

            def ahead(g, s):
                split(g + (s + 2) // SLOTS, (s + 2) % SLOTS)

            def product(g, s):
                act.wait_ge(chunk_done, g * SLOTS + (s + 1 + SLOTS))

            def power_half(dst, src, scale, bias):
                A_(dst, src, ACT.Ln, scale=scale, bias=bias)
                act.drain()
                return A_(dst, dst, ACT.Exp, scale=-0.5)

            def evac(g, s, dst, func=ACT.Copy, scale=1.0):
                product(g, s)
                return A_(dst, lin[s % 2][:, 0:TOK], func, scale=scale)

            act.wait_ge(set_up, 1)
            split(0, 0)
            split(0, 1)

            with act.Fori(0, LAYERS) as l:
                G = l * G_LAYER
                load_exp_ln(nc, act)
                act.wait_ge(lay_ready, l + 1)
                A_(decay_rate[:, :], lay[:, C_DECAY:C_DECAY + 16], ACT.Exp).then_inc(rate_ready, 1)
                act.wait_ge(h_ready, l * 2 + 1)
                A_(wide[:, :, :], h[:, :, :], ACT.Square).then_inc(norm_sq, 1)
                act.wait_ge(norm_bc, l * 4 + 1)
                power_half(rstd[:, :], ps[0][:, 0:TOK], 1.0, eps[:, 0:1]).then_inc(norm_rstd, 1)
                for k in range(KT):
                    act.wait_ge(u_ready, (l * 2) * KT + k + 1)
                    A_(x_hi[:, k, :], wide[:, k, :], ACT.Copy).then_inc(u_hi, 1)
                act.wait_ge(bias_stored, 16)
                with act.Fori(0, 2) as i:
                    for s in range(SLOTS):
                        ahead(G + G_GATE + i, s)
                        evac(G + G_GATE + i, s, at(gates, i * 4 + s), ACT.Silu).then_inc(acc_free[s % 2], 1)
                with act.Fori(0, 4) as i:
                    for s in range(SLOTS):
                        ahead(G + G_SIG + i, s)
                        evac(G + G_SIG + i, s, at(gates, i * 4 + (s + KT)), ACT.Sigmoid).then_inc(acc_free[s % 2], 1)
                act.drain().then_inc(gates_ready, 1)
                load_exp_ln(nc, act)
                with act.Fori(0, PAIRS) as i:
                    u = l * PAIRS + i
                    g = G + G_RET + i
                    for j in range(2):
                        act.wait_ge(decay_arg, u * 2 + j + 1)
                        A_(decay[:, j, :], decay[:, j, :], ACT.Exp, scale=-1.0).then_inc(decay_ready, 1)
                    for s in range(SLOTS):
                        ahead(g, s)
                        product(g, s)
                        dst = raw_qk[:, s, :] if s < 2 else raw_v[:, s - 2, :]
                        A_(dst, lin[s % 2][:, 0:TOK], ACT.Copy).then_inc(ret_raw, 1)
                        act.drain().then_inc(acc_free[s % 2], 1)
                    for j in range(2):
                        act.wait_ge(v_turned, u * 2 + j + 1)
                        A_(v_tok[:, j, 0:2, :], ps[2 + j][:, 0:256].rearrange("p (t n) -> p t n", t=2), ACT.Copy)
                        A_(v_tok[0:16, j, 2, :], ps[2 + j][0:16, 256:384], ACT.Copy).then_inc(v_ready, 1)
                    for j in range(2):
                        act.wait_ge(head_out, u * 2 + j + 1)
                        A_(head_sq[:, j, :], ps[(0, 5)[j]][:, 0:TOK], ACT.Square).then_inc(squared, 1)
                    for j in range(2):
                        act.wait_ge(var_done, u * 2 + j + 1)
                        power_half(head_rstd[:, j, :], ps[(1, 2)[j]][:, 0:TOK], 1.0, eps[:, 0:1]).then_inc(head_rs, 1)
                    for j in range(2):
                        act.wait_ge(y_ready, u * 2 + j + 1)
                        A_(at(f_hi, i * 2 + j), head_y[:, j, :], ACT.Copy).then_inc(y_hi, 1)
                for s in range(SLOTS):
                    g = G + G_ATT
                    ahead(g, s)
                    product(g, s)
                    if s < 2:
                        dst = raw_qk[:, 1, :] if s == 0 else raw_v[:, 0, :]
                        A_(dst, lin[s % 2][:, 0:TOK], ACT.Copy).then_inc(a_raw, 1)
                        act.drain().then_inc(acc_free[s % 2], 1)
                    else:
                        A_(q_att[:, s - 2, :], lin[s % 2][:, 0:TOK], ACT.Copy).then_inc(acc_free[s % 2], 1)
                for s in range(SLOTS):
                    g = G + G_ATT + 1
                    ahead(g, s)
                    if s < 2:
                        product(g, s)
                        A_(q_att[:, s + 2, :], lin[s % 2][:, 0:TOK], ACT.Copy).then_inc(acc_free[s % 2], 1)
                act.wait_ge(a_vt, l + 1)
                A_(v_tok[:, 0, 0:2, :], ps[2][:, 0:256].rearrange("p (t n) -> p t n", t=2), ACT.Copy)
                A_(v_tok[0:16, 0, 2, :], ps[2][0:16, 256:384], ACT.Copy).then_inc(a_v, 1)
                act.drain()
                with act.Fori(0, PAIRS) as i:
                    u = l * PAIRS + i
                    A_(raw_qk[:, 0, :], at(q_att, i), ACT.Copy).then_inc(a_stage, 1)
                    for j in range(2):
                        act.wait_ge(a_max, u * 2 + j + 1)
                        for t, (t0, tn) in enumerate(TILES):
                            A_(prob[0:tn, j, t, :], prob[0:tn, j, t, :], ACT.Exp, bias=small[0:tn, j, 1, t:t + 1],
                               accum_out=small[0:tn, j, 2, t:t + 1])
                        for t, (t0, tn) in enumerate(TILES):
                            mm = A_(small[0:tn, j, 3, t:t + 1], sink_col[0:tn, j:j + 1], ACT.Exp,
                                    bias=small[0:tn, j, 1, t:t + 1])
                        mm.then_inc(a_exp, 1)
                    for j in range(2):
                        act.wait_ge(a_pt, u * 2 + j + 1)
                        for k, (k0, kn) in enumerate(TILES):
                            mm = A_(prob_t[0:kn, j, k, :], ps[3 * j + k][0:kn, 0:TOK], ACT.Copy)
                        mm.then_inc(a_ptc, 1)
                    for j in range(2):
                        p = slice(64 * j, 64 * j + 64)
                        act.wait_ge(a_o, u * 2 + j + 1)
                        A_(at(f_hi, i + 8, p=p), ps[3 * j][p, 0:TOK], ACT.Copy).then_inc(a_hi, 1)
                    act.wait_ge(a_lo, u * 2 + 2)
                with act.Fori(0, 2) as i:
                    for s in range(SLOTS):
                        ahead(G + G_RETO + i, s)
                for s in range(SLOTS):
                    ahead(G + G_ATTO, s)
                for k in range(KT):
                    act.wait_ge(m_ready, l * KT + k + 1)
                    A_(x_hi[:, k, :], wide[:, k, :], ACT.Copy).then_inc(m_hi, 1)
                with act.Fori(0, 2) as i:
                    for s in range(SLOTS):
                        ahead(G + G_MIX + i, s)
                        if s == 0:
                            act.wait_ge(m_lo, l + 1)
                        evac(G + G_MIX + i, s, at(wide, i * 4 + s)).then_inc(acc_free[s % 2], 1)
                act.drain().then_inc(mix_ready, 1)
                A_(gates[:, 0:KT, :], wide[:, :, :], ACT.Square).then_inc(norm_sq, 1)
                act.wait_ge(norm_bc, l * 4 + 2)
                power_half(rstd[:, :], ps[0][:, 0:TOK], 1.0, eps[:, 0:1]).then_inc(norm_rstd, 1)
                act.wait_ge(h_ready, l * 2 + 2)
                A_(wide[:, :, :], h[:, :, :], ACT.Square).then_inc(norm_sq, 1)
                act.wait_ge(norm_bc, l * 4 + 3)
                power_half(rstd[:, :], ps[0][:, 0:TOK], 1.0, eps[:, 0:1]).then_inc(norm_rstd, 1)
                for k in range(KT):
                    act.wait_ge(u_ready, (l * 2 + 1) * KT + k + 1)
                    A_(x_hi[:, k, :], wide[:, k, :], ACT.Copy).then_inc(u_hi, 1)
                with act.Fori(0, FF_HALVES) as f:
                    with act.Fori(0, 4) as i:
                        for s in range(SLOTS):
                            ahead(G + G_FF + f * G_HALF + i, s)
                            act.wait_ge(f_act, (l * FF_HALVES + f) * FF_BLOCKS + i * 4 + (s + 1))
                            A_(at(f_hi, i * 4 + s), head_y[:, s % 2, :], ACT.Copy).then_inc(f_hi_s, 1)
                    with act.Fori(0, 4) as i:
                        for s in range(SLOTS):
                            ahead(G + G_FF + 4 + f * G_HALF + i, s)
                act.wait_ge(y_sum, l + 1)
                A_(gates[:, 0:KT, :], wide[:, :, :], ACT.Square).then_inc(norm_sq, 1)
                act.wait_ge(norm_bc, l * 4 + 4)
                power_half(rstd[:, :], ps[0][:, 0:TOK], 1.0, eps[:, 0:1]).then_inc(norm_rstd, 1)

            act.wait_ge(h_ready, 2 * LAYERS + 1)
            A_(x_hi[:, :, 0:SEQ], h[:, :, META:TOK], ACT.Copy).then_inc(x1_hi, 1)
            with act.Fori(0, 6) as i:
                for s in range(SLOTS):
                    ahead(i + G_QKV, s)
                    product(i + G_QKV, s)
                    A_(at(gates, i * 4 + s, SEQ), lin[s % 2][:, 0:SEQ], ACT.Copy).then_inc(acc_free[s % 2], 1)
            act.drain()

            def stage(block0, u):
                A_(raw_qk[:, 0, 0:SEQ], at(gates, block0, SEQ), ACT.Copy, scale=0.125)
                A_(raw_qk[:, 1, 0:SEQ], at(gates, block0 + 1, SEQ), ACT.Copy)
                A_(raw_v[:, 0, 0:SEQ], at(gates, block0 + 2, SEQ), ACT.Copy)
                act.drain().then_inc(s_stage, 1)
                act.wait_ge(s_vt, u + 1)
                A_(v_tok[:, 0, 0:2, :], ps[2][:, 0:256].rearrange("p (t n) -> p t n", t=2), ACT.Copy)\
                    .then_inc(s_v, 1)

            def finish(u):
                act.wait_ge(s_o, u + 1)
                A_(head_sq[:, 0, 0:SEQ], ps[4][:, 0:SEQ], ACT.Square).then_inc(s_sq, 1)
                act.wait_ge(s_var, u + 1)
                power_half(head_rstd[:, 0, 0:SEQ], ps[5][:, 0:SEQ], 1.0, eps[:, 0:1]).then_inc(s_rs, 1)
                act.wait_ge(s_y, u + 1)
                A_(at(x_hi, u, SEQ), head_y[:, 0, 0:SEQ], ACT.Copy).then_inc(s_hi, 1)
                act.wait_ge(s_lo, u + 1)

            with act.Fori(0, PAIRS) as u:
                stage(u * 3, u)
                for j in range(2):
                    act.wait_ge(s_z, u * 2 + j + 1)
                    t = prob_flat[:, j, :]
                    A_(t, ps[j][:, 0:384], ACT.Abs)
                    act.drain()
                    A_(t, t, ACT.Exp, scale=-1.0)
                    act.drain()
                    A_(t, t, ACT.Ln, bias=1.0).then_inc(s_log, 1)
                for j in range(2):
                    act.wait_ge(s_arg, u * 2 + j + 1)
                    A_(prob_tf[:, j, :], prob_flat[:, j, :], ACT.Exp).then_inc(s_a, 1)
                finish(u)
            with act.Fori(0, PAIRS) as n:
                u = n + PAIRS
                stage(n * 3 + 12, u)
                for j in range(2):
                    act.wait_ge(d_max, n * 2 + j + 1)
                    P = prob_flat[:, j, :]
                    A_(P[:, 0:128], ps[j][:, 0:128], ACT.Exp, bias=small[:, j, 1, 0:1], accum_out=small[:, j, 2, 0:1])
                    A_(P[:, 128:384], ps[j][:, 128:384], ACT.Exp, bias=small[:, j, 1, 1:2],
                       accum_out=small[:, j, 2, 1:2]).then_inc(d_exp, 1)
                for j in range(2):
                    act.wait_ge(d_pt, n * 2 + j + 1)
                    T = prob_tf[:, j, :]
                    A_(T, ps[j][:, 0:384], ACT.Copy).then_inc(d_ptc, 1)
                finish(u)
            with act.Fori(0, 2) as i:
                for s in range(SLOTS):
                    ahead(i + G_OUT, s)

            def layer_norm(k):
                act.wait_ge(ln_c, k + 1)
                A_(gates[:, 0:KT, 0:SEQ], wide[:, :, 0:SEQ], ACT.Square).then_inc(ln_sq, 1)
                act.wait_ge(ln_var, k + 1)
                power_half(rstd[:, 0:SEQ], ps[1][:, 0:SEQ], 1.0, eps[:, 1:2]).then_inc(ln_rs, 1)

            layer_norm(0)
            act.wait_ge(ln_out, 1)
            act.wait_ge(tok_turned, 1)
            A_(tok_hi, sum_bank, ACT.Copy).then_inc(tok_hi_s, 1)
            act.wait_ge(rt_max, 1)
            for t in range(2):
                mm = A_(rt[:, t, 2, :], rt[:, t, 0, :], ACT.Exp, bias=rt[:, t, 1, 0:1], accum_out=rt[:, t, 1, 1:2])
            mm.then_inc(rt_exp, 1)
            for e in range(EXPERTS):
                act.wait_ge(rt_bc, e + 1)
                A_(gates[:, e, 0:SEQ], lin[e % 2][:, 0:SEQ], ACT.Copy).then_inc(rt_all, 1)

            def experts(p):
                base = G_EXP + p * (G_END - G_EXP)

                def take_x(half, X):
                    act.wait_ge(gathered, X * 2 + (half + 1))
                    dst = (slot_x_hi, slot_x_lo)[half]
                    A_(dst.rearrange("p k n -> p (k n)"), gate_bank, ACT.Copy)\
                        .then_inc((x_hi_got, x_lo_got)[half], 1)

                take_x(0, 17 * p)
                take_x(1, 17 * p)
                with act.Fori(0, EXPERTS) as e:
                    E = e + EXPERTS * p
                    X = e + 17 * p
                    for n in range(24):
                        ahead(e * 6 + (base + n // SLOTS), n % SLOTS)
                        if n == 9:
                            product(e * 6 + (base + 1), 3)
                            A_(silu_row, gate_bank, ACT.Silu).then_inc(silu_done, 1)
                        if n == 15:
                            act.wait_ge(hid_turned, E + 1)
                            A_(slot_h_hi.rearrange("p k n -> p (k n)"), gate_bank, ACT.Copy).then_inc(hid_hi, 1)
                        if n == 19:
                            take_x(0, X + 1)
                        if n == 22:
                            take_x(1, X + 1)
                        if n == 23:
                            product(e * 6 + (base + 5), 3)
                            A_(out_hi, up_bank, ACT.Copy, scale=slot_gate[:, 0:1]).then_inc(gated_hi, 1)

            experts(0)
            act.wait_ge(flag_ready, 1)
            crowded = act.value_load(flag[0:1, 0:1], min_val=0, max_val=1)
            with act.If(crowded > 0):
                experts(1)
            load_exp_ln(nc, act)
            act.wait_ge(var_ready, 1)
            power_half(moments[:, :, 2:3], moments[:, :, 1:2], 1.0, eps[:, 1:2]).then_inc(fin_rstd, 1)

        @block.vector
        def _(dve):
            TT, TS, STT = nc.vector.tensor_tensor, nc.vector.tensor_scalar, nc.vector.scalar_tensor_tensor

            def split(g, s):
                dve.wait_ge(hi_ready, g * SLOTS + (s + 1))
                TT(w_lo[:, s, :, :], raw[:, s, :, :], w_hi[:, s, :, :], ALU.subtract).then_inc(split_ready, 1)

            def ahead(g, s):
                split(g + (s + 2) // SLOTS, (s + 2) % SLOTS)

            def product(g, s):
                dve.wait_ge(chunk_done, g * SLOTS + (s + 1 + SLOTS))

            def norm_sums(w, src):
                dve.wait_ge(norm_sq, w + 1)
                nc.vector.tensor_reduce(row_sum[:, :], src[:, 0:KT, :].rearrange("p k n -> p n k"), AX.X, ALU.add)\
                    .then_inc(norm_sum, 1)
                dve.wait_ge(norm_rstd, w + 1)

            def scaled_input(w, which, gain):
                norm_sums(w, wide)
                for k in range(KT):
                    STT(wide[:, k, :], h[:, k, :], lay[:, gain + k:gain + k + 1], rstd[:, :],
                        ALU.mult, ALU.mult).then_inc(u_ready, 1)
                for k in range(KT):
                    dve.wait_ge(u_hi, which * KT + k + 1)
                    TT(x_lo[:, k, :], wide[:, k, :], x_hi[:, k, :], ALU.subtract)
                dve.drain().then_inc(u_lo, 1)

            def add_normed(w, gain):
                norm_sums(w, gates)
                for k in range(KT):
                    STT(wide[:, k, :], wide[:, k, :], lay[:, gain + k:gain + k + 1], rstd[:, :], ALU.mult, ALU.mult)
                dve.drain()
                for k in range(KT):
                    TT(h[:, k, :], h[:, k, :], wide[:, k, :], ALU.add)
                dve.drain().then_inc(h_ready, 1)

            def rope(dst, raw_in, turned, tab):
                TT(head_sq[:, 0, :], raw_in, rope_t[:, tab, :], ALU.mult)
                TT(head_sq[:, 1, :], turned, rope_t[:, tab + 1, :], ALU.mult)
                dve.drain()
                return TT(dst, head_sq[:, 0, :], head_sq[:, 1, :], ALU.add)

            dve.memset(eps[:, 0:1], RMS_EPS)
            dve.memset(eps[:, 1:2], LN_EPS)
            dve.memset(small[:, :, :, :], 1.0)
            dve.drain().then_inc(set_up, 1)
            dve.sem_inc(split_ready, SLOTS)
            dve.sem_inc(acc_free[0], 1)
            dve.sem_inc(acc_free[1], 1)
            dve.wait_ge(h_in_s, 16)
            dve.wait_ge(consts, 16 * N_CONST)
            dve.sem_inc(h_ready, 1)
            dve.wait_ge(bmm_s, 1)
            TT(brow[:, :], ps[5][0:8, :], badd[:, :], ALU.add).then_inc(brow_s, 1)
            split(0, 0)
            split(0, 1)

            with dve.Fori(0, LAYERS) as l:
                G = l * G_LAYER
                nc.vector.tensor_copy(lay[:, :], at(par, l, C_LAYER)).then_inc(lay_ready, 1)
                dve.drain()
                scaled_input(l * 4, l * 2, C_GAIN)
                with dve.Fori(0, 6) as i:
                    for s in range(SLOTS):
                        ahead(G + G_GATE + i, s)
                with dve.Fori(0, PAIRS) as i:
                    dve.wait_ge(gates_ready, l + 1)
                    dve.wait_ge(rate_ready, l + 1)
                    u = l * PAIRS + i
                    g = G + G_RET + i
                    for j in range(2):
                        TS(decay[:, j, :], dist[:, 0, :], col(decay_rate, i * 2 + j), None, ALU.mult)
                    dve.drain()
                    for j in range(2):
                        STT(decay[:, j, :], dist[:, 1, :], col(decay_rate, i * 2 + (8 + j)), decay[:, j, :],
                            ALU.mult, ALU.add).then_inc(decay_arg, 1)
                    ahead(g, 0)
                    ahead(g, 1)
                    ahead(g, 2)
                    for j in range(2):
                        dve.wait_ge(perm_done, u * 2 + j + 1)
                        rope((q_rot, k_rot)[j][:, :], raw_qk[:, j, :], ps[j][:, 0:TOK], 2 * j).then_inc(ret_rot, 1)
                        dve.drain()
                        if j == 0:
                            ahead(g, 3)
                    for j in range(2):
                        dve.wait_ge(scores, u * 2 + j + 1)
                        dve.wait_ge(decay_ready, u * 2 + j + 1)
                        for t, (t0, tn) in enumerate(TILES):
                            TT(prob_t[0:tn, j, t, :], ps[((0, 1, 4), (5, 2, 3))[j][t]][0:tn, 0:TOK],
                               decay[0:tn, j, 256 - t0:256 - t0 + TOK], ALU.mult)
                        dve.drain().then_inc(decayed, 1)
                    for j in range(2):
                        dve.wait_ge(head_rs, u * 2 + j + 1)
                        TT(head_y[:, j, :], ps[(0, 5)[j]][:, 0:TOK], head_rstd[:, j, :], ALU.mult)
                    dve.drain()
                    for j in range(2):
                        TT(head_y[:, j, :], head_y[:, j, :], at(gates, i * 2 + j), ALU.mult)
                    dve.drain().then_inc(y_ready, 2)
                    for j in range(2):
                        dve.wait_ge(y_hi, u * 2 + j + 1)
                        TT(at(f_lo, i * 2 + j), head_y[:, j, :], at(f_hi, i * 2 + j), ALU.subtract)
                    dve.drain().then_inc(y_lo, 2)
                for s in range(SLOTS):
                    ahead(G + G_ATT, s)
                for s in range(SLOTS):
                    ahead(G + G_ATT + 1, s)
                dve.wait_ge(a_perm, l + 1)
                rope(k_rot[:, :], raw_qk[:, 1, :], ps[0][:, 0:TOK], 6).then_inc(a_rot, 1)
                dve.drain()
                with dve.Fori(0, PAIRS) as i:
                    u = l * PAIRS + i
                    dve.wait_ge(a_qperm, u + 1)
                    rope(q_rot[:, :], raw_qk[:, 0, :], ps[0][:, 0:TOK], 4).then_inc(a_qrot, 1)
                    dve.drain()
                    for j in range(2):
                        dve.wait_ge(a_scores, u * 2 + j + 1)
                        nc.vector.tensor_copy(sink_col[:, j:j + 1], col(lay, i * 2 + (C_SINK + j)))
                        dve.drain()
                        for t, (t0, tn) in enumerate(TILES):
                            nc.vector.tensor_tensor_reduce(
                                prob[0:tn, j, t, :], ps[3 * j + t][0:tn, 0:TOK], mask[0:tn, t, :], 1.0,
                                sink_col[0:tn, j:j + 1], ALU.add, ALU.max, small[0:tn, j, 0, t:t + 1])
                        dve.drain()
                        TS(small[:, j, 1, 0:3], small[:, j, 0, 0:3], -1.0, None, ALU.mult).then_inc(a_max, 1)
                    for j in range(2):
                        dve.wait_ge(a_exp, u * 2 + j + 1)
                        TT(small[:, j, 2, 0:3], small[:, j, 2, 0:3], small[:, j, 3, 0:3], ALU.add)
                        dve.drain()
                        nc.vector.reciprocal(small[:, j, 2, 0:3], small[:, j, 2, 0:3])
                        dve.drain()
                        for t, (t0, tn) in enumerate(TILES):
                            TS(prob[0:tn, j, t, :], prob[0:tn, j, t, :], small[0:tn, j, 2, t:t + 1], None, ALU.mult)
                        dve.drain().then_inc(a_prob, 1)
                    for j in range(2):
                        p = slice(64 * j, 64 * j + 64)
                        dve.wait_ge(a_hi, u * 2 + j + 1)
                        TT(at(f_lo, i + 8, p=p), ps[3 * j][p, 0:TOK], at(f_hi, i + 8, p=p), ALU.subtract)\
                            .then_inc(a_lo, 1)
                with dve.Fori(0, 2) as i:
                    for s in range(SLOTS):
                        ahead(G + G_RETO + i, s)
                        product(G + G_RETO + i, s)
                        TT(at(wide, i * 4 + s), lin[s % 2][:, 0:TOK], at(gates, i * 4 + (s + KT)), ALU.mult)\
                            .then_inc(acc_free[s % 2], 1)
                dve.drain()
                for s in range(SLOTS):
                    ahead(G + G_ATTO, s)
                    product(G + G_ATTO, s)
                    for b in range(2):
                        TT(head_y[:, b, :], lin[b][:, 0:TOK], gates[:, 2 * KT + 2 * s + b, :], ALU.mult)\
                            .then_inc(acc_free[b], 1)
                    dve.drain()
                    for b in range(2):
                        TT(wide[:, 2 * s + b, :], wide[:, 2 * s + b, :], head_y[:, b, :], ALU.add)\
                            .then_inc(m_ready, 1)
                    dve.drain()
                for k in range(KT):
                    dve.wait_ge(m_hi, l * KT + k + 1)
                    TT(x_lo[:, k, :], wide[:, k, :], x_hi[:, k, :], ALU.subtract)
                dve.drain().then_inc(m_lo, 1)
                with dve.Fori(0, 2) as i:
                    for s in range(SLOTS):
                        ahead(G + G_MIX + i, s)
                dve.wait_ge(mix_ready, l + 1)
                add_normed(l * 4 + 1, C_GAIN + 8)
                scaled_input(l * 4 + 2, l * 2 + 1, C_GAIN + 16)
                dve.memset(wide[:, :, :], 0.0)
                dve.drain()
                with dve.Fori(0, FF_HALVES) as f:
                    with dve.Fori(0, 4) as i:
                        g = G + G_FF + f * G_HALF + i
                        n = (l * FF_HALVES + f) * FF_BLOCKS + i * 4
                        for s in range(SLOTS):
                            ahead(g, s)
                            product(g, s)
                            dst = head_y[:, s % 2, :]
                            TS(dst, lin[s % 2][:, 0:TOK], 0.0, None, ALU.max).then_inc(acc_free[s % 2], 1)
                            dve.drain()
                            TT(dst, dst, dst, ALU.mult).then_inc(f_act, 1)
                            dve.wait_ge(f_hi_s, n + (s + 1))
                            TT(at(f_lo, i * 4 + s), dst, at(f_hi, i * 4 + s), ALU.subtract).then_inc(f_lo_s, 1)
                            dve.drain()
                    with dve.Fori(0, 4) as i:
                        g = G + G_FF + 4 + f * G_HALF + i
                        for s in range(SLOTS):
                            ahead(g, s)
                            if s % 2 == 1:
                                product(g, s)
                                b = s // 2
                                dst = at(wide, i * 2 + b)
                                TT(dst, lin[b][:, 0:TOK], dst, ALU.add).then_inc(acc_free[b], 1)
                    dve.drain()
                dve.drain().then_inc(y_sum, 1)
                add_normed(l * 4 + 3, C_GAIN + 24)

            dve.wait_ge(x1_hi, 1)
            TT(x_lo[:, :, 0:SEQ], h[:, :, META:TOK], x_hi[:, :, 0:SEQ], ALU.subtract).then_inc(x1_lo, 1)
            dve.drain()
            with dve.Fori(0, 6) as i:
                for s in range(SLOTS):
                    ahead(i + G_QKV, s)

            def finish(u):
                dve.wait_ge(s_rs, u + 1)
                STT(head_y[:, 0, 0:SEQ], ps[4][:, 0:SEQ], col(par2, u + C_GHEAD), head_rstd[:, 0, 0:SEQ],
                    ALU.mult, ALU.mult).then_inc(s_y, 1)
                dve.wait_ge(s_hi, u + 1)
                TT(at(x_lo, u, SEQ), head_y[:, 0, 0:SEQ], at(x_hi, u, SEQ), ALU.subtract).then_inc(s_lo, 1)
                dve.drain()

            with dve.Fori(0, PAIRS) as u:
                for j in range(2):
                    dve.wait_ge(s_log, u * 2 + j + 1)
                    sp_ = prob_flat[:, j, :]
                    L = log_rest[:, j, :]
                    STT(L, ps[j][:, 0:384], 0.0, sp_, ALU.max, ALU.add)
                    dve.drain()
                    TT(L, L, tri[:, 1, :], ALU.mult)
                    STT(sp_, ps[j][:, 0:384], 0.0, sp_, ALU.min, ALU.subtract)
                    dve.drain().then_inc(s_L, 1)
                for j in range(2):
                    dve.wait_ge(s_btw, u * 2 + j + 1)
                    TT(prob_flat[:, j, :], prob_flat[:, j, :], ps[j][:, 0:384], ALU.add).then_inc(s_arg, 1)
                for j in range(2):
                    dve.wait_ge(s_a, u * 2 + j + 1)
                    TT(prob_tf[:, j, :], prob_tf[:, j, :], tri[:, 0, :], ALU.mult).then_inc(s_am, 1)
                finish(u)
            with dve.Fori(0, PAIRS) as n:
                u = n + PAIRS
                for j in range(2):
                    dve.wait_ge(d_S, n * 2 + j + 1)
                    nc.vector.tensor_reduce(small[:, j, 0, 0:1], ps[j][:, 0:128], AX.X, ALU.max)
                    nc.vector.tensor_reduce(small[:, j, 0, 1:2], ps[j][:, 128:384], AX.X, ALU.max)
                    dve.drain()
                    TS(small[:, j, 1, 0:2], small[:, j, 0, 0:2], -1.0, None, ALU.mult).then_inc(d_max, 1)
                for j in range(2):
                    dve.wait_ge(d_exp, n * 2 + j + 1)
                    P = prob_flat[:, j, :]
                    nc.vector.reciprocal(small[:, j, 2, 0:2], small[:, j, 2, 0:2])
                    dve.drain()
                    TS(P[:, 0:128], P[:, 0:128], small[:, j, 2, 0:1], None, ALU.mult)
                    TS(P[:, 128:384], P[:, 128:384], small[:, j, 2, 1:2], None, ALU.mult)
                    dve.drain().then_inc(d_prob, 1)
                finish(u)
            with dve.Fori(0, 2) as i:
                for s in range(SLOTS):
                    ahead(i + G_OUT, s)
                    product(i + G_OUT, s)
                    src = h[:, bass.ds(i * 4 + s, 1), META:TOK].rearrange("p a n -> p (a n)")
                    STT(at(wide, i * 4 + s, SEQ), src, ALPHA, lin[s % 2][:, 0:SEQ], ALU.mult, ALU.add)\
                        .then_inc(acc_free[s % 2], 1)
            dve.drain()

            def layer_norm(k, dst):
                nc.vector.tensor_reduce(row_sum[:, 0:SEQ], wide[:, :, 0:SEQ].rearrange("p k n -> p n k"),
                                        AX.X, ALU.add).then_inc(ln_s1, 1)
                dve.wait_ge(ln_mean, k + 1)
                for t in range(KT):
                    TT(wide[:, t, 0:SEQ], wide[:, t, 0:SEQ], ps[0][:, 0:SEQ], ALU.subtract)
                dve.drain().then_inc(ln_c, 1)
                dve.wait_ge(ln_sq, k + 1)
                nc.vector.tensor_reduce(row_sum[:, 0:SEQ], gates[:, 0:KT, 0:SEQ].rearrange("p k n -> p n k"),
                                        AX.X, ALU.add).then_inc(ln_s2, 1)
                dve.wait_ge(ln_rs, k + 1)
                for t in range(KT):
                    TT(wide[:, t, 0:SEQ], wide[:, t, 0:SEQ], rstd[:, 0:SEQ], ALU.mult)
                dve.drain()
                c = C_LN + 16 * k
                for t in range(KT):
                    TS(dst[:, t, 0:SEQ], wide[:, t, 0:SEQ], par2[:, c + t:c + t + 1],
                       par2[:, c + 8 + t:c + 9 + t], ALU.mult, ALU.add)
                dve.drain().then_inc(ln_out, 1)

            layer_norm(0, h)
            dve.wait_ge(logit_s, 1)
            for t in range(2):
                TT(rt[:, t, 0, :], ps[0][:, t * 16:(t + 1) * 16], par2[:, C_BROUTER:C_BROUTER + 16], ALU.add)
            dve.drain()
            for t in range(2):
                nc.vector.tensor_reduce(rt[:, t, 1, 2:3], rt[:, t, 0, :], AX.X, ALU.max)
            dve.drain()
            for t in range(2):
                TS(rt[:, t, 1, 0:1], rt[:, t, 1, 2:3], -1.0, None, ALU.mult)
            dve.drain().then_inc(rt_max, 1)
            dve.wait_ge(rt_exp, 1)
            for t in range(2):
                nc.vector.reciprocal(rt[:, t, 1, 3:4], rt[:, t, 1, 1:2])
            dve.drain()
            for t in range(2):
                TS(rt[:, t, 3, :], rt[:, t, 2, :], rt[:, t, 1, 3:4], None, ALU.mult)
            dve.drain()

            def others_ahead(t, values, n_in, width, dst):
                a = values.rearrange("p (g e) -> p g e", e=n_in)
                g = width // n_in
                m = n_in * n_in * g
                shape4 = lambda x: x.rearrange("p (g a b) -> p g a b", a=n_in, b=n_in)
                other = a.unsqueeze(2).broadcast_to((128, g, n_in, n_in))
                own = a.unsqueeze(3).broadcast_to((128, g, n_in, n_in))
                TT(shape4(cmp[:, t, 0, 0:m]), other, own, ALU.is_gt)
                TT(shape4(cmp[:, t, 1, 0:m]), other, own, ALU.is_equal)
                dve.drain()
                TT(cmp[:, t, 1, 0:m], cmp[:, t, 1, 0:m], early[:, 0:m], ALU.mult)
                dve.drain()
                TT(cmp[:, t, 0, 0:m], cmp[:, t, 0, 0:m], cmp[:, t, 1, 0:m], ALU.add)
                dve.drain()
                nc.vector.tensor_reduce(dst, cmp[:, t, 0, 0:m].rearrange("p (a b) -> p a b", b=n_in), AX.X, ALU.add)
                dve.drain()

            for t in range(2):
                R = lambda i, n=16: rt[:, t, i, 0:n]
                others_ahead(t, R(3), 4, 16, R(4))
                TS(R(5), R(4), 1.5, None, ALU.is_lt)
                dve.drain()
                TT(R(6), R(5), R(3), ALU.mult)
                dve.drain()
                nc.vector.tensor_reduce(R(7, 4), R(6).rearrange("p (g e) -> p g e", e=4), AX.X, ALU.add)
                dve.drain()
                others_ahead(t, R(7, 4), 4, 4, R(8, 4))
                TS(R(9, 4), R(8, 4), 0.5, None, ALU.is_lt)
                nc.vector.reciprocal(rt[:, t, 9, 4:8], R(7, 4))
                dve.drain()
                TT(rt[:, t, 10, 0:4], R(9, 4), rt[:, t, 9, 4:8], ALU.mult)
                dve.drain()
                TT(R(11).rearrange("p (g e) -> p g e", e=4), R(6).rearrange("p (g e) -> p g e", e=4),
                   rt[:, t, 10, 0:4].unsqueeze(2).broadcast_to((128, 4, 4)), ALU.mult)
                dve.drain()
            for t in range(2):
                TS(rt[:, t, 12, :], rt[:, t, 11, :], 0.0, None, ALU.is_gt)
            dve.drain().then_inc(rt_gate, 1)
            dve.wait_ge(slots_mm, 1)
            dve.memset(slot_of[:, :, :], -1.0)
            dve.drain()
            for t in range(2):
                STT(rt[:, t, 13, :], ps[1][:, 16 * t:16 * t + 16], 1.0, rt[:, t, 12, :], ALU.add, ALU.mult)
            nc.vector.tensor_reduce(flag_f[:, :], ps[1][:, 32:48], AX.X, ALU.max)
            dve.drain()
            for t in range(2):
                TS(slot_of[:, t, 0:EXPERTS], rt[:, t, 13, :], -1.0, None, ALU.add)
            dve.drain().then_inc(slots_ready, 1)
            TS(flag[:, :], flag_f[:, :], 128.5, None, ALU.is_gt).then_inc(flag_ready, 1)
            dve.wait_ge(rt_t, 1)
            nc.vector.tensor_copy(gate_row[:, :], ps[1][0:EXPERTS, 0:SEQ]).then_inc(rt_row, 1)
            TS(res_row, sum_bank, ALPHA, None, ALU.mult)
            dve.wait_ge(tok_hi_s, 1)
            TT(tok_lo, sum_bank, tok_hi, ALU.subtract)
            dve.memset(sel_t[:, :].bitcast(F32), 0.0)
            dve.memset(out_hi.bitcast(F32), 0.0)
            dve.memset(out_lo.bitcast(F32), 0.0)
            dve.memset(slot_none[:, :], 0.0)
            dve.drain().then_inc(tok_split, 1)
            dve.sem_inc(gated_lo, 1)
            dve.wait_ge(rt_all, EXPERTS)

            def experts(p):
                base = G_EXP + p * (G_END - G_EXP)

                def select(e):
                    for t in range(2):
                        TS(sel[:, t, :], lane[:, 2 + 128 * p:130 + 128 * p], col(slot_of[:, t, :], e), None,
                           ALU.is_equal)
                    dve.drain().then_inc(sel_ready, 1)

                if p == 0:
                    dve.wait_ge(lane_s, 16)
                select(0)
                with dve.Fori(0, EXPERTS) as e:
                    E = e + EXPERTS * p
                    for n in range(24):
                        ahead(e * 6 + (base + n // SLOTS), n % SLOTS)
                        if n == 15:
                            dve.wait_ge(silu_done, E + 1)
                            product(e * 6 + (base + 3), 3)
                            TT(hid_row, silu_row, up_bank, ALU.mult).then_inc(hid_done, 1)
                            dve.wait_ge(hid_turned, E + 1)
                            nc.vector.tensor_copy(slot_gate[:, :], banks[:, 2, 0:1])
                            dve.wait_ge(hid_hi, E + 1)
                            TT(slot_h_lo.rearrange("p k n -> p (k n)"), gate_bank,
                               slot_h_hi.rearrange("p k n -> p (k n)"), ALU.subtract)
                            dve.drain().then_inc(hid_lo, 1)
                        if n == 16:
                            select(e + 1)
                        if n == 17:
                            dve.wait_ge(scattered, E + (p + 1))
                            TS(sel_t[:, :], at(gates, e, SEQ), lane[:, p:p + 1], None, ALU.is_equal)
                        if n == 23:
                            dve.wait_ge(gated_hi, E + 1)
                            STT(out_lo, up_bank, slot_gate[:, 0:1], out_hi, ALU.mult, ALU.subtract)
                            dve.drain().then_inc(gated_lo, 1)

            experts(0)
            crowded = dve.value_load(flag[0:1, 0:1], min_val=0, max_val=1)
            with dve.If(crowded > 0):
                dve.wait_ge(scattered, EXPERTS + 1)
                dve.memset(sel_t[:, :].bitcast(F32), 0.0)
                dve.drain().then_inc(cleared, 1)
                experts(1)
            dve.wait_ge(sum_done, 1)
            for t in range(2):
                for b in range(2):
                    nc.vector.bn_stats(stats[:, t, b, :], banks[:, 4 + 2 * t + b, :])
            dve.drain()
            for t in range(2):
                nc.vector.bn_aggr(moments[:, t, 0:2], stats[:, t, :, :].rearrange("p b n -> p (b n)"))
            dve.drain().then_inc(var_ready, 1)
            dve.wait_ge(fin_rstd, 1)
            dve.wait_ge(rows_s, 32)
            for t in range(2):
                y = res_row[:, t * ROW:(t + 1) * ROW]
                TS(y, sum_bank[:, t * ROW:(t + 1) * ROW], moments[:, t, 0:1], moments[:, t, 2:3],
                   ALU.subtract, ALU.mult)
                dve.drain()
                TT(y, y, gain_rows[:, 0:ROW], ALU.mult)
                dve.drain()
                TT(y, y, gain_rows[:, ROW:2 * ROW], ALU.add).then_inc(y_half, 1)


_INS = ["weights", "h_in", "layer_par", "second_par", "rope", "toeplitz", "att_mask", "squares", "stick",
        "bias_map", "bias_add", "rel_bias", "w_router", "tie_order", "lanes", "ln_rows"]


def feature_blocks(v):
    import numpy as np
    v = np.asarray(v)
    return np.moveaxis(v.reshape(*v.shape[:-1], -1, 128), -1, 0)


def lay_out_weights(x):
    import numpy as np
    weights = np.zeros((GROUPS * SLOTS, 128, KT * 128), np.float32)

    def tile_rows(w):
        return w.reshape(-1, 128, w.shape[-1]).transpose(1, 0, 2)

    def put(at, w, block, k0=0):
        weights[at] = w[:, k0:k0 + KT, block * 128:(block + 1) * 128].reshape(128, -1)

    for l in range(LAYERS):
        at = l * G_LAYER * SLOTS
        w_in = x["w_in"][l]
        cuts = np.cumsum([0, 512, 512, 1024, 1024, 512, 128, 128, 1024, 1024])
        q_r, k_r, v_r, g_r, q_a, k_a, v_a, gate_r, gate_a = [
            tile_rows(w_in[:, a:b]) for a, b in zip(cuts[:-1], cuts[1:])]
        q_a = q_a.reshape(128, KT, 2, PAIRS, 64).transpose(0, 1, 3, 2, 4).reshape(128, KT, 512)
        order = [(g_r, b) for b in range(KT)] + [(gate_r, b) for b in range(KT)] + [(gate_a, b) for b in range(KT)]
        for i in range(PAIRS):
            order += [(q_r, i), (k_r, i), (v_r, 2 * i), (v_r, 2 * i + 1)]
        order += [(k_a, 0), (v_a, 0)] + [(q_a, i) for i in range(PAIRS)]
        for n, (w, b) in enumerate(order):
            put(at + n, w, b)
        ret_o, mix_o = tile_rows(x["w_ret_o"][l]), tile_rows(x["w_mix_o"][l])
        att_o = x["w_att_o"][l].reshape(2, PAIRS, 64, D).transpose(1, 0, 2, 3).reshape(512, D)
        att_o = tile_rows(att_o)
        for b in range(KT):
            put(at + G_RETO * SLOTS + b, ret_o, b)
            put(at + G_MIX * SLOTS + b, mix_o, b)
        for n in range(KT // 2):
            two = att_o[:, :, n * 256:(n + 1) * 256].reshape(128, 4, 2, 128).transpose(0, 2, 1, 3)
            weights[at + G_ATTO * SLOTS + n] = two.reshape(128, -1)
        ff1, ff2 = tile_rows(x["w_ff1"][l]), tile_rows(x["w_ff2"][l])
        for f in range(FF_HALVES):
            base = at + (G_FF + f * G_HALF) * SLOTS
            for n in range(FF_BLOCKS):
                put(base + n, ff1, f * FF_BLOCKS + n)
                put(base + FF_BLOCKS + n, ff2, n // 2, f * FF_BLOCKS + KT * (n % 2))
    w_in = x["w_in_2"][0]
    sb_q, sb_k, sb_v, dl_q, dl_k, dl_v = [tile_rows(w_in[:, i * 512:(i + 1) * 512]) for i in range(6)]
    n = G_QKV * SLOTS
    for three in ((sb_q, sb_k, sb_v), (dl_q, dl_k, dl_v)):
        for i in range(PAIRS):
            for w in three:
                put(n, w, i)
                n += 1
    w_out = tile_rows(x["w_out_2"][0])
    for b in range(KT):
        put(G_OUT * SLOTS + b, w_out, b)
    n = G_EXP * SLOTS
    for e in range(EXPERTS):
        for name in ("w_gate_2", "w_up_2", "w_down_2"):
            weights[n:n + KT] = x[name][0, e].reshape(KT, 128, D)
            n += KT
    weights[G_END * SLOTS:] = weights[G_EXP * SLOTS:(G_EXP + 1) * SLOTS]
    return weights


def bucket(dist):
    import math

    import numpy as np
    d = np.maximum(dist, 0)
    ratio = np.log(np.maximum(d, 1).astype(np.float32) / np.float32(16)) / np.float32(math.log(2048 / 16))
    large = np.minimum(16 + (ratio * np.float32(16)).astype(np.int32), 31)
    return np.where(d < 16, d, large)


def tables():
    import numpy as np
    f = np.float32
    pos = np.arange(TOK, dtype=f)
    rope = np.zeros((128, 8, TOK), f)
    turn = {}
    for at, (theta, dim) in ((0, (10000.0, 64)), (4, (500000.0, 16))):
        half = dim // 2
        freqs = np.power(f(theta), -np.arange(0, dim, 2, dtype=f) / f(dim)).astype(f)
        ang = (pos[:, None] * freqs[None, :]).astype(f)
        cos, sin = np.ones((64, TOK), f), np.zeros((64, TOK), f)
        cos[:half] = cos[half:dim] = np.cos(ang).T
        sin[:half] = sin[half:dim] = np.sin(ang).T
        for n, t in enumerate((cos / 8, sin / 8, cos, sin)):
            rope[:, at + n] = np.tile(t, (2, 1))
        m = np.zeros((64, 64), f)
        for i in range(half):
            m[i + half, i], m[i, i + half] = -1, 1
        turn[at] = np.kron(np.eye(2, dtype=f), m)
    eye = np.eye(128, dtype=f)
    row, column = np.arange(128)[:, None], np.arange(128)[None, :]
    squares = np.stack([
        turn[0], turn[4], eye - f(1 / 128), eye, np.full((128, 128), 1 / D, f), np.full((128, 128), 1 / 128, f),
        np.kron(np.eye(2, dtype=f), np.full((64, 64), 1 / 64, f)), (row > column).astype(f),
        np.ones((128, 128), f), eye[::-1]], 1)
    rel = np.arange(SPAN)[None, :] - 256 - np.arange(128)[:, None]
    toeplitz = np.stack([np.maximum(rel, 0), np.maximum(-rel, 0)], 1).astype(f)
    i = np.arange(3)[None, :, None] * 128 + np.arange(128)[:, None, None]
    j = np.arange(TOK)[None, None, :]
    att_mask = np.where((j < META) | (np.abs(i - j) <= 128), 0, NEG).astype(f)
    causal = np.concatenate([np.arange(128)[:, None] < np.arange(SEQ)[None, :], row < column], 1).astype(f)
    stick = np.stack([causal, -causal], 1)
    dist = 255 - np.arange(512)
    bias_map = (bucket(dist)[None, :] == np.arange(32)[:, None]).astype(f)
    times = (dist <= 128) * 1 + (dist % 4 == 0) * 1 + (dist % 16 == 0) * 1
    times = np.where(dist >= 0, times, 0)
    add = np.where(times > 0, np.log(np.maximum(times, 1)), NEG).astype(f)
    bias_add = np.tile(add, (8, 1))
    own, other = np.arange(4)[:, None], np.arange(4)[None, :]
    tie_order = np.tile((other < own).astype(f).ravel(), (128, 4))
    lanes = np.concatenate([np.arange(128)[:, None] + [[0, 128]], np.tile(np.arange(SEQ), (128, 1))], 1).astype(f)
    return dict(rope=rope, toeplitz=toeplitz, att_mask=att_mask, squares=np.ascontiguousarray(squares),
                stick=stick, bias_map=bias_map, bias_add=bias_add, tie_order=tie_order, lanes=lanes)


def kernel(**inputs):
    import numpy as np
    import concourse.bacc as bacc
    from concourse.bass_utils import run_bass_kernel_spmd as run

    x = {k: np.asarray(v) for k, v in inputs.items()}
    arrays = tables()
    arrays["weights"] = lay_out_weights(x)
    tokens = np.concatenate([x["meta_tokens"], x["x"][0]], 0)
    arrays["h_in"] = tokens.T.reshape(KT, 128, TOK).transpose(1, 0, 2)
    gains = np.stack([feature_blocks(x[n]) for n in (
        "norm_mix_pre", "norm_mix_post", "norm_ff_pre", "norm_ff_post")], 2)
    every = lambda v: np.broadcast_to(v[None], (128, *v.shape))
    sink = x["attn_sink"].reshape(LAYERS, 2, PAIRS).transpose(0, 2, 1).reshape(LAYERS, 8)
    arrays["layer_par"] = np.concatenate([
        gains.reshape(128, LAYERS, 32), every(x["ret_decay"].reshape(LAYERS, 16)), every(sink)], 2)
    arrays["second_par"] = np.concatenate(
        [feature_blocks(x[n][0]) for n in ("ln1_g_2", "ln1_b_2", "ln2_g_2", "ln2_b_2", "g_sb_2", "g_dil_2")]
        + [every(x["b_router_2"])], 1)
    arrays["ln_rows"] = np.stack([x["ln2_g_2"][0], x["ln2_b_2"][0]])
    arrays["rel_bias"] = x["rel_bias_2"]
    arrays["w_router"] = x["w_router_2"].reshape(KT, 128, EXPERTS).transpose(1, 0, 2)

    nc = bacc.Bacc("TRN2", target_bir_lowering=False, num_devices=1)
    arrays = {f"in_{n}": np.ascontiguousarray(arrays[n]) for n in _INS}
    args = [nc.dram_tensor(n, a.shape, mybir.dt.from_np(a.dtype), kind="ExternalInput").ap()
            for n, a in arrays.items()]
    args.append(nc.dram_tensor("y_out", (2, 128, D), F32, kind="ExternalOutput").ap())
    build_program(nc, *args)
    r = run(nc, [arrays], core_ids=[0])
    return r.results[0]["y_out"].reshape(1, SEQ, D)
```

```python
from contextlib import ExitStack

import concourse.bass as bass
from concourse import mybir

F32 = mybir.dt.float32
F32R = mybir.dt.float32r
ALU = mybir.AluOpType
ACT = mybir.ActivationFunctionType
AX = mybir.AxisListType

D = 1024
SEQ = 256
META = 16
TOK = SEQ + META
LAYERS = 2
KT = D // 128
PAIRS = 4
D_FF = 4 * D
FF_HALVES = 2
FF_BLOCKS = D_FF // 128 // FF_HALVES
EXPERTS = 16
TILES = [(0, 128), (128, 128), (256, TOK - 256)]
SPAN = 2 * TOK
ALPHA = 2.0 ** 0.25
RMS_EPS, HEAD_EPS, LN_EPS = 1e-6, 1e-6, 1e-5
NEG = -1e30

SLOTS = 4
AHEAD = 3
G_GATE, G_SIG, G_RET, G_ATT = 0, 2, 6, 10
G_RETO, G_ATTO, G_MIX, G_FF = 12, 14, 15, 17
G_HALF = 8
G_LAYER = 33
G_QKV = LAYERS * G_LAYER
G_OUT = G_QKV + 6
G_EXP = G_OUT + 2
G_END = G_EXP + 6 * EXPERTS
GROUPS = G_END + 2
RAW = 6

A_GATE, A_SIG, A_RET, A_ATT, A_RETO, A_ATTO, A_MIX, A_FF = 0, 4, 12, 20, 23, 27, 31, 35
A_HALF = 12
A_LAYER = 59
A_QKV = LAYERS * A_LAYER
A_OUT = A_QKV + 12
A_EXP = A_OUT + 4

C_GAIN, C_DECAY, C_SINK, C_LAYER = 0, 32, 48, 56
C_LN, C_GHEAD, C_BROUTER, C_SECOND = 0, 32, 40, 56
LN_SETS = 6


def load_exp_ln(nc, act):
    act.add_instruction(mybir.InstLoadActFuncSet(
        name=nc.get_next_instruction_name(), engine=mybir.EngineType.Activation,
        act_func_set_id=LN_SETS, ins=[], outs=[]))


def build_program(nc, weights, h_in, layer_par, second_par, rope, toeplitz, att_mask, squares,
                  stick, bias_map, bias_add, rel_bias, w_router, tie_order, lanes, ln_rows, out):
    with ExitStack() as ctx:
        def sb(name, shape, dt=F32):
            return ctx.enter_context(nc.sbuf_tensor(name, shape, dt))

        def sem(name):
            return ctx.enter_context(nc.semaphore(name))

        raw = sb("raw", [128, SLOTS, KT, 128])
        w_hi = sb("w_hi", [128, SLOTS, KT, 128], F32R)
        w_lo = sb("w_lo", [128, SLOTS, KT, 128], F32R)
        h = sb("h", [128, KT, TOK])
        wide = sb("wide", [128, KT, TOK])
        x_hi = sb("x_hi", [128, KT, TOK], F32R)
        x_lo = sb("x_lo", [128, KT, TOK], F32R)
        f_hi = sb("f_hi", [128, FF_BLOCKS, TOK], F32R)
        f_lo = sb("f_lo", [128, FF_BLOCKS, TOK], F32R)
        gates = sb("gates", [128, 3 * KT, TOK])
        q_att = sb("q_att", [128, PAIRS + 1, TOK])
        raw_qk = sb("raw_qk", [128, 2, TOK])
        raw_v = sb("raw_v", [128, 2, TOK])
        q_rot = sb("q_rot", [128, TOK])
        k_rot = sb("k_rot", [128, TOK])
        v_tok = sb("v_tok", [128, 2, 3, 128])
        probs = sb("probs", [128, 4 * 3 * TOK])
        prob = probs[:, 0:6 * TOK].rearrange("p (j t n) -> p j t n", j=2, t=3)
        prob_t = probs[:, 6 * TOK:12 * TOK].rearrange("p (j t n) -> p j t n", j=2, t=3)
        decay = probs[:, 0:2 * SPAN].rearrange("p (j n) -> p j n", j=2)
        head_bias = probs[:, 0:8 * 384].rearrange("p (h n) -> p h n", h=8)
        head_sq = sb("head_sq", [128, 2, TOK])
        head_rstd = sb("head_rstd", [128, 2, TOK])
        head_y = sb("head_y", [128, 2, TOK])
        row_sum = sb("row_sum", [128, TOK])
        rstd = sb("rstd", [128, TOK])
        small = sb("small", [128, 2, 4, 4])
        sink_col = sb("sink_col", [128, 2])
        decay_rate = sb("decay_rate", [128, 16])
        par = sb("par", [128, LAYERS, C_LAYER])
        lay = sb("lay", [128, C_LAYER])
        par2 = sb("par2", [128, C_SECOND])
        rope_t = sb("rope_t", [128, 8, TOK])
        dist = sb("dist", [128, 2, SPAN])
        mask = sb("mask", [128, 3, TOK])
        sq = sb("sq", [128, 10, 128])
        tri = sb("tri", [128, 2, 384])
        eps = sb("eps", [128, 2])
        def two_tiles(t):
            axes = "p a n -> p (a n)"
            return t[:, :, :].rearrange(axes)[:, 0:2 * 384].rearrange("p (j n) -> p j n", j=2)
        prob_flat = two_tiles(q_att)
        prob_tf = two_tiles(dist)
        log_rest = two_tiles(mask)
        dil_flat, dil_tf = [wide[:, :, :].rearrange("p a n -> p (a n)")[:, i * 768:(i + 1) * 768]
                            .rearrange("p (j n) -> p j n", j=2) for i in range(2)]
        staged_q, staged_k = (raw_qk[:, 0, :], q_rot[:, :]), (raw_qk[:, 1, :], k_rot[:, :])
        start = gates[:, 2 * KT:3 * KT, :].rearrange("p a n -> p (a n)")
        bmap, badd, brow = start[0:32, 0:512], start[0:8, 512:1024], start[0:8, 1024:1536]
        relb = sb("relb", [32, 8])
        wr = sb("wr", [128, KT, EXPERTS])
        rt = sb("rt", [128, 2, 14, 16])
        slot_of = sb("slot_of", [128, 2, EXPERTS + 2])
        slot_gate = sb("slot_gate", [128, 2])
        flag_f = sb("flag_f", [128, 1])
        flag = sb("flag", [128, 1], mybir.dt.int32)
        stats = sb("stats", [128, 2, 2, 6])
        moments = sb("moments", [128, 2, 4])
        early = sb("early", [128, 64])
        bias_dram = nc.dram_tensor("bias_dram", (8, 512), F32).ap()

        PERM_R, PERM_A, CENTER, IDENT, ONES_D, ONES_HEAD, ONES_HALF, AFTER, ALL_ONES, FLIP = range(10)
        banks = ctx.enter_context(nc.psum_tensor("banks", [128, 8, 512], F32))
        lin = [banks[:, i, :] for i in range(2)]
        ps = [banks[:, 2 + i, :] for i in range(6)]

        def flat(t):
            return t[:, :, :].rearrange("p a n -> p (a n)")
        ROW = D
        tok_hi, tok_lo = flat(f_hi)[:, 0:2 * ROW], flat(f_lo)[:, 0:2 * ROW]
        out_hi, out_lo = flat(f_hi)[:, 2 * ROW:3 * ROW], flat(f_lo)[:, 2 * ROW:3 * ROW]
        PAIR = 2 * 128
        sel = [flat(t)[:, 4 * ROW:4 * ROW + PAIR] for t in (f_hi, f_lo)]
        sel_t = [flat(t)[:, 2 * ROW:2 * ROW + 128] for t in (x_hi, x_lo)]
        cmp = flat(head_sq)[:, 0:256].rearrange("p (t c m) -> p t c m", t=2, c=2)
        slot_none = flat(head_rstd)[0:1, 0:512]
        lane = flat(head_y)[:, 0:2 + SEQ]
        slot_row = flat(x_hi)[0:EXPERTS, 0:SEQ]
        pick = flat(x_lo)[0:EXPERTS, 0:EXPERTS]
        slot_x_hi = flat(x_hi)[:, 0:2 * ROW].rearrange("p (k n) -> p k n", k=KT)
        slot_x_lo = flat(x_lo)[:, 0:2 * ROW].rearrange("p (k n) -> p k n", k=KT)
        slot_h_hi = flat(f_hi)[:, 3 * ROW:4 * ROW].rearrange("p (k n) -> p k n", k=KT)
        slot_h_lo = flat(f_lo)[:, 3 * ROW:4 * ROW].rearrange("p (k n) -> p k n", k=KT)
        raw_x = [raw[:, i, :, :].rearrange("p k m -> p (k m)") for i in range(SLOTS)]
        raw_x += [flat(h)[:, i * ROW:(i + 1) * ROW] for i in range(RAW - SLOTS)]
        silu_row, hid_row = probs[:, 0:ROW], probs[:, ROW:2 * ROW]
        res_row = flat(wide)[:, 0:2 * ROW]
        gain_rows = flat(gates)[:, 2 * KT * TOK:2 * KT * TOK + 2 * ROW]
        two_banks = [banks[:, 2 * i:2 * i + 2, :].rearrange("p a n -> p (a n)") for i in range(2)]
        sum_bank = banks[:, 4:8, :].rearrange("p a n -> p (a n)")

        landed = [sem(f"landed{i}") for i in range(SLOTS)]
        landed_x = [sem(f"landed_x{i}") for i in range(RAW)]
        hi_ready = sem("hi_ready")
        split_ready = sem("split_ready")
        chunk_done = sem("chunk_done")
        acc_free = [sem("acc_free0"), sem("acc_free1")]
        consts, later_consts = sem("consts"), sem("later_consts")
        h_in_s = sem("h_in_s")
        bias_s = sem("bias_s")
        brow_s = sem("brow_s")
        bias_stored = sem("bias_stored")
        bmm_s = sem("bmm_s")
        lay_ready = sem("lay_ready")
        set_up = sem("set_up")
        rate_ready = sem("rate_ready")
        norm_sq, norm_sum, norm_bc, norm_rstd = sem("norm_sq"), sem("norm_sum"), sem("norm_bc"), sem("norm_rstd")
        h_ready = sem("h_ready")
        u_ready, u_hi, u_lo = sem("u_ready"), sem("u_hi"), sem("u_lo")
        gates_ready = sem("gates_ready")
        ret_raw, perm_done, ret_rot = sem("ret_raw"), sem("perm_done"), sem("ret_rot")
        v_turned, v_ready = sem("v_turned"), sem("v_ready")
        decay_arg, decay_ready = sem("decay_arg"), sem("decay_ready")
        scores, decayed = sem("scores"), sem("decayed")
        head_out, squared, var_done, head_rs = sem("head_out"), sem("squared"), sem("var_done"), sem("head_rs")
        y_ready, y_hi, y_lo = sem("y_ready"), sem("y_hi"), sem("y_lo")
        a_perm, a_rot, a_vt, a_v = sem("a_perm"), sem("a_rot"), sem("a_vt"), sem("a_v")
        a_stage, a_qperm, a_qrot = sem("a_stage"), sem("a_qperm"), sem("a_qrot")
        a_scores, a_max, a_exp, a_prob, a_pt, a_ptc, a_o, a_hi, a_lo = [
            sem("a_" + n) for n in ("scores", "max", "exp", "prob", "pt", "ptc", "o", "hi", "lo")]
        m_ready, m_hi, m_lo = sem("m_ready"), sem("m_hi"), sem("m_lo")
        mix_ready = sem("mix_ready")
        f_act, f_hi_s, f_lo_s = sem("f_act"), sem("f_hi_s"), sem("f_lo_s")
        s_stage, s_vt, s_v, s_z = sem("s_stage"), sem("s_vt"), sem("s_v"), sem("s_z")
        s_abs, s_log, s_L, s_btw, s_arg, s_a, s_am = [sem("s_" + n) for n in ("abs", "log", "L", "btw", "arg", "a", "am")]
        s_o, s_sq, s_var, s_rs, s_y, s_hi, s_lo = [sem("s_" + n) for n in ("o", "sq", "var", "rs", "y", "hi", "lo")]
        d_S, d_max, d_exp, d_prob, d_pt, d_ptc = [sem("d_" + n) for n in ("S", "max", "exp", "prob", "pt", "ptc")]
        qkv_ready = sem("qkv_ready")
        r_ready = sem("r_ready")
        ln_s1, ln_mean, ln_c, ln_sq, ln_var, ln_rs, ln_out = [
            sem("ln_" + n) for n in ("s1", "mean", "c", "sq", "var", "rs", "out")]
        x1_hi, x1_lo = sem("x1_hi"), sem("x1_lo")
        logit_s, rt_max, rt_exp, rt_gate, rt_t, rt_row, rt_bc, rt_all = [
            sem("rt_" + n) for n in ("logit", "max", "exp", "gate", "t", "row", "bc", "all")]
        slots_mm, slots_ready, flag_ready = sem("slots_mm"), sem("slots_ready"), sem("flag_ready")
        tok_turned, tok_split, sum_open = sem("tok_turned"), sem("tok_split"), sem("sum_open")
        tok_hi_s = sem("tok_hi_s")
        sel_ready = sem("sel_ready")
        gathered = sem("gathered")
        x_got = sem("x_got")
        slot_gate_mm, slot_gate_s = sem("slot_gate_mm"), sem("slot_gate_s")
        silu_done, hid_done, hid_turned = sem("silu_done"), sem("hid_done"), sem("hid_turned")
        hid_hi, hid_lo = sem("hid_hi"), sem("hid_lo")
        gated_hi = sem("gated_hi")
        gated_lo = sem("gated_lo")
        scattered = sem("scattered")
        cleared = sem("cleared")
        sum_done = sem("sum_done")
        rows_s = sem("rows_s")
        lane_s = sem("lane_s")
        var_ready, fin_rstd = sem("var_ready"), sem("fin_rstd")
        y_half = sem("y_half")
        out_s = sem("out_s")

        FIRST = ((par, layer_par), (sq, squares), (bmap, bias_map), (badd, bias_add), (relb, rel_bias))
        LATER = ((rope_t, rope), (dist, toeplitz), (mask, att_mask), (par2, second_par), (tri, stick),
                 (wr, w_router), (early, tie_order))
        TURNS, TAKES = (17, 19, 21, 22), (18, 20, 22, 23)
        block = ctx.enter_context(nc.Block())

        def at(t, i, n=TOK, p=slice(0, 128), c0=0):
            if type(i) is int:
                return t[p, i, c0:c0 + n]
            return t[p, bass.ds(i, 1), c0:c0 + n].rearrange("p a n -> p (a n)")

        def col(t, i):
            return t[:, bass.ds(i, 1)] if type(i) is not int else t[:, i:i + 1]

        @block.sync
        def _(sp):
            sp.dma_start(h[:, :, :], h_in).then_inc(h_in_s, 16)
            def load(pairs, done):
                for dst, src in pairs:
                    sp.dma_start(dst[tuple(slice(None) for _ in dst.shape)], src).then_inc(done, 16)

            def load_chunk(g, s):
                sp.wait_ge(split_ready, g * SLOTS + (s + 1))
                src = weights[g * SLOTS + s] if type(g) is int else \
                    weights[bass.ds(g * SLOTS + s, 1)].rearrange("a p m -> p (a m)")
                sp.dma_start(raw[:, s, :, :].rearrange("p k m -> p (k m)"), src).then_inc(landed[s], 16)

            load(FIRST, consts)
            for s in range(SLOTS):
                load_chunk(0, s)
            load(LATER, later_consts)
            with sp.Fori(0, G_EXP - 1) as g:
                for s in range(SLOTS):
                    load_chunk(g + 1, s)
            first = G_EXP * SLOTS
            for i in range(RAW):
                if i < SLOTS:
                    sp.wait_ge(split_ready, first + i + 1)
                else:
                    sp.wait_ge(tok_turned, 1)
                done = landed[i] if i < AHEAD else landed_x[i]
                sp.dma_start(raw_x[i], weights[first + i]).then_inc(done, 16)
                if i < AHEAD:
                    sp.sem_inc(landed_x[i], 16)

            def stream(p):
                with sp.Fori(0, (G_END - G_EXP) * SLOTS // RAW) as g:
                    for i in range(RAW):
                        sp.wait_ge(split_ready, g * RAW + (first + p * (G_END - G_EXP) * SLOTS + i + SLOTS + 1))
                        sp.dma_start(raw_x[i], weights[bass.ds(g * RAW + (first + RAW + i), 1)]
                                     .rearrange("a p m -> p (a m)")).then_inc(landed_x[i], 16)

            stream(0)
            sp.wait_ge(flag_ready, 1)
            crowded = sp.value_load(flag[0:1, 0:1], min_val=0, max_val=1)
            with sp.If(crowded > 0):
                stream(1)
            for t in range(2):
                sp.wait_ge(y_half, t + 1)
                sp.dma_start(out[t], res_row[:, t * ROW:(t + 1) * ROW]).then_inc(out_s, 16)
            sp.wait_ge(out_s, 32)

        @block.gpsimd
        def _(pool):
            pool.wait_ge(brow_s, 1)
            pool.dma_start(bias_dram, brow[:, :]).then_inc(bias_stored, 16)
            pool.wait_ge(bias_stored, 16)
            pool.wait_ge(mix_ready, LAYERS * KT)
            for first, start, n in ((0, 128, 128), (128, 0, 256)):
                src = bass.AP(bias_dram.tensor, start, [[1, 128], [512, 8], [1, n]])
                pool.dma_start(head_bias[:, :, first:first + n], src).then_inc(bias_s, 16)
            pool.wait_ge(ln_s1, 1)
            for r in range(2):
                pool.dma_start(gain_rows[:, r * ROW:(r + 1) * ROW],
                               bass.AP(ln_rows.tensor, r * ROW, [[0, 128], [1, ROW]])).then_inc(rows_s, 16)
            pool.dma_start(lane, lanes).then_inc(lane_s, 16)

        @block.tensor
        def _(pe):
            def chunk_mm(g, s, bank, rhs, kts, n, first=True, last=True, lhs_k=0, done=True, split_k=None):
                hi, lo = rhs
                steps = len(kts)
                for i, k in enumerate(kts):
                    if split_k is not None:
                        pe.wait_ge(split_k[0], split_k[1] + (k + 1))
                    pe.matmul(lin[bank][:, 0:n], w_lo[:, s, lhs_k + i, :], hi[:, k, 0:n],
                              start=first and i == 0, stop=False)
                    pe.matmul(lin[bank][:, 0:n], w_hi[:, s, lhs_k + i, :], lo[:, k, 0:n],
                              start=False, stop=False)
                    mm = pe.matmul(lin[bank][:, 0:n], w_hi[:, s, lhs_k + i, :], hi[:, k, 0:n],
                                   start=False, stop=last and i == steps - 1)
                if done:
                    mm.then_inc(chunk_done, 1)
                return mm

            def chunk(g, s, bank, a, rhs, kts, n, first=True, last=True, split_k=None):
                pe.wait_ge(split_ready, g * SLOTS + (s + 1 + SLOTS))
                if first:
                    pe.wait_ge(acc_free[bank], a + 1)
                chunk_mm(g, s, bank, rhs, kts, n, first, last, split_k=split_k)

            def group(g, a, rhs, n, split_k=None):
                for s in range(SLOTS):
                    chunk(g, s, s % 2, a + s // 2, rhs, range(KT), n, split_k=split_k if s == 0 else None)

            def pre_norm(l, which):
                for k in range(KT):
                    pe.wait_ge(norm_sq, (l * 2 + which) * KT + (k + 1))
                    mm = pe.matmul(ps[0][:, 0:TOK], sq[:, ONES_D, :], wide[:, k, :], start=k == 0, stop=k == KT - 1)
                mm.then_inc(norm_bc, 1)

            def post_norm(l, which):
                pe.wait_ge(norm_sum, l * 2 + (which + 1))
                pe.matmul(ps[0][:, 0:TOK], sq[:, ONES_D, :], row_sum[:, 0:TOK], start=True, stop=True)\
                    .then_inc(norm_bc, 1)

            X = (x_hi, x_lo)
            FF = (f_hi, f_lo)

            pe.sem_inc(chunk_done, SLOTS)
            pe.wait_ge(consts, 16 * len(FIRST))
            pe.matmul(ps[5][0:8, :], relb[:, :], bmap[:, :], start=True, stop=True).then_inc(bmm_s, 1)

            with pe.Fori(0, LAYERS) as l:
                G = l * G_LAYER
                A = l * A_LAYER
                pre_norm(l, 0)
                with pe.Fori(0, 2) as i:
                    group(G + G_GATE + i, A + A_GATE + i * 2, X, TOK, (u_lo, l * 2 * KT))
                with pe.Fori(0, 4) as i:
                    group(G + G_SIG + i, A + A_SIG + i * 2, X, TOK)
                group(G + G_RET, A + A_RET, X, TOK)
                with pe.Fori(0, PAIRS) as i:
                    u = l * PAIRS + i
                    raw_at = (l * (PAIRS + 1) + i) * SLOTS

                    def next_chunk(s):
                        chunk(G + (G_RET + 1) + i, s, s % 2, A + A_RET + i * 2 + (2 + s // 2), X, range(KT), TOK)

                    pe.wait_ge(y_ready, u * 2 + 2)
                    for j in range(2):
                        pe.wait_ge(ret_raw, raw_at + (j + 1))
                        pe.matmul(ps[j][:, 0:TOK], sq[:, PERM_R, :], raw_qk[:, j, :],
                                  start=True, stop=True).then_inc(perm_done, 1)
                    for j in range(2):
                        pe.wait_ge(ret_raw, raw_at + (j + 3))
                        for t, (t0, tn) in enumerate(TILES):
                            mm = pe.matmul(ps[2 + j][0:tn, t * 128:(t + 1) * 128], raw_v[:, j, t0:t0 + tn],
                                           sq[:, CENTER, :], start=True, stop=True)
                        mm.then_inc(v_turned, 1)
                    next_chunk(0)
                    pe.wait_ge(ret_rot, u * 2 + 2)
                    bank = [[0, 1, 4], [5, 2, 3]]
                    for j in range(2):
                        p = slice(64 * j, 64 * j + 64)
                        if j == 1:
                            pe.wait_ge(v_ready, u * 2 + 2)
                        for t, (t0, tn) in enumerate(TILES):
                            mm = pe.matmul(ps[bank[j][t]][0:tn, 0:TOK], k_rot[p, t0:t0 + tn], q_rot[p, :],
                                           start=True, stop=True)
                        mm.then_inc(scores, 1)
                    next_chunk(1)
                    for j in range(2):
                        pe.wait_ge(decayed, u * 2 + j + 1)
                        for t, (t0, tn) in enumerate(TILES):
                            mm = pe.matmul(ps[bank[j][0]][:, 0:TOK], v_tok[0:tn, j, t, :], prob_t[0:tn, j, t, :],
                                           start=t == 0, stop=t == 2)
                        mm.then_inc(head_out, 1)
                    next_chunk(2)
                    for j in range(2):
                        pe.wait_ge(squared, u * 2 + j + 1)
                        pe.matmul(ps[bank[j][1]][:, 0:TOK], sq[:, ONES_HEAD, :], head_sq[:, j, :],
                                  start=True, stop=True).then_inc(var_done, 1)
                    next_chunk(3)
                for s in range(2):
                    chunk(G + G_ATT + 1, s, s % 2, A + A_ATT + 2, X, range(KT), TOK)
                for s in range(2, SLOTS):
                    pe.drain()
                    pe.wait_ge(split_ready, (G + G_ATT + 1) * SLOTS + (s + 1 + SLOTS))
                    pe.sem_inc(chunk_done, 1)
                pe.wait_ge(ret_raw, (l + 1) * (PAIRS + 1) * SLOTS - 2)
                pe.matmul(ps[0][:, 0:TOK], sq[:, PERM_A, :], raw_qk[:, 1, :], start=True, stop=True)\
                    .then_inc(a_perm, 1)
                pe.wait_ge(ret_raw, (l + 1) * (PAIRS + 1) * SLOTS - 1)
                for t, (t0, tn) in enumerate(TILES):
                    mm = pe.matmul(ps[2][0:tn, t * 128:(t + 1) * 128], raw_v[:, 0, t0:t0 + tn],
                                   sq[:, IDENT, :], start=True, stop=True)
                mm.then_inc(a_vt, 1)

                def turn_q(n):
                    pe.matmul(ps[1][:, 0:TOK], sq[:, PERM_A, :], at(q_att, n), start=True, stop=True)\
                        .then_inc(a_qperm, 1)

                pe.wait_ge(a_stage, l + 1)
                turn_q(0)

                def reto_chunk(i, s):
                    pe.wait_ge(y_lo, (l + 1) * 2 * PAIRS)
                    chunk(G + G_RETO + i, s, s % 2, A + A_RETO + i * 2 + s // 2, FF, range(KT), TOK)

                with pe.Fori(0, PAIRS // 2) as i:
                    for q in range(2):
                        u = l * PAIRS + i * 2 + q
                        pe.wait_ge(a_rot, l + 1)
                        pe.wait_ge(a_v, l + 1)
                        pe.wait_ge(a_qrot, u + (l + 1))
                        for j in range(2):
                            p = slice(64 * j, 64 * j + 64)
                            pe.wait_ge(a_lo, u * 2 + (j + 1))
                            for t, (t0, tn) in enumerate(TILES):
                                mm = pe.matmul(ps[3 * j + t][0:tn, 0:TOK], q_rot[p, t0:t0 + tn], k_rot[p, :],
                                               start=True, stop=True)
                            mm.then_inc(a_scores, 1)
                        reto_chunk(i, 2 * q)
                        for j in range(2):
                            pe.wait_ge(a_prob, u * 2 + j + 1)
                            for k, (k0, kn) in enumerate(TILES):
                                for t, (t0, tn) in enumerate(TILES):
                                    mm = pe.transpose(ps[3 * j + k][0:kn, t0:t0 + tn], prob[0:tn, j, t, k0:k0 + kn],
                                                      sq[0:tn, IDENT, 0:tn])
                            mm.then_inc(a_pt, 1)
                        reto_chunk(i, 2 * q + 1)
                        pe.wait_ge(a_ptc, u * 2 + 1)
                        turn_q(i * 2 + (q + 1))
                        for j in range(2):
                            p = slice(64 * j, 64 * j + 64)
                            pe.wait_ge(a_ptc, u * 2 + j + 1)
                            for k, (k0, kn) in enumerate(TILES):
                                mm = pe.matmul(ps[3 * j][p, 0:TOK], v_tok[0:kn, 0, k, p], prob_t[0:kn, j, k, :],
                                               start=k == 0, stop=k == 2)
                            mm.then_inc(a_o, 1)
                pe.wait_ge(a_lo, (l + 1) * 2 * PAIRS + 2)
                for s in range(SLOTS):
                    pe.wait_ge(split_ready, (G + G_ATTO) * SLOTS + (s + 1 + SLOTS))
                    for b in range(2):
                        pe.wait_ge(acc_free[b], A + A_ATTO + s + 1)
                        chunk_mm(0, s, b, FF, range(8, 12), TOK, lhs_k=4 * b, done=b == 1)
                with pe.Fori(0, 2) as i:
                    group(G + G_MIX + i, A + A_MIX + i * 2, X, TOK, (m_lo, l * KT))
                post_norm(l, 0)
                pre_norm(l, 1)
                with pe.Fori(0, FF_HALVES) as f:
                    with pe.Fori(0, 4) as i:
                        group(G + G_FF + f * G_HALF + i, A + A_FF + f * A_HALF + i * 2, X, TOK,
                              (u_lo, (l * 2 + 1) * KT))
                    with pe.Fori(0, 4) as i:
                        for s in range(SLOTS):
                            chunk(G + G_FF + 4 + f * G_HALF + i, s, s // 2, A + A_FF + 8 + f * A_HALF + i, FF,
                                  range(KT * (s % 2), KT * (s % 2) + KT), TOK, first=s % 2 == 0, last=s % 2 == 1,
                                  split_k=(f_lo_s, (l * FF_HALVES + f) * FF_BLOCKS) if s < 2 else None)
                post_norm(l, 1)

            with pe.Fori(0, 6) as i:
                group(i + G_QKV, i * 2 + A_QKV, X, SEQ, (x1_lo, 0))

            def stage_values(u, kind):
                pe.wait_ge(s_stage, u * 2 + (kind + 1))
                for t in range(2):
                    mm = pe.matmul(ps[2 + kind][:, t * 128:(t + 1) * 128],
                                   raw_v[:, kind, t * 128:(t + 1) * 128], sq[:, IDENT, :], start=True, stop=True)
                mm.then_inc(s_vt, 1)

            def head_output(u, kind, ready, weights_t):
                pe.wait_ge(s_v, u * 2 + (kind + 1))
                for j in range(2):
                    p = slice(64 * j, 64 * j + 64)
                    pe.wait_ge(ready, u * 2 + (j + 1))
                    pe.matmul(ps[4 - kind][p, 0:SEQ], v_tok[:, kind, 0, p], weights_t[:, j, 0:SEQ],
                              start=True, stop=False)
                    mm = pe.matmul(ps[4 - kind][p, 128:SEQ], v_tok[:, kind, 1, p], weights_t[:, j, SEQ:384],
                                   start=False, stop=True)
                mm.then_inc(s_o, 1)

            with pe.Fori(0, PAIRS) as u:
                for kind in range(2):
                    stage_values(u, kind)
                for j in range(2):
                    p = slice(64 * j, 64 * j + 64)
                    q, k = staged_q[0], staged_k[0]
                    pe.matmul(ps[j][:, 0:SEQ], k[p, 0:128], q[p, 0:SEQ], start=True, stop=True)
                    pe.matmul(ps[j][:, SEQ:384], k[p, 128:SEQ], q[p, 128:SEQ], start=True, stop=True)\
                        .then_inc(s_z, 1)
                for j in range(2):
                    p = slice(64 * j, 64 * j + 64)
                    q, k = staged_q[1], staged_k[1]
                    pe.wait_ge(bias_s, 32)
                    pe.matmul(lin[j][:, 0:384], sq[:, FLIP, :], at(head_bias, u * 2 + j, 384),
                              start=True, stop=False)
                    pe.matmul(lin[j][:, 0:128], q[p, 0:128], k[p, 0:128], start=False, stop=False)
                    pe.matmul(lin[j][:, 128:384], q[p, 128:SEQ], k[p, 0:SEQ], start=False, stop=True)\
                        .then_inc(d_S, 1)
                for j in range(2):
                    pe.wait_ge(s_L, u * 2 + j + 1)
                    L = log_rest[:, j, :]
                    pe.matmul(ps[j][:, 0:SEQ], sq[:, AFTER, :], L[:, 0:SEQ], start=True, stop=False)
                    pe.matmul(ps[j][:, 128:SEQ], sq[:, ALL_ONES, :], L[:, SEQ:384], start=False, stop=True)
                    pe.matmul(ps[j][:, SEQ:384], sq[:, AFTER, :], L[:, SEQ:384], start=True, stop=True)\
                        .then_inc(s_btw, 1)
                for j in range(2):
                    pe.wait_ge(d_prob, u * 2 + j + 1)
                    P = dil_flat[:, j, :]
                    pe.transpose(lin[j][:, 0:128], P[:, 0:128], sq[:, IDENT, :])
                    pe.transpose(lin[j][:, 128:256], P[:, 128:256], sq[:, IDENT, :])
                    pe.transpose(lin[j][:, 256:384], P[:, 256:384], sq[:, IDENT, :]).then_inc(d_pt, 1)
                head_output(u, 0, s_am, prob_tf)
                head_output(u, 1, d_ptc, dil_tf)
                for kind in range(2):
                    pe.wait_ge(s_sq, u * 2 + (kind + 1))
                    pe.matmul(ps[5 - 3 * kind][:, 0:SEQ], sq[:, ONES_HALF, :], head_sq[:, kind, 0:SEQ],
                              start=True, stop=True).then_inc(s_var, 1)

            pe.wait_ge(s_lo, 2 * PAIRS)
            with pe.Fori(0, 2) as i:
                group(i + G_OUT, i * 2 + A_OUT, X, SEQ)

            pe.wait_ge(ln_s1, 1)
            pe.matmul(ps[0][:, 0:SEQ], sq[:, ONES_D, :], row_sum[:, 0:SEQ], start=True, stop=True)\
                .then_inc(ln_mean, 1)
            for k in range(KT):
                pe.wait_ge(ln_sq, k + 1)
                mm = pe.matmul(ps[1][:, 0:SEQ], sq[:, ONES_D, :], gates[:, k, 0:SEQ], start=k == 0, stop=k == KT - 1)
            mm.then_inc(ln_var, 1)
            pe.wait_ge(later_consts, 16 * len(LATER))
            for k in range(KT):
                pe.wait_ge(ln_out, k + 1)
                for t in range(2):
                    mm = pe.matmul(ps[t][:, 0:16], h[:, k, t * 128:(t + 1) * 128], wr[:, k, :],
                                   start=k == 0, stop=k == KT - 1)
            mm.then_inc(logit_s, 1)
            for t in range(2):
                for k in range(KT):
                    mm = pe.transpose(sum_bank[:, t * ROW + k * 128:t * ROW + (k + 1) * 128],
                                      h[:, k, t * 128:(t + 1) * 128], sq[:, IDENT, :])
            mm.then_inc(tok_turned, 1)
            pe.wait_ge(rt_gate, 1)
            before = tri[:, 0, 0:128]
            pe.matmul(ps[1][:, 0:16], before, rt[:, 0, 12, :], start=True, stop=True)
            pe.matmul(ps[1][:, 16:32], before, rt[:, 1, 12, :], start=True, stop=False)
            pe.matmul(ps[1][:, 16:32], sq[:, ALL_ONES, :], rt[:, 0, 12, :], start=False, stop=True)
            pe.matmul(ps[1][:, 32:48], sq[:, ALL_ONES, :], rt[:, 0, 12, :], start=True, stop=False)
            pe.matmul(ps[1][:, 32:48], sq[:, ALL_ONES, :], rt[:, 1, 12, :], start=False, stop=True)\
                .then_inc(slots_mm, 1)
            pe.wait_ge(slots_ready, 1)
            for t in range(2):
                mm = pe.transpose(ps[1][0:EXPERTS, t * 128:(t + 1) * 128], slot_of[:, t, 0:EXPERTS], sq[:, IDENT, :])
            mm.then_inc(rt_t, 1)
            pe.wait_ge(rt_row, 1)
            for b in range(EXPERTS // 2):
                if b >= 2:
                    pe.wait_ge(rt_all, b - 1)
                for e in (2 * b, 2 * b + 1):
                    mm = pe.matmul(lin[b % 2][:, SEQ * (e % 2):SEQ * (e % 2) + SEQ],
                                   pick[:, e:e + 1].broadcast_to((EXPERTS, 128)), slot_row, start=True, stop=True)
                mm.then_inc(rt_bc, 1)
            pe.wait_ge(rt_all, EXPERTS // 2)
            pe.wait_ge(tok_split, 1)
            for b in range(4):
                mm = pe.matmul(banks[:, 4 + b, :], sq[:, IDENT, :], res_row[:, b * 512:(b + 1) * 512],
                               start=True, stop=False, skip_group_check=True)
            mm.then_inc(sum_open, 1)

            def gather(j):
                src = (tok_hi, tok_lo)[j // 2]
                for i in range(KT // 2):
                    k = i + KT // 2 * (j % 2)
                    for t in range(2):
                        mm = pe.matmul(two_banks[0][:, i * PAIR:(i + 1) * PAIR],
                                       src[:, t * ROW + k * 128:t * ROW + (k + 1) * 128], sel[t],
                                       start=t == 0, stop=t == 1)
                mm.then_inc(gathered, 1)

            def scatter():
                for t in range(2):
                    for src in (out_lo, out_hi):
                        for b in range(2):
                            mm = pe.matmul(banks[:, 4 + 2 * t + b, :], sel_t[t],
                                           src[:, b * 512:(b + 1) * 512], start=False, stop=False,
                                           skip_group_check=True)
                mm.then_inc(scattered, 1)

            def experts(p):
                base = G_EXP + p * (G_END - G_EXP)
                pe.wait_ge(sel_ready, 9 * p + 1)
                for j in range(4):
                    if j > 0:
                        pe.wait_ge(x_got, 36 * p + j)
                    gather(j)
                with pe.Fori(0, EXPERTS // 2) as pair:
                    for q in range(2):
                        E = pair * 2 + (q + EXPERTS * p)

                        def rows(n, hi, lo, x0, dst):
                            s, k = n % SLOTS, n % KT
                            pe.wait_ge(split_ready,
                                       (pair * 12 + (base + 6 * q + n // SLOTS)) * SLOTS + (s + 1 + SLOTS))
                            wh, wl = [w[:, s, :, :].rearrange("p k m -> p (k m)") for w in (w_hi, w_lo)]
                            steps = [(lo, wh), (hi, wl), (hi, wh)]
                            for i, (x, w) in enumerate(steps):
                                for b in range(2):
                                    mm = pe.matmul(banks[:, 2 * dst + b, :], x[:, k, x0:x0 + 128],
                                                   w[:, b * 512:(b + 1) * 512],
                                                   start=k == 0 and i == 0, stop=k == KT - 1 and i == 2)
                            mm.then_inc(chunk_done, 1)

                        if q == 0:
                            pe.wait_ge(x_got, (pair + 9 * p) * 4 + 4)
                        for n in range(0, 8):
                            rows(n, slot_x_hi, slot_x_lo, 128 * q, q)
                        pe.wait_ge(gated_lo, E + 1)
                        for n in range(8, 16):
                            rows(n, slot_x_hi, slot_x_lo, 128 * q, 1 - q)
                        scatter()
                        if q == 0:
                            pe.wait_ge(silu_done, E + 1)
                            for i in range(2):
                                for t in range(2):
                                    mm = pe.matmul(banks[:, 0, i:i + 1],
                                                   sel[t][:, 128 * i:128 * i + 128].bitcast(F32),
                                                   col(rt[:, t, 11, :], pair * 2 + i), start=t == 0, stop=t == 1)
                            mm.then_inc(slot_gate_mm, 1)
                        for half in range(2):
                            pe.wait_ge(hid_done, E * 2 + (half + 1))
                            for k in range(4 * half, 4 * half + 4):
                                mm = pe.transpose(two_banks[1 - q][:, k * 128:(k + 1) * 128],
                                                  hid_row[:, k * 128:(k + 1) * 128], sq[:, IDENT, :])
                            mm.then_inc(hid_turned, 1)
                        for n in range(16, 24):
                            if n == 16 and q == 0:
                                pe.wait_ge(slot_gate_s, pair + (EXPERTS // 2 * p + 1))
                            if n in (16, 20):
                                pe.wait_ge(hid_lo, E * 2 + (1 if n == 16 else 2))
                            rows(n, slot_h_hi, slot_h_lo, 0, q)
                            if q == 1 and n in TURNS:
                                j = TURNS.index(n)
                                if j == 0:
                                    pe.wait_ge(hid_lo, E * 2 + 2)
                                    pe.wait_ge(sel_ready, pair + (9 * p + 2))
                                else:
                                    pe.wait_ge(x_got, (pair + (9 * p + 1)) * 4 + j)
                                gather(j)
                pe.wait_ge(gated_lo, EXPERTS * (p + 1) + 1)
                scatter()

            experts(0)
            pe.wait_ge(flag_ready, 1)
            crowded = pe.value_load(flag[0:1, 0:1], min_val=0, max_val=1)
            with pe.If(crowded > 0):
                pe.wait_ge(cleared, 1)
                experts(1)
            for b in range(4):
                mm = pe.matmul(banks[:, 4 + b, :], slot_none[0:1, 0:128], slot_none[0:1, 0:512],
                               start=False, stop=True, skip_group_check=True)
            mm.then_inc(sum_done, 1)

        @block.scalar
        def _(act):
            A_ = nc.scalar.activation

            def split(g, s):
                act.wait_ge(landed[s], (g + 1) * 16)
                act.wait_ge(chunk_done, g * SLOTS + (s + 1))
                A_(w_hi[:, s, :, :], raw[:, s, :, :], ACT.Copy).then_inc(hi_ready, 1)

            def ahead(g, s):
                split(g + (s + AHEAD) // SLOTS, (s + AHEAD) % SLOTS)

            def product(g, s):
                act.wait_ge(chunk_done, g * SLOTS + (s + 1 + SLOTS))

            def power_half(dst, src, scale, bias):
                A_(dst, src, ACT.Ln, scale=scale, bias=bias)
                act.drain()
                return A_(dst, dst, ACT.Exp, scale=-0.5)

            def evac(g, s, dst, func=ACT.Copy, scale=1.0):
                product(g, s)
                return A_(dst, lin[s % 2][:, 0:TOK], func, scale=scale)

            def squares(w):
                for k in range(KT):
                    act.wait_ge(h_ready, w * KT + (k + 1))
                    A_(wide[:, k, :], h[:, k, :], ACT.Square).then_inc(norm_sq, 1)

            act.wait_ge(set_up, 1)
            for s in range(AHEAD):
                split(0, s)

            with act.Fori(0, LAYERS) as l:
                G = l * G_LAYER
                load_exp_ln(nc, act)
                act.wait_ge(lay_ready, l + 1)
                A_(decay_rate[:, :], lay[:, C_DECAY:C_DECAY + 16], ACT.Exp).then_inc(rate_ready, 1)
                squares(l * 2)
                act.wait_ge(norm_bc, l * 4 + 1)
                power_half(rstd[:, :], ps[0][:, 0:TOK], 1.0, eps[:, 0:1]).then_inc(norm_rstd, 1)
                for k in range(KT):
                    act.wait_ge(u_ready, (l * 2) * KT + k + 1)
                    A_(x_hi[:, k, :], wide[:, k, :], ACT.Copy).then_inc(u_hi, 1)
                with act.Fori(0, 2) as i:
                    for s in range(SLOTS):
                        ahead(G + G_GATE + i, s)
                        evac(G + G_GATE + i, s, at(gates, i * 4 + s), ACT.Silu).then_inc(acc_free[s % 2], 1)
                act.wait_ge(bias_stored, 16)
                with act.Fori(0, 4) as i:
                    for s in range(SLOTS):
                        ahead(G + G_SIG + i, s)
                        evac(G + G_SIG + i, s, at(gates, i * 4 + (s + KT)), ACT.Sigmoid).then_inc(acc_free[s % 2], 1)
                act.drain().then_inc(gates_ready, 1)
                load_exp_ln(nc, act)
                def take(g, s):
                    product(g, s)
                    dst = raw_qk[:, s, :] if s < 2 else raw_v[:, s - 2, :]
                    A_(dst, lin[s % 2][:, 0:TOK], ACT.Copy).then_inc(ret_raw, 1)
                    act.drain().then_inc(acc_free[s % 2], 1)

                for s in range(SLOTS):
                    ahead(G + G_RET, s)
                    take(G + G_RET, s)
                with act.Fori(0, PAIRS) as i:
                    u = l * PAIRS + i
                    g = G + (G_RET + 1) + i
                    for j in range(2):
                        act.wait_ge(v_turned, u * 2 + j + 1)
                        A_(v_tok[:, j, 0:2, :], ps[2 + j][:, 0:256].rearrange("p (t n) -> p t n", t=2), ACT.Copy)
                        A_(v_tok[0:16, j, 2, :], ps[2 + j][0:16, 256:384], ACT.Copy).then_inc(v_ready, 1)
                    ahead(g, 0)
                    for j in range(2):
                        act.wait_ge(decay_arg, u * 2 + j + 1)
                        A_(decay[:, j, :], decay[:, j, :], ACT.Exp, scale=-1.0).then_inc(decay_ready, 1)
                    for s in range(2):
                        if s > 0:
                            ahead(g, s)
                        act.wait_ge(ret_rot, u * 2 + (s + 1))
                        take(g, s)
                    for j in range(2):
                        act.wait_ge(head_out, u * 2 + j + 1)
                        A_(head_sq[:, j, :], ps[(0, 5)[j]][:, 0:TOK], ACT.Square).then_inc(squared, 1)
                    ahead(g, 2)
                    take(g, 2)
                    for j in range(2):
                        act.wait_ge(var_done, u * 2 + j + 1)
                        power_half(head_rstd[:, j, :], ps[(1, 2)[j]][:, 0:TOK], 1.0, eps[:, 0:1]).then_inc(head_rs, 1)
                    ahead(g, 3)
                    for j in range(2):
                        act.wait_ge(y_ready, u * 2 + j + 3)
                        A_(at(f_hi, i * 2 + j), head_y[:, j, :], ACT.Copy).then_inc(y_hi, 1)
                    take(g, 3)
                act.drain()
                for n in (0, PAIRS):
                    A_(q_att[:, n, :], raw_qk[:, 0, :], ACT.Copy)
                A_(q_att[:, 1, :], raw_v[:, 1, :], ACT.Copy)
                for s in range(SLOTS):
                    g = G + G_ATT + 1
                    ahead(g, s)
                    if s < 2:
                        product(g, s)
                        A_(q_att[:, s + 2, :], lin[s % 2][:, 0:TOK], ACT.Copy).then_inc(acc_free[s % 2], 1)
                act.drain().then_inc(a_stage, 1)
                act.wait_ge(a_vt, l + 1)
                A_(v_tok[:, 0, 0:2, :], ps[2][:, 0:256].rearrange("p (t n) -> p t n", t=2), ACT.Copy)
                A_(v_tok[0:16, 0, 2, :], ps[2][0:16, 256:384], ACT.Copy).then_inc(a_v, 1)
                with act.Fori(0, PAIRS // 2) as i:
                    for q in range(2):
                        u = l * PAIRS + i * 2 + q
                        for j in range(2):
                            act.wait_ge(a_max, u * 2 + j + 1)
                            for t, (t0, tn) in enumerate(TILES):
                                A_(prob[0:tn, j, t, :], prob[0:tn, j, t, :], ACT.Exp, bias=small[0:tn, j, 1, t:t + 1],
                                   accum_out=small[0:tn, j, 2, t:t + 1])
                            for t, (t0, tn) in enumerate(TILES):
                                mm = A_(small[0:tn, j, 3, t:t + 1], sink_col[0:tn, j:j + 1], ACT.Exp,
                                        bias=small[0:tn, j, 1, t:t + 1])
                            mm.then_inc(a_exp, 1)
                        ahead(G + G_RETO + i, 2 * q)
                        for j in range(2):
                            act.wait_ge(a_pt, u * 2 + j + 1)
                            for k, (k0, kn) in enumerate(TILES):
                                mm = A_(prob_t[0:kn, j, k, :], ps[3 * j + k][0:kn, 0:TOK], ACT.Copy)
                            mm.then_inc(a_ptc, 1)
                        for j in range(2):
                            p = slice(64 * j, 64 * j + 64)
                            act.wait_ge(a_o, u * 2 + j + 1)
                            A_(at(f_hi, i * 2 + (q + 8), p=p), ps[3 * j][p, 0:TOK], ACT.Copy).then_inc(a_hi, 1)
                        ahead(G + G_RETO + i, 2 * q + 1)
                        act.wait_ge(a_lo, u * 2 + 4)
                for s in range(SLOTS):
                    ahead(G + G_ATTO, s)
                    for k in (2 * s, 2 * s + 1):
                        act.wait_ge(m_ready, l * KT + k + 1)
                        A_(x_hi[:, k, :], wide[:, k, :], ACT.Copy).then_inc(m_hi, 1)
                with act.Fori(0, 2) as i:
                    for s in range(SLOTS):
                        ahead(G + G_MIX + i, s)
                        if s == 0:
                            act.wait_ge(m_lo, (l + 1) * KT)
                        evac(G + G_MIX + i, s, at(wide, i * 4 + s)).then_inc(acc_free[s % 2], 1)
                        act.drain().then_inc(mix_ready, 1)
                act.wait_ge(norm_bc, l * 4 + 2)
                power_half(rstd[:, :], ps[0][:, 0:TOK], 1.0, eps[:, 0:1]).then_inc(norm_rstd, 1)
                squares(l * 2 + 1)
                act.wait_ge(norm_bc, l * 4 + 3)
                power_half(rstd[:, :], ps[0][:, 0:TOK], 1.0, eps[:, 0:1]).then_inc(norm_rstd, 1)
                for k in range(KT):
                    act.wait_ge(u_ready, (l * 2 + 1) * KT + k + 1)
                    A_(x_hi[:, k, :], wide[:, k, :], ACT.Copy).then_inc(u_hi, 1)
                with act.Fori(0, FF_HALVES) as f:
                    with act.Fori(0, 4) as i:
                        for s in range(SLOTS):
                            ahead(G + G_FF + f * G_HALF + i, s)
                            act.wait_ge(f_act, (l * FF_HALVES + f) * FF_BLOCKS + i * 4 + (s + 1))
                            A_(at(f_hi, i * 4 + s), head_y[:, s % 2, :], ACT.Copy).then_inc(f_hi_s, 1)
                    with act.Fori(0, 4) as i:
                        for s in range(SLOTS):
                            ahead(G + G_FF + 4 + f * G_HALF + i, s)
                act.wait_ge(norm_bc, l * 4 + 4)
                power_half(rstd[:, :], ps[0][:, 0:TOK], 1.0, eps[:, 0:1]).then_inc(norm_rstd, 1)

            for k in range(KT):
                act.wait_ge(h_ready, 2 * LAYERS * KT + k + 1)
                A_(x_hi[:, k, 0:SEQ], h[:, k, META:TOK], ACT.Copy).then_inc(x1_hi, 1)
            with act.Fori(0, 6) as i:
                for s in range(SLOTS):
                    ahead(i + G_QKV, s)
                    product(i + G_QKV, s)
                    A_(at(gates, i * 4 + s, SEQ), lin[s % 2][:, 0:SEQ], ACT.Copy).then_inc(acc_free[s % 2], 1)
            act.drain()

            with act.Fori(0, PAIRS) as u:
                for kind in range(2):
                    block0 = u * 3 + 12 * kind
                    A_(staged_q[kind][:, 0:SEQ], at(gates, block0, SEQ), ACT.Copy, scale=0.125)
                    A_(staged_k[kind][:, 0:SEQ], at(gates, block0 + 1, SEQ), ACT.Copy)
                    A_(raw_v[:, kind, 0:SEQ], at(gates, block0 + 2, SEQ), ACT.Copy)
                    act.drain().then_inc(s_stage, 1)
                for kind in range(2):
                    act.wait_ge(s_vt, u * 2 + (kind + 1))
                    A_(v_tok[:, kind, 0:2, :], ps[2 + kind][:, 0:SEQ]
                       .rearrange("p (t n) -> p t n", t=2), ACT.Copy).then_inc(s_v, 1)
                for j in range(2):
                    act.wait_ge(s_z, u * 2 + j + 1)
                    A_(prob_flat[:, j, :], ps[j][:, 0:384], ACT.Abs)
                act.drain()
                for j in range(2):
                    A_(prob_flat[:, j, :], prob_flat[:, j, :], ACT.Exp, scale=-1.0)
                act.drain()
                for j in range(2):
                    A_(prob_flat[:, j, :], prob_flat[:, j, :], ACT.Ln, bias=1.0).then_inc(s_log, 1)
                for j in range(2):
                    act.wait_ge(d_max, u * 2 + j + 1)
                    P = dil_flat[:, j, :]
                    A_(P[:, 0:128], lin[j][:, 0:128], ACT.Exp, bias=small[:, j, 1, 0:1], accum_out=small[:, j, 2, 0:1])
                    A_(P[:, 128:384], lin[j][:, 128:384], ACT.Exp, bias=small[:, j, 1, 1:2],
                       accum_out=small[:, j, 2, 1:2]).then_inc(d_exp, 1)
                for j in range(2):
                    act.wait_ge(s_arg, u * 2 + j + 1)
                    A_(prob_tf[:, j, :], prob_flat[:, j, :], ACT.Exp).then_inc(s_a, 1)
                for j in range(2):
                    act.wait_ge(d_pt, u * 2 + j + 1)
                    A_(dil_tf[:, j, :], lin[j][:, 0:384], ACT.Copy).then_inc(d_ptc, 1)
                for kind in range(2):
                    act.wait_ge(s_o, u * 2 + (kind + 1))
                    A_(head_sq[:, kind, 0:SEQ], ps[4 - kind][:, 0:SEQ], ACT.Square).then_inc(s_sq, 1)
                for kind in range(2):
                    act.wait_ge(s_var, u * 2 + (kind + 1))
                    power_half(head_rstd[:, kind, 0:SEQ], ps[5 - 3 * kind][:, 0:SEQ], 1.0, eps[:, 0:1])\
                        .then_inc(s_rs, 1)
                for kind in range(2):
                    act.wait_ge(s_y, u * 2 + (kind + 1))
                    A_(at(x_hi, u + 4 * kind, SEQ), head_y[:, kind, 0:SEQ], ACT.Copy).then_inc(s_hi, 1)
            with act.Fori(0, 2) as i:
                for s in range(SLOTS):
                    ahead(i + G_OUT, s)

            for k in range(KT):
                act.wait_ge(ln_c, k + 1)
                A_(gates[:, k, 0:SEQ], wide[:, k, 0:SEQ], ACT.Square).then_inc(ln_sq, 1)
            act.wait_ge(ln_var, 1)
            power_half(rstd[:, 0:SEQ], ps[1][:, 0:SEQ], 1.0, eps[:, 1:2]).then_inc(ln_rs, 1)
            act.wait_ge(tok_turned, 1)
            A_(tok_hi, sum_bank, ACT.Copy).then_inc(tok_hi_s, 1)
            act.wait_ge(rt_max, 1)
            for t in range(2):
                mm = A_(rt[:, t, 2, :], rt[:, t, 0, :], ACT.Exp, bias=rt[:, t, 1, 0:1], accum_out=rt[:, t, 1, 1:2])
            mm.then_inc(rt_exp, 1)
            for b in range(EXPERTS // 2):
                act.wait_ge(rt_bc, b + 1)
                A_(gates[:, 2 * b:2 * b + 2, 0:SEQ], lin[b % 2].rearrange("p (e n) -> p e n", e=2), ACT.Copy)\
                    .then_inc(rt_all, 1)

            def experts(p):
                base = G_EXP + p * (G_END - G_EXP)

                def take_x(j, P):
                    act.wait_ge(gathered, P * 4 + (j + 1))
                    dst = (slot_x_hi, slot_x_lo)[j // 2].rearrange("p k n -> p (k n)")
                    A_(dst[:, ROW * (j % 2):ROW * (j % 2) + ROW], two_banks[0], ACT.Copy).then_inc(x_got, 1)

                for j in range(4):
                    take_x(j, 9 * p)
                def ahead_x(pair, q, n):
                    m = 24 * q + n + AHEAD
                    s = m % SLOTS
                    act.wait_ge(landed_x[m % RAW], (pair * 8 + (64 * p + m // RAW + 1)) * 16)
                    act.wait_ge(chunk_done, (pair * 12 + (base + m // SLOTS)) * SLOTS + (s + 1))
                    A_(w_hi[:, s, :, :].rearrange("p k m -> p (k m)"), raw_x[m % RAW], ACT.Copy).then_inc(hi_ready, 1)

                with act.Fori(0, EXPERTS // 2) as pair:
                    for q in range(2):
                        E = pair * 2 + (q + EXPERTS * p)
                        for n in range(24):
                            g = pair * 12 + (base + 6 * q)
                            ahead_x(pair, q, n)
                            if n == 8:
                                product(g + 1, 3)
                                A_(silu_row, two_banks[q], ACT.Silu).then_inc(silu_done, 1)
                            if n == 15:
                                for half in range(2):
                                    act.wait_ge(hid_turned, E * 2 + (half + 1))
                                    c = slice(512 * half, 512 * half + 512)
                                    A_(slot_h_hi.rearrange("p k n -> p (k n)")[:, c], two_banks[1 - q][:, c],
                                       ACT.Copy).then_inc(hid_hi, 1)
                            if q == 1 and n in TAKES:
                                take_x(TAKES.index(n), pair + (9 * p + 1))
                            if n == 23:
                                product(g + 5, 3)
                                A_(out_hi, two_banks[q], ACT.Copy, scale=slot_gate[:, q:q + 1])\
                                    .then_inc(gated_hi, 1)

            experts(0)
            act.wait_ge(flag_ready, 1)
            crowded = act.value_load(flag[0:1, 0:1], min_val=0, max_val=1)
            with act.If(crowded > 0):
                experts(1)
            load_exp_ln(nc, act)
            act.wait_ge(var_ready, 1)
            power_half(moments[:, :, 2:3], moments[:, :, 1:2], 1.0, eps[:, 1:2]).then_inc(fin_rstd, 1)

        @block.vector
        def _(dve):
            TT, TS, STT = nc.vector.tensor_tensor, nc.vector.tensor_scalar, nc.vector.scalar_tensor_tensor

            def split(g, s):
                dve.wait_ge(hi_ready, g * SLOTS + (s + 1))
                TT(w_lo[:, s, :, :], raw[:, s, :, :], w_hi[:, s, :, :], ALU.subtract).then_inc(split_ready, 1)

            def ahead(g, s):
                split(g + (s + AHEAD) // SLOTS, (s + AHEAD) % SLOTS)

            def product(g, s):
                dve.wait_ge(chunk_done, g * SLOTS + (s + 1 + SLOTS))

            def scaled_input(w, which, gain):
                dve.wait_ge(norm_rstd, w + 1)

                def lower(k):
                    dve.wait_ge(u_hi, which * KT + k + 1)
                    TT(x_lo[:, k, :], wide[:, k, :], x_hi[:, k, :], ALU.subtract).then_inc(u_lo, 1)

                for k in range(KT):
                    STT(wide[:, k, :], h[:, k, :], lay[:, gain + k:gain + k + 1], rstd[:, :],
                        ALU.mult, ALU.mult).then_inc(u_ready, 1)
                    if k >= 2:
                        lower(k - 2)
                lower(KT - 2)
                lower(KT - 1)
                dve.drain()

            def add_square(v, b):
                TT(head_sq[:, b, :], v, v, ALU.mult)
                dve.drain()
                TT(row_sum[:, :], row_sum[:, :], head_sq[:, b, :], ALU.add)

            def add_normed(w, gain):
                dve.drain().then_inc(norm_sum, 1)
                dve.wait_ge(norm_rstd, w + 1)
                for k0 in (0, KT // 2):
                    ks = range(k0, k0 + KT // 2)
                    for k in ks:
                        STT(wide[:, k, :], wide[:, k, :], lay[:, gain + k:gain + k + 1], rstd[:, :],
                            ALU.mult, ALU.mult)
                    dve.drain()
                    for k in ks:
                        TT(h[:, k, :], h[:, k, :], wide[:, k, :], ALU.add).then_inc(h_ready, 1)
                dve.drain()

            def rope(dst, raw_in, turned, tab):
                TT(head_sq[:, 0, :], raw_in, rope_t[:, tab, :], ALU.mult)
                TT(head_sq[:, 1, :], turned, rope_t[:, tab + 1, :], ALU.mult)
                dve.drain()
                return TT(dst, head_sq[:, 0, :], head_sq[:, 1, :], ALU.add)

            dve.memset(eps[:, 0:1], RMS_EPS)
            dve.memset(eps[:, 1:2], LN_EPS)
            dve.memset(small[:, :, :, :], 1.0)
            dve.drain().then_inc(set_up, 1)
            dve.sem_inc(split_ready, SLOTS)
            dve.sem_inc(acc_free[0], 1)
            dve.sem_inc(acc_free[1], 1)
            dve.sem_inc(y_ready, 2)
            dve.sem_inc(a_lo, 2)
            dve.wait_ge(h_in_s, 16)
            dve.wait_ge(consts, 16 * len(FIRST))
            dve.sem_inc(h_ready, KT)
            dve.wait_ge(bmm_s, 1)
            TT(brow[:, :], ps[5][0:8, :], badd[:, :], ALU.add).then_inc(brow_s, 1)
            for s in range(AHEAD):
                split(0, s)

            with dve.Fori(0, LAYERS) as l:
                G = l * G_LAYER
                nc.vector.tensor_copy(lay[:, :], at(par, l, C_LAYER)).then_inc(lay_ready, 1)
                dve.drain()
                scaled_input(l * 4, l * 2, C_GAIN)
                with dve.Fori(0, 6) as i:
                    for s in range(SLOTS):
                        ahead(G + G_GATE + i, s)
                dve.wait_ge(later_consts, 16 * len(LATER))
                for s in range(SLOTS):
                    ahead(G + G_RET, s)
                with dve.Fori(0, PAIRS) as i:
                    u = l * PAIRS + i
                    g = G + (G_RET + 1) + i
                    for j in range(2):
                        dve.wait_ge(perm_done, u * 2 + j + 1)
                        rope((q_rot, k_rot)[j][:, :], raw_qk[:, j, :], ps[j][:, 0:TOK], 2 * j).then_inc(ret_rot, 1)
                        dve.drain()
                    dve.wait_ge(rate_ready, l + 1)
                    for j in range(2):
                        TS(decay[:, j, :], dist[:, 0, :], col(decay_rate, i * 2 + j), None, ALU.mult)
                    dve.drain()
                    for j in range(2):
                        STT(decay[:, j, :], dist[:, 1, :], col(decay_rate, i * 2 + (8 + j)), decay[:, j, :],
                            ALU.mult, ALU.add).then_inc(decay_arg, 1)
                    ahead(g, 0)
                    for j in range(2):
                        dve.wait_ge(scores, u * 2 + j + 1)
                        dve.wait_ge(decay_ready, u * 2 + j + 1)
                        for t, (t0, tn) in enumerate(TILES):
                            TT(prob_t[0:tn, j, t, :], ps[((0, 1, 4), (5, 2, 3))[j][t]][0:tn, 0:TOK],
                               decay[0:tn, j, 256 - t0:256 - t0 + TOK], ALU.mult)
                        dve.drain().then_inc(decayed, 1)
                    ahead(g, 1)
                    ahead(g, 2)
                    dve.wait_ge(gates_ready, l + 1)
                    for j in range(2):
                        dve.wait_ge(head_rs, u * 2 + j + 1)
                        TT(head_y[:, j, :], ps[(0, 5)[j]][:, 0:TOK], head_rstd[:, j, :], ALU.mult)
                    dve.drain()
                    for j in range(2):
                        TT(head_y[:, j, :], head_y[:, j, :], at(gates, i * 2 + j), ALU.mult)
                    dve.drain().then_inc(y_ready, 2)
                    ahead(g, 3)
                    for j in range(2):
                        dve.wait_ge(y_hi, u * 2 + j + 1)
                        TT(at(f_lo, i * 2 + j), head_y[:, j, :], at(f_hi, i * 2 + j), ALU.subtract)
                    dve.drain().then_inc(y_lo, 2)
                for s in range(SLOTS):
                    ahead(G + G_ATT + 1, s)
                dve.wait_ge(a_perm, l + 1)
                rope(k_rot[:, :], raw_qk[:, 1, :], ps[0][:, 0:TOK], 6).then_inc(a_rot, 1)
                dve.drain()

                def rotate_q(n, turned):
                    dve.wait_ge(a_qperm, turned)
                    rope(q_rot[:, :], at(q_att, n), ps[1][:, 0:TOK], 4).then_inc(a_qrot, 1)
                    dve.drain()

                rotate_q(0, l * (PAIRS + 1) + 1)

                def reto(i, s):
                    ahead(G + G_RETO + i, s)
                    product(G + G_RETO + i, s)
                    TT(at(wide, i * 4 + s), lin[s % 2][:, 0:TOK], at(gates, i * 4 + (s + KT)), ALU.mult)\
                        .then_inc(acc_free[s % 2], 1)

                with dve.Fori(0, PAIRS // 2) as i:
                    for q in range(2):
                        u = l * PAIRS + i * 2 + q
                        for j in range(2):
                            dve.wait_ge(a_scores, u * 2 + j + 1)
                            nc.vector.tensor_copy(sink_col[:, j:j + 1], col(lay, i * 4 + (2 * q + C_SINK + j)))
                            dve.drain()
                            for t, (t0, tn) in enumerate(TILES):
                                nc.vector.tensor_tensor_reduce(
                                    prob[0:tn, j, t, :], ps[3 * j + t][0:tn, 0:TOK], mask[0:tn, t, :], 1.0,
                                    sink_col[0:tn, j:j + 1], ALU.add, ALU.max, small[0:tn, j, 0, t:t + 1])
                            dve.drain()
                            TS(small[:, j, 1, 0:3], small[:, j, 0, 0:3], -1.0, None, ALU.mult).then_inc(a_max, 1)
                        for j in range(2):
                            dve.wait_ge(a_exp, u * 2 + j + 1)
                            TT(small[:, j, 2, 0:3], small[:, j, 2, 0:3], small[:, j, 3, 0:3], ALU.add)
                            dve.drain()
                            nc.vector.reciprocal(small[:, j, 2, 0:3], small[:, j, 2, 0:3])
                            dve.drain()
                            for t, (t0, tn) in enumerate(TILES):
                                TS(prob[0:tn, j, t, :], prob[0:tn, j, t, :], small[0:tn, j, 2, t:t + 1], None, ALU.mult)
                            dve.drain().then_inc(a_prob, 1)
                        reto(i, 2 * q)
                        rotate_q(i * 2 + (q + 1), u + (l + 2))
                        for j in range(2):
                            p = slice(64 * j, 64 * j + 64)
                            dve.wait_ge(a_hi, u * 2 + j + 1)
                            TT(at(f_lo, i * 2 + (q + 8), p=p), ps[3 * j][p, 0:TOK], at(f_hi, i * 2 + (q + 8), p=p), ALU.subtract)\
                                .then_inc(a_lo, 1)
                        reto(i, 2 * q + 1)
                dve.drain()

                def mix_lower(ks):
                    for k in ks:
                        dve.wait_ge(m_hi, l * KT + k + 1)
                        TT(x_lo[:, k, :], wide[:, k, :], x_hi[:, k, :], ALU.subtract).then_inc(m_lo, 1)
                    dve.drain()

                for s in range(SLOTS):
                    ahead(G + G_ATTO, s)
                    product(G + G_ATTO, s)
                    for b in range(2):
                        TT(head_y[:, b, :], lin[b][:, 0:TOK], gates[:, 2 * KT + 2 * s + b, :], ALU.mult)\
                            .then_inc(acc_free[b], 1)
                    dve.drain()
                    for b in range(2):
                        TT(wide[:, 2 * s + b, :], wide[:, 2 * s + b, :], head_y[:, b, :], ALU.add)\
                            .then_inc(m_ready, 1)
                    if s > 0:
                        mix_lower((2 * s - 2, 2 * s - 1))
                mix_lower((KT - 2, KT - 1))
                dve.memset(row_sum[:, :], 0.0)
                with dve.Fori(0, 2) as i:
                    for s in range(SLOTS):
                        ahead(G + G_MIX + i, s)
                        dve.wait_ge(mix_ready, l * KT + i * 4 + (s + 1))
                        add_square(at(wide, i * 4 + s), s % 2)
                add_normed(l * 4 + 1, C_GAIN + 8)
                scaled_input(l * 4 + 2, l * 2 + 1, C_GAIN + 16)
                dve.memset(wide[:, :, :], 0.0)
                dve.drain()
                with dve.Fori(0, FF_HALVES) as f:
                    with dve.Fori(0, 4) as i:
                        g = G + G_FF + f * G_HALF + i
                        n = (l * FF_HALVES + f) * FF_BLOCKS + i * 4
                        for s in range(SLOTS):
                            product(g, s)
                            dst = head_y[:, s % 2, :]
                            TS(dst, lin[s % 2][:, 0:TOK], 0.0, None, ALU.max).then_inc(acc_free[s % 2], 1)
                            dve.drain()
                            TT(dst, dst, dst, ALU.mult).then_inc(f_act, 1)
                            ahead(g, s)
                            dve.wait_ge(f_hi_s, n + (s + 1))
                            TT(at(f_lo, i * 4 + s), dst, at(f_hi, i * 4 + s), ALU.subtract).then_inc(f_lo_s, 1)
                            dve.drain()
                    dve.memset(row_sum[:, :], 0.0)
                    with dve.Fori(0, 4) as i:
                        g = G + G_FF + 4 + f * G_HALF + i
                        for s in range(SLOTS):
                            ahead(g, s)
                            if s % 2 == 1:
                                product(g, s)
                                b = s // 2
                                dst = at(wide, i * 2 + b)
                                TT(dst, lin[b][:, 0:TOK], dst, ALU.add).then_inc(acc_free[b], 1)
                                dve.drain()
                                add_square(dst, b)
                    dve.drain()
                add_normed(l * 4 + 3, C_GAIN + 24)

            for k in range(KT):
                dve.wait_ge(x1_hi, k + 1)
                TT(x_lo[:, k, 0:SEQ], h[:, k, META:TOK], x_hi[:, k, 0:SEQ], ALU.subtract).then_inc(x1_lo, 1)
            dve.drain()
            with dve.Fori(0, 6) as i:
                for s in range(SLOTS):
                    ahead(i + G_QKV, s)

            with dve.Fori(0, PAIRS) as u:
                for j in range(2):
                    dve.wait_ge(d_S, u * 2 + j + 1)
                    nc.vector.tensor_reduce(small[:, j, 0, 0:1], lin[j][:, 0:128], AX.X, ALU.max)
                    nc.vector.tensor_reduce(small[:, j, 0, 1:2], lin[j][:, 128:384], AX.X, ALU.max)
                    dve.drain()
                    TS(small[:, j, 1, 0:2], small[:, j, 0, 0:2], -1.0, None, ALU.mult).then_inc(d_max, 1)
                for j in range(2):
                    dve.wait_ge(s_log, u * 2 + j + 1)
                    sp_ = prob_flat[:, j, :]
                    L = log_rest[:, j, :]
                    STT(L, ps[j][:, 0:384], 0.0, sp_, ALU.max, ALU.add)
                    dve.drain()
                    TT(L, L, tri[:, 1, :], ALU.mult)
                    STT(sp_, ps[j][:, 0:384], 0.0, sp_, ALU.min, ALU.subtract)
                    dve.drain().then_inc(s_L, 1)
                for j in range(2):
                    dve.wait_ge(d_exp, u * 2 + j + 1)
                    P = dil_flat[:, j, :]
                    nc.vector.reciprocal(small[:, j, 2, 0:2], small[:, j, 2, 0:2])
                    dve.drain()
                    TS(P[:, 0:128], P[:, 0:128], small[:, j, 2, 0:1], None, ALU.mult)
                    TS(P[:, 128:384], P[:, 128:384], small[:, j, 2, 1:2], None, ALU.mult)
                    dve.drain().then_inc(d_prob, 1)
                for j in range(2):
                    dve.wait_ge(s_btw, u * 2 + j + 1)
                    TT(prob_flat[:, j, :], prob_flat[:, j, :], ps[j][:, 0:384], ALU.add).then_inc(s_arg, 1)
                for j in range(2):
                    dve.wait_ge(s_a, u * 2 + j + 1)
                    TT(prob_tf[:, j, :], prob_tf[:, j, :], tri[:, 0, :], ALU.mult).then_inc(s_am, 1)
                for kind in range(2):
                    dve.wait_ge(s_rs, u * 2 + (kind + 1))
                    STT(head_y[:, kind, 0:SEQ], ps[4 - kind][:, 0:SEQ], col(par2, u + (C_GHEAD + 4 * kind)),
                        head_rstd[:, kind, 0:SEQ], ALU.mult, ALU.mult).then_inc(s_y, 1)
                for kind in range(2):
                    dve.wait_ge(s_hi, u * 2 + (kind + 1))
                    TT(at(x_lo, u + 4 * kind, SEQ), head_y[:, kind, 0:SEQ], at(x_hi, u + 4 * kind, SEQ),
                       ALU.subtract).then_inc(s_lo, 1)
                dve.drain()
            dve.memset(row_sum[:, :], 0.0)
            with dve.Fori(0, 2) as i:
                for s in range(SLOTS):
                    ahead(i + G_OUT, s)
                    product(i + G_OUT, s)
                    src = h[:, bass.ds(i * 4 + s, 1), META:TOK].rearrange("p a n -> p (a n)")
                    STT(at(wide, i * 4 + s, SEQ), src, ALPHA, lin[s % 2][:, 0:SEQ], ALU.mult, ALU.add)\
                        .then_inc(acc_free[s % 2], 1)
                    dve.drain()
                    TT(row_sum[:, 0:SEQ], row_sum[:, 0:SEQ], at(wide, i * 4 + s, SEQ), ALU.add)
            dve.drain().then_inc(ln_s1, 1)
            dve.wait_ge(ln_mean, 1)
            for k in range(KT):
                TT(wide[:, k, 0:SEQ], wide[:, k, 0:SEQ], ps[0][:, 0:SEQ], ALU.subtract).then_inc(ln_c, 1)
            dve.wait_ge(ln_rs, 1)
            for k in range(KT):
                TT(wide[:, k, 0:SEQ], wide[:, k, 0:SEQ], rstd[:, 0:SEQ], ALU.mult)
            dve.drain()
            for k in range(KT):
                TS(h[:, k, 0:SEQ], wide[:, k, 0:SEQ], par2[:, C_LN + k:C_LN + k + 1],
                   par2[:, C_LN + 8 + k:C_LN + 9 + k], ALU.mult, ALU.add).then_inc(ln_out, 1)
            dve.drain()

            dve.wait_ge(logit_s, 1)
            for t in range(2):
                TT(rt[:, t, 0, :], ps[t][:, 0:16], par2[:, C_BROUTER:C_BROUTER + 16], ALU.add)
            dve.drain()
            nc.vector.tensor_reduce(rt[:, :, 1, 2:3], rt[:, :, 0, :], AX.X, ALU.max)
            dve.drain()
            TS(rt[:, :, 1, 0:1], rt[:, :, 1, 2:3], -1.0, None, ALU.mult)
            dve.drain().then_inc(rt_max, 1)
            dve.wait_ge(rt_exp, 1)
            nc.vector.reciprocal(rt[:, :, 1, 3:4], rt[:, :, 1, 1:2])
            dve.drain()
            for t in range(2):
                TS(rt[:, t, 3, :], rt[:, t, 2, :], rt[:, t, 1, 3:4], None, ALU.mult)
            dve.drain()

            def others_ahead(row, n_in, width, dst):
                g = width // n_in
                m = n_in * n_in * g
                shape4 = lambda x: x.rearrange("p (g a b) -> p g a b", a=n_in, b=n_in)
                for t in range(2):
                    a = rt[:, t, row, 0:width].rearrange("p (g e) -> p g e", e=n_in)
                    other = a.unsqueeze(2).broadcast_to((128, g, n_in, n_in))
                    own = a.unsqueeze(3).broadcast_to((128, g, n_in, n_in))
                    TT(shape4(cmp[:, t, 0, 0:m]), other, own, ALU.is_gt)
                    TT(shape4(cmp[:, t, 1, 0:m]), other, own, ALU.is_equal)
                dve.drain()
                for t in range(2):
                    TT(cmp[:, t, 1, 0:m], cmp[:, t, 1, 0:m], early[:, 0:m], ALU.mult)
                dve.drain()
                TT(cmp[:, :, 0, 0:m], cmp[:, :, 0, 0:m], cmp[:, :, 1, 0:m], ALU.add)
                dve.drain()
                for t in range(2):
                    nc.vector.tensor_reduce(rt[:, t, dst, 0:width], cmp[:, t, 0, 0:m].rearrange(
                        "p (a b) -> p a b", b=n_in), AX.X, ALU.add)
                dve.drain()

            R = lambda i, n=16: rt[:, :, i, 0:n]
            others_ahead(3, 4, 16, 4)
            TS(R(5), R(4), 1.5, None, ALU.is_lt)
            dve.drain()
            TT(R(6), R(5), R(3), ALU.mult)
            dve.drain()
            for t in range(2):
                nc.vector.tensor_reduce(rt[:, t, 7, 0:4], rt[:, t, 6, :].rearrange("p (g e) -> p g e", e=4),
                                        AX.X, ALU.add)
            dve.drain()
            others_ahead(7, 4, 4, 8)
            TS(R(9, 4), R(8, 4), 0.5, None, ALU.is_lt)
            nc.vector.reciprocal(rt[:, :, 9, 4:8], R(7, 4))
            dve.drain()
            TT(R(10, 4), R(9, 4), rt[:, :, 9, 4:8], ALU.mult)
            dve.drain()
            for t in range(2):
                TT(rt[:, t, 11, :].rearrange("p (g e) -> p g e", e=4),
                   rt[:, t, 6, :].rearrange("p (g e) -> p g e", e=4),
                   rt[:, t, 10, 0:4].unsqueeze(2).broadcast_to((128, 4, 4)), ALU.mult)
            dve.drain()
            TS(R(12), R(11), 0.0, None, ALU.is_gt)
            dve.drain().then_inc(rt_gate, 1)
            dve.wait_ge(slots_mm, 1)
            dve.memset(slot_of[:, :, :], -1.0)
            dve.drain()
            for t in range(2):
                STT(rt[:, t, 13, :], ps[1][:, 16 * t:16 * t + 16], 1.0, rt[:, t, 12, :], ALU.add, ALU.mult)
            nc.vector.tensor_reduce(flag_f[:, :], ps[1][:, 32:48], AX.X, ALU.max)
            dve.drain()
            for t in range(2):
                TS(slot_of[:, t, 0:EXPERTS], rt[:, t, 13, :], -1.0, None, ALU.add)
            dve.drain().then_inc(slots_ready, 1)
            TS(flag[:, :], flag_f[:, :], 128.5, None, ALU.is_gt).then_inc(flag_ready, 1)
            dve.wait_ge(rt_t, 1)
            nc.vector.tensor_copy(pick, sq[0:EXPERTS, IDENT, 0:EXPERTS])
            nc.vector.tensor_copy(slot_row, ps[1][0:EXPERTS, 0:SEQ])
            dve.drain().then_inc(rt_row, 1)
            TS(res_row, sum_bank, ALPHA, None, ALU.mult)
            dve.wait_ge(tok_hi_s, 1)
            TT(tok_lo, sum_bank, tok_hi, ALU.subtract)
            for t in range(2):
                dve.memset(sel_t[t].bitcast(F32), 0.0)
            dve.memset(out_hi.bitcast(F32), 0.0)
            dve.memset(out_lo.bitcast(F32), 0.0)
            dve.memset(slot_none[:, :], 0.0)
            dve.drain().then_inc(tok_split, 1)
            dve.sem_inc(gated_lo, 1)
            dve.wait_ge(rt_all, EXPERTS // 2)

            def experts(p):
                base = G_EXP + p * (G_END - G_EXP)

                def select(pair):
                    for i in range(2):
                        for t in range(2):
                            TS(sel[t][:, 128 * i:128 * i + 128], lane[:, 2 + 128 * p:130 + 128 * p],
                               col(slot_of[:, t, :], pair * 2 + i), None, ALU.is_equal)
                    dve.drain().then_inc(sel_ready, 1)

                if p == 0:
                    dve.wait_ge(lane_s, 16)
                select(0)
                def ahead_x(pair, q, n):
                    m = 24 * q + n + AHEAD
                    s = m % SLOTS
                    dve.wait_ge(hi_ready, (pair * 12 + (base + m // SLOTS)) * SLOTS + (s + 1))
                    TT(w_lo[:, s, :, :].rearrange("p k m -> p (k m)"), raw_x[m % RAW],
                       w_hi[:, s, :, :].rearrange("p k m -> p (k m)"), ALU.subtract).then_inc(split_ready, 1)

                with dve.Fori(0, EXPERTS // 2) as pair:
                    for q in range(2):
                        e = pair * 2 + q
                        E = pair * 2 + (q + EXPERTS * p)
                        for n in range(24):
                            g = pair * 12 + (base + 6 * q)
                            ahead_x(pair, q, n)
                            if n == 15:
                                dve.wait_ge(silu_done, E + 1)
                                product(g + 3, 3)
                                for half in range(2):
                                    c = slice(512 * half, 512 * half + 512)
                                    TT(hid_row[:, c], silu_row[:, c], two_banks[1 - q][:, c], ALU.mult)\
                                        .then_inc(hid_done, 1)
                                if q == 0:
                                    dve.wait_ge(slot_gate_mm, pair + (EXPERTS // 2 * p + 1))
                                    nc.vector.tensor_copy(slot_gate[:, :], banks[:, 0, 0:2])
                                    dve.drain().then_inc(slot_gate_s, 1)
                                for half in range(2):
                                    c = slice(512 * half, 512 * half + 512)
                                    dve.wait_ge(hid_hi, E * 2 + (half + 1))
                                    TT(slot_h_lo.rearrange("p k n -> p (k n)")[:, c], two_banks[1 - q][:, c],
                                       slot_h_hi.rearrange("p k n -> p (k n)")[:, c], ALU.subtract)\
                                        .then_inc(hid_lo, 1)
                            if n == 16 and q == 0:
                                select(pair + 1)
                            if n == 17:
                                dve.wait_ge(scattered, E + (p + 1))
                                for t in range(2):
                                    TS(sel_t[t], at(gates, e, 128, c0=128 * t), lane[:, p:p + 1], None,
                                       ALU.is_equal)
                            if n == 23:
                                dve.wait_ge(gated_hi, E + 1)
                                STT(out_lo, two_banks[q], slot_gate[:, q:q + 1], out_hi, ALU.mult, ALU.subtract)
                                dve.drain().then_inc(gated_lo, 1)

            experts(0)
            crowded = dve.value_load(flag[0:1, 0:1], min_val=0, max_val=1)
            with dve.If(crowded > 0):
                dve.wait_ge(scattered, EXPERTS + 1)
                for t in range(2):
                    dve.memset(sel_t[t].bitcast(F32), 0.0)
                dve.drain().then_inc(cleared, 1)
                experts(1)
            dve.wait_ge(sum_done, 1)
            for t in range(2):
                for b in range(2):
                    nc.vector.bn_stats(stats[:, t, b, :], banks[:, 4 + 2 * t + b, :])
            dve.drain()
            for t in range(2):
                nc.vector.bn_aggr(moments[:, t, 0:2], stats[:, t, :, :].rearrange("p b n -> p (b n)"))
            dve.drain().then_inc(var_ready, 1)
            dve.wait_ge(rows_s, 32)
            for t in range(2):
                STT(res_row[:, t * ROW:(t + 1) * ROW], sum_bank[:, t * ROW:(t + 1) * ROW], moments[:, t, 0:1],
                    gain_rows[:, 0:ROW], ALU.subtract, ALU.mult)
            dve.drain()
            dve.wait_ge(fin_rstd, 1)
            for t in range(2):
                STT(res_row[:, t * ROW:(t + 1) * ROW], res_row[:, t * ROW:(t + 1) * ROW], moments[:, t, 2:3],
                    gain_rows[:, ROW:2 * ROW], ALU.mult, ALU.add).then_inc(y_half, 1)


_INS = ["weights", "h_in", "layer_par", "second_par", "rope", "toeplitz", "att_mask", "squares", "stick",
        "bias_map", "bias_add", "rel_bias", "w_router", "tie_order", "lanes", "ln_rows"]


def feature_blocks(v):
    import numpy as np
    v = np.asarray(v)
    return np.moveaxis(v.reshape(*v.shape[:-1], -1, 128), -1, 0)


def lay_out_weights(x):
    import numpy as np
    weights = np.zeros((GROUPS * SLOTS, 128, KT * 128), np.float32)

    def tile_rows(w):
        return w.reshape(-1, 128, w.shape[-1]).transpose(1, 0, 2)

    def put(at, w, block, k0=0):
        weights[at] = w[:, k0:k0 + KT, block * 128:(block + 1) * 128].reshape(128, -1)

    for l in range(LAYERS):
        at = l * G_LAYER * SLOTS
        w_in = x["w_in"][l]
        cuts = np.cumsum([0, 512, 512, 1024, 1024, 512, 128, 128, 1024, 1024])
        q_r, k_r, v_r, g_r, q_a, k_a, v_a, gate_r, gate_a = [
            tile_rows(w_in[:, a:b]) for a, b in zip(cuts[:-1], cuts[1:])]
        q_a = q_a.reshape(128, KT, 2, PAIRS, 64).transpose(0, 1, 3, 2, 4).reshape(128, KT, 512)
        order = [(g_r, b) for b in range(KT)] + [(gate_r, b) for b in range(KT)] + [(gate_a, b) for b in range(KT)]
        for i in range(PAIRS):
            order += [(q_r, i), (k_r, i), (v_r, 2 * i), (v_r, 2 * i + 1)]
        order += [(q_a, 0), (k_a, 0), (v_a, 0)] + [(q_a, i) for i in range(1, PAIRS)]
        for n, (w, b) in enumerate(order):
            put(at + n, w, b)
        ret_o, mix_o = tile_rows(x["w_ret_o"][l]), tile_rows(x["w_mix_o"][l])
        att_o = x["w_att_o"][l].reshape(2, PAIRS, 64, D).transpose(1, 0, 2, 3).reshape(512, D)
        att_o = tile_rows(att_o)
        for b in range(KT):
            put(at + G_RETO * SLOTS + b, ret_o, b)
            put(at + G_MIX * SLOTS + b, mix_o, b)
        for n in range(KT // 2):
            two = att_o[:, :, n * 256:(n + 1) * 256].reshape(128, 4, 2, 128).transpose(0, 2, 1, 3)
            weights[at + G_ATTO * SLOTS + n] = two.reshape(128, -1)
        ff1, ff2 = tile_rows(x["w_ff1"][l]), tile_rows(x["w_ff2"][l])
        for f in range(FF_HALVES):
            base = at + (G_FF + f * G_HALF) * SLOTS
            for n in range(FF_BLOCKS):
                put(base + n, ff1, f * FF_BLOCKS + n)
                put(base + FF_BLOCKS + n, ff2, n // 2, f * FF_BLOCKS + KT * (n % 2))
    w_in = x["w_in_2"][0]
    sb_q, sb_k, sb_v, dl_q, dl_k, dl_v = [tile_rows(w_in[:, i * 512:(i + 1) * 512]) for i in range(6)]
    n = G_QKV * SLOTS
    for three in ((sb_q, sb_k, sb_v), (dl_q, dl_k, dl_v)):
        for i in range(PAIRS):
            for w in three:
                put(n, w, i)
                n += 1
    w_out = tile_rows(x["w_out_2"][0])
    for b in range(KT):
        put(G_OUT * SLOTS + b, w_out, b)
    n = G_EXP * SLOTS
    for e in range(EXPERTS):
        for name in ("w_gate_2", "w_up_2", "w_down_2"):
            weights[n:n + KT] = x[name][0, e].reshape(KT, 128, D)
            n += KT
    weights[G_END * SLOTS:] = weights[G_EXP * SLOTS:(G_EXP + GROUPS - G_END) * SLOTS]
    return weights


def bucket(dist):
    import math

    import numpy as np
    d = np.maximum(dist, 0)
    ratio = np.log(np.maximum(d, 1).astype(np.float32) / np.float32(16)) / np.float32(math.log(2048 / 16))
    large = np.minimum(16 + (ratio * np.float32(16)).astype(np.int32), 31)
    return np.where(d < 16, d, large)


def tables():
    import numpy as np
    f = np.float32
    pos = np.arange(TOK, dtype=f)
    rope = np.zeros((128, 8, TOK), f)
    turn = {}
    for at, (theta, dim) in ((0, (10000.0, 64)), (4, (500000.0, 16))):
        half = dim // 2
        freqs = np.power(f(theta), -np.arange(0, dim, 2, dtype=f) / f(dim)).astype(f)
        ang = (pos[:, None] * freqs[None, :]).astype(f)
        cos, sin = np.ones((64, TOK), f), np.zeros((64, TOK), f)
        cos[:half] = cos[half:dim] = np.cos(ang).T
        sin[:half] = sin[half:dim] = np.sin(ang).T
        for n, t in enumerate((cos / 8, sin / 8, cos, sin)):
            rope[:, at + n] = np.tile(t, (2, 1))
        m = np.zeros((64, 64), f)
        for i in range(half):
            m[i + half, i], m[i, i + half] = -1, 1
        turn[at] = np.kron(np.eye(2, dtype=f), m)
    eye = np.eye(128, dtype=f)
    row, column = np.arange(128)[:, None], np.arange(128)[None, :]
    squares = np.stack([
        turn[0], turn[4], eye - f(1 / 128), eye, np.full((128, 128), 1 / D, f), np.full((128, 128), 1 / 128, f),
        np.kron(np.eye(2, dtype=f), np.full((64, 64), 1 / 64, f)), (row > column).astype(f),
        np.ones((128, 128), f), eye[::-1]], 1)
    rel = np.arange(SPAN)[None, :] - 256 - np.arange(128)[:, None]
    toeplitz = np.stack([np.maximum(rel, 0), np.maximum(-rel, 0)], 1).astype(f)
    i = np.arange(3)[None, :, None] * 128 + np.arange(128)[:, None, None]
    j = np.arange(TOK)[None, None, :]
    att_mask = np.where((j < META) | (np.abs(i - j) <= 128), 0, NEG).astype(f)
    causal = np.concatenate([np.arange(128)[:, None] < np.arange(SEQ)[None, :], row < column], 1).astype(f)
    stick = np.stack([causal, -causal], 1)
    dist = 255 - np.arange(512)
    bias_map = (bucket(dist)[None, :] == np.arange(32)[:, None]).astype(f)
    times = (dist <= 128) * 1 + (dist % 4 == 0) * 1 + (dist % 16 == 0) * 1
    times = np.where(dist >= 0, times, 0)
    add = np.where(times > 0, np.log(np.maximum(times, 1)), NEG).astype(f)
    bias_add = np.tile(add, (8, 1))
    own, other = np.arange(4)[:, None], np.arange(4)[None, :]
    tie_order = np.tile((other < own).astype(f).ravel(), (128, 4))
    lanes = np.concatenate([np.arange(128)[:, None] + [[0, 128]], np.tile(np.arange(SEQ), (128, 1))], 1).astype(f)
    return dict(rope=rope, toeplitz=toeplitz, att_mask=att_mask, squares=np.ascontiguousarray(squares),
                stick=stick, bias_map=bias_map, bias_add=bias_add, tie_order=tie_order, lanes=lanes)


def kernel(**inputs):
    import numpy as np
    import concourse.bacc as bacc
    from concourse.bass_utils import run_bass_kernel_spmd as run

    x = {k: np.asarray(v) for k, v in inputs.items()}
    arrays = tables()
    arrays["weights"] = lay_out_weights(x)
    tokens = np.concatenate([x["meta_tokens"], x["x"][0]], 0)
    arrays["h_in"] = tokens.T.reshape(KT, 128, TOK).transpose(1, 0, 2)
    gains = np.stack([feature_blocks(x[n]) for n in (
        "norm_mix_pre", "norm_mix_post", "norm_ff_pre", "norm_ff_post")], 2)
    every = lambda v: np.broadcast_to(v[None], (128, *v.shape))
    sink = x["attn_sink"].reshape(LAYERS, 2, PAIRS).transpose(0, 2, 1).reshape(LAYERS, 8)
    arrays["layer_par"] = np.concatenate([
        gains.reshape(128, LAYERS, 32), every(x["ret_decay"].reshape(LAYERS, 16)), every(sink)], 2)
    arrays["second_par"] = np.concatenate(
        [feature_blocks(x[n][0]) for n in ("ln1_g_2", "ln1_b_2", "ln2_g_2", "ln2_b_2", "g_sb_2", "g_dil_2")]
        + [every(x["b_router_2"])], 1)
    arrays["ln_rows"] = np.stack([x["ln2_g_2"][0], x["ln2_b_2"][0]])
    arrays["rel_bias"] = x["rel_bias_2"]
    arrays["w_router"] = x["w_router_2"].reshape(KT, 128, EXPERTS).transpose(1, 0, 2)

    nc = bacc.Bacc("TRN2", target_bir_lowering=False, num_devices=1)
    arrays = {f"in_{n}": np.ascontiguousarray(arrays[n]) for n in _INS}
    args = [nc.dram_tensor(n, a.shape, mybir.dt.from_np(a.dtype), kind="ExternalInput").ap()
            for n, a in arrays.items()]
    args.append(nc.dram_tensor("y_out", (2, 128, D), F32, kind="ExternalOutput").ap())
    build_program(nc, *args)
    r = run(nc, [arrays], core_ids=[0])
    return r.results[0]["y_out"].reshape(1, SEQ, D)
```
